# Optimizing a Trainium2 kernel written in Bass

```python
import jax, jax.numpy as jnp
from jax import lax
import numpy as np

D_MODEL = 2048
BATCH = 1
SEQ = 256
DEPTH = 1

CHUNK = 64
D_PLE = 256

FOX_HEAD_DIM = 64
FOX_WIDTH = D_MODEL // 2
FOX_HEADS = FOX_WIDTH // FOX_HEAD_DIM
Q_BLOCK = 128

SSD_HEAD_DIM = 64
SSD_WIDTH = D_MODEL // 2
SSD_HEADS = SSD_WIDTH // SSD_HEAD_DIM
SSD_GROUPS = 2
SSD_STATE = 128
SSD_CONV = 4
SSD_CONV_DIM = SSD_WIDTH + 2 * SSD_GROUPS * SSD_STATE

MIX_WIDTH = FOX_WIDTH + SSD_WIDTH

IN_SPLITS = [
    FOX_WIDTH,
    FOX_WIDTH,
    FOX_WIDTH,
    FOX_HEADS,
    SSD_WIDTH,
    SSD_GROUPS * SSD_STATE,
    SSD_GROUPS * SSD_STATE,
    SSD_WIDTH,
    SSD_HEADS,
]
IN_COLS = int(sum(IN_SPLITS))

D_FF = 5632
FFN_CONV = 3

EPS = 1e-6

kernel_name = "hybrid_fox_ssd_convffn_ple"

def rmsnorm(u, w):
    uf = u.astype(jnp.float32)
    y = uf * lax.rsqrt(jnp.mean(uf * uf, axis=-1, keepdims=True) + EPS)
    return (y * w.astype(jnp.float32)).astype(u.dtype)

def causal_dwconv(u, w, b):
    K = w.shape[0]
    S = u.shape[1]
    up = jnp.pad(u, ((0, 0), (K - 1, 0), (0, 0)))
    return sum(up[:, k:k + S] * w[k] for k in range(K)) + b

def fox_attention(q, k, v, f_logit, b_f):
    Bsz, S, _ = q.shape
    H, Dh = FOX_HEADS, FOX_HEAD_DIM
    scale = Dh ** -0.5
    qh = q.reshape(Bsz, S, H, Dh).transpose(0, 2, 1, 3).astype(jnp.float32)
    kh = k.reshape(Bsz, S, H, Dh).transpose(0, 2, 1, 3).astype(jnp.float32)
    vh = v.reshape(Bsz, S, H, Dh).transpose(0, 2, 1, 3).astype(jnp.float32)
    log_f = jax.nn.log_sigmoid(f_logit.astype(jnp.float32) + b_f.astype(jnp.float32))
    c = jnp.cumsum(log_f, axis=1).transpose(0, 2, 1)
    n_blk = S // Q_BLOCK
    q_blk = qh.reshape(Bsz, H, n_blk, Q_BLOCK, Dh).transpose(2, 0, 1, 3, 4)
    c_blk = c.reshape(Bsz, H, n_blk, Q_BLOCK).transpose(2, 0, 1, 3)
    k_pos = jnp.arange(S)

    def one_block(args):
        qb, cb, i = args
        s = jnp.einsum('bhqd,bhkd->bhqk', qb, kh) * scale
        s = s + cb[..., :, None] - c[..., None, :]
        q_pos = i * Q_BLOCK + jnp.arange(Q_BLOCK)
        mask = k_pos[None, :] <= q_pos[:, None]
        s = jnp.where(mask[None, None], s, -jnp.inf)
        pr = jax.nn.softmax(s, axis=-1)
        return jnp.einsum('bhqk,bhkd->bhqd', pr, vh)

    out = lax.map(one_block, (q_blk, c_blk, jnp.arange(n_blk)))
    out = out.transpose(1, 0, 3, 2, 4).reshape(Bsz, S, H * Dh)
    return out.astype(q.dtype)

def ssd_mixer(xs, Bm, Cm, z, dt_raw, conv_w, conv_b, dt_bias, A_log, D_skip, norm_w):
    Bsz, S, _ = xs.shape
    H, P, G, N, L = SSD_HEADS, SSD_HEAD_DIM, SSD_GROUPS, SSD_STATE, CHUNK
    nc = S // L
    xbc = jnp.concatenate([xs, Bm, Cm], axis=-1)
    xbc = jax.nn.silu(causal_dwconv(xbc, conv_w, conv_b))
    xs, Bm, Cm = jnp.split(xbc, [SSD_WIDTH, SSD_WIDTH + G * N], axis=-1)

    xc = xs.astype(jnp.float32).reshape(Bsz, nc, L, H, P)
    Bc = Bm.astype(jnp.float32).reshape(Bsz, nc, L, G, N)
    Cc = Cm.astype(jnp.float32).reshape(Bsz, nc, L, G, N)
    dt = jax.nn.softplus(dt_raw.astype(jnp.float32) + dt_bias.astype(jnp.float32))
    A = -jnp.exp(A_log.astype(jnp.float32))
    dtc = dt.reshape(Bsz, nc, L, H)
    a_cum = jnp.cumsum(dtc * A, axis=2)

    rep = H // G
    Bh = jnp.repeat(Bc, rep, axis=3)
    Ch = jnp.repeat(Cc, rep, axis=3)

    causal = jnp.tril(jnp.ones((L, L), dtype=bool))
    seg = a_cum[:, :, :, None, :] - a_cum[:, :, None, :, :]
    decay = jnp.exp(jnp.where(causal[None, None, :, :, None], seg, -jnp.inf))
    CB = jnp.einsum('bclgn,bcsgn->bcgls', Cc, Bc)
    CB = jnp.repeat(CB, rep, axis=2)
    y_diag = jnp.einsum('bchls,bclsh,bcsh,bcshp->bclhp', CB, decay, dtc, xc)

    decay_to_end = jnp.exp(a_cum[:, :, -1:, :] - a_cum)
    states = jnp.einsum('bcshn,bcsh,bcsh,bcshp->bchpn', Bh, decay_to_end, dtc, xc)
    chunk_decay = jnp.exp(a_cum[:, :, -1, :])

    def step(h, inp):
        st, dec = inp
        return h * dec[..., None, None] + st, h

    h0 = jnp.zeros((Bsz, H, P, N), jnp.float32)
    _, h_prev = lax.scan(step, h0, (states.transpose(1, 0, 2, 3, 4), chunk_decay.transpose(1, 0, 2)))
    h_prev = h_prev.transpose(1, 0, 2, 3, 4)
    y_off = jnp.einsum('bclhn,bchpn,bclh->bclhp', Ch, h_prev, jnp.exp(a_cum))

    y = y_diag + y_off + D_skip.astype(jnp.float32)[:, None] * xc
    y = y.reshape(Bsz, S, H * P)
    y = y * jax.nn.silu(z.astype(jnp.float32))
    return rmsnorm(y, norm_w).astype(xs.dtype)

def setup_inputs(seed: int = 0) -> dict:
    key = jax.random.key(seed)
    ks = jax.random.split(key, 24)
    f32 = jnp.float32

    def nrm(k, shape, scale):
        return jax.random.normal(k, shape, f32) * scale

    def gain(k, shape):
        return 1.0 + 0.05 * jax.random.normal(k, shape, f32)

    dt0 = jnp.exp(jax.random.uniform(ks[8], (DEPTH, SSD_HEADS), f32,
                                     np.log(1e-3).astype(np.float32), np.log(1e-1).astype(np.float32)))
    dt_bias = dt0 + jnp.log(-jnp.expm1(-dt0))
    return {
        "x": jax.random.normal(ks[0], (BATCH, SEQ, D_MODEL), f32),
        "p": jax.random.normal(ks[1], (DEPTH, BATCH, SEQ, D_PLE), f32),
        "mix_norm_w": gain(ks[2], (DEPTH, D_MODEL)),
        "w_in": nrm(ks[3], (DEPTH, D_MODEL, IN_COLS), D_MODEL ** -0.5),
        "fox_forget_bias": jax.random.uniform(ks[4], (DEPTH, FOX_HEADS), f32, 1.0, 4.0),
        "ssd_conv_w": nrm(ks[5], (DEPTH, SSD_CONV, SSD_CONV_DIM), SSD_CONV ** -0.5),
        "ssd_conv_b": nrm(ks[6], (DEPTH, SSD_CONV_DIM), 0.02),
        "ssd_dt_bias": dt_bias,
        "ssd_A_log": jnp.log(jax.random.uniform(ks[7], (DEPTH, SSD_HEADS), f32, 1.0, 16.0)),
        "ssd_D": gain(ks[9], (DEPTH, SSD_HEADS)),
        "ssd_norm_w": gain(ks[10], (DEPTH, SSD_WIDTH)),
        "w_out": nrm(ks[11], (DEPTH, MIX_WIDTH, D_MODEL), MIX_WIDTH ** -0.5),
        "ffn_norm_w": gain(ks[12], (DEPTH, D_MODEL)),
        "w_gate_up": nrm(ks[13], (DEPTH, D_MODEL, 2 * D_FF), D_MODEL ** -0.5),
        "ffn_conv_w": nrm(ks[14], (DEPTH, FFN_CONV, D_FF), FFN_CONV ** -0.5),
        "ffn_conv_b": nrm(ks[15], (DEPTH, D_FF), 0.02),
        "w_down": nrm(ks[16], (DEPTH, D_FF, D_MODEL), D_FF ** -0.5),
        "ple_norm_w": gain(ks[17], (DEPTH, D_MODEL)),
        "w_ple_gate": nrm(ks[18], (DEPTH, D_MODEL, D_MODEL), D_MODEL ** -0.5),
        "w_ple_proj": nrm(ks[19], (DEPTH, D_PLE, D_MODEL), D_PLE ** -0.5),
        "final_norm_w": gain(ks[20], (D_MODEL,)),
    }

def reference(x, p, mix_norm_w, w_in, fox_forget_bias, ssd_conv_w, ssd_conv_b, ssd_dt_bias,
              ssd_A_log, ssd_D, ssd_norm_w, w_out, ffn_norm_w, w_gate_up, ffn_conv_w,
              ffn_conv_b, w_down, ple_norm_w, w_ple_gate, w_ple_proj, final_norm_w):
    split_idx = [int(v) for v in np.cumsum(IN_SPLITS)[:-1]]
    for i in range(DEPTH):
        h = rmsnorm(x, mix_norm_w[i])
        u = h @ w_in[i]
        q, k, v, f_logit, xs, Bm, Cm, z, dt_raw = jnp.split(u, split_idx, axis=-1)
        y_fox = fox_attention(q, k, v, f_logit, fox_forget_bias[i])
        y_ssd = ssd_mixer(xs, Bm, Cm, z, dt_raw, ssd_conv_w[i], ssd_conv_b[i], ssd_dt_bias[i],
                          ssd_A_log[i], ssd_D[i], ssd_norm_w[i])
        x = x + jnp.concatenate([y_fox, y_ssd], axis=-1) @ w_out[i]

        h = rmsnorm(x, ffn_norm_w[i])
        g, up = jnp.split(h @ w_gate_up[i], [D_FF], axis=-1)
        g = causal_dwconv(g, ffn_conv_w[i], ffn_conv_b[i])
        x = x + (jax.nn.silu(g) * up) @ w_down[i]

        h = rmsnorm(x, ple_norm_w[i])
        gate = jax.nn.sigmoid(h @ w_ple_gate[i])
        x = x + gate * (p[i] @ w_ple_proj[i])
    return rmsnorm(x, final_norm_w)


_drawn_inputs = setup_inputs


def setup_inputs(seed=0):
    import zlib

    import numpy as np

    out = dict(_drawn_inputs(seed))
    spreads = {}
    factors = {'ssd_conv_b': 3.428, 'ffn_conv_b': 6.964, 'ple_norm_w': 8.0}
    for name, (base, spread) in spreads.items():
        noise = np.random.default_rng([zlib.crc32(name.encode()), seed]).standard_normal(out[name].shape)
        drawn = base * np.exp(spread * noise) if base else spread * noise
        out[name] = __import__('jax').numpy.asarray(drawn.astype(out[name].dtype))
    for name, factor in factors.items():
        out[name] = (out[name] * factor).astype(out[name].dtype)
    return out
```

```python
from contextlib import ExitStack

import concourse.bass as bass
from concourse import mybir

F32 = mybir.dt.float32
F32R = mybir.dt.float32r
BF16 = mybir.dt.bfloat16
ALU = mybir.AluOpType
ACT = mybir.ActivationFunctionType
AX_X = mybir.AxisListType.X

P = 128
EPS = 1e-6
MASKED = -1e30
RING = 4
CHUNK = 1024
COLS = 512
MT = COLS // P
CONV_STEPS = 9
GATE_STEPS = 7
SOFTPLUS_STEPS = 16


def build(nc, x, p, mix_norm_w, w_in, fox_forget_bias, ssd_conv_w, ssd_conv_b, ssd_dt_bias, ssd_A_log,
          ssd_D, ssd_norm_w, w_out, ffn_norm_w, w_gate_up, ffn_conv_w, ffn_conv_b, w_down, ple_norm_w,
          w_ple_gate, w_ple_proj, final_norm_w, out):
    _, T, D = x.shape
    TT = T // P
    KD = D // P
    DP = p.shape[3]
    H = fox_forget_bias.shape[1]
    W = ssd_norm_w.shape[1]
    HD = W // H
    WT = W // P
    CW = ssd_conv_w.shape[2]
    GN = (CW - W) // 2
    G = GN // P
    CT = CW // P
    F = ffn_conv_w.shape[2]
    FT = F // P
    KC = ssd_conv_w.shape[1]
    KF = ffn_conv_w.shape[1]
    assert T == 256 and TT == 2 and DP == 2 * P and HD == 64 and KC == 4 and KF == 3 and G == 2

    c_q, c_k, c_v = 0, W, 2 * W
    c_f = 3 * W
    c_x = c_f + H
    c_b = c_x + W
    c_z = c_b + 2 * GN
    c_dt = c_z + W

    rows = lambda w: w[0].rearrange("(k p) n -> p k n", p=P)
    win_v, wout_v, wgu_v, wdn_v, wpg_v, wpp_v = map(rows, (w_in, w_out, w_gate_up, w_down, w_ple_gate, w_ple_proj))

    class Group:

        def __init__(self, name, view, col, operand, banks, chunks, by_token=False):
            self.name, self.view, self.col, self.operand = name, view, col, operand
            self.banks, self.chunks, self.by_token = banks, chunks, by_token

    SET_A, SET_B, SET_C, SET_D = (2, 3), (4, 5), (0, 1), (6, 7)
    KP = KD // 2
    in_cols = [("q0", c_q), ("bc", c_b), ("x0", c_x), ("x1", c_x + COLS), ("k0", c_k), ("q1", c_q + COLS),
               ("k1", c_k + COLS), ("v0", c_v), ("v1", c_v + COLS), ("z0", c_z), ("z1", c_z + COLS)]
    in_groups = [Group(n, win_v, c, "h", (SET_A, SET_B)[i % 2], KP, n[0] in "vz") for i, (n, c) in enumerate(in_cols)]
    out_groups = [Group(f"o{i}", wout_v, COLS * i, "mix", b, KP) for i, b in enumerate((SET_B, SET_A, SET_C, SET_D))]
    halves = [(0, 0, KP // 2), (1, 0, KP // 2), (0, KP // 2, KP), (1, KP // 2, KP), (2, 0, KP), (3, 0, KP)]
    front = [(g, c) for g in in_groups for c in range(KP)]
    front += [(out_groups[g], c) for g, a, b in halves for c in range(a, b)]
    NG = F // COLS
    n_ffn = len(front)
    n_down = n_ffn + NG * KD
    KDN = FT // 2
    NDN = D // COLS
    n_ple = n_down + NDN * KDN
    tail = []
    for i in range(NDN):
        gate, proj = ((SET_B, SET_D), (SET_C, SET_A))[i % 2]
        tail += [(Group(f"pp{i}", wpp_v, COLS * i, "p", proj, 1), 0)]
        pg = Group(f"pg{i}", wpg_v, COLS * i, "h", gate, KP)
        tail += [(pg, c) for c in range(KP)]
    assert n_ffn % RING == 0 and n_down % RING == 0 and n_ple % RING == 0 and NG % 2 == 1 and KDN % RING == 2

    def last_of(steps, base):
        return {g.name: base + i for i, (g, c) in enumerate(steps)}

    done = last_of(front, 0) | last_of(tail, n_ple)

    ctx = ExitStack()
    with ctx:
        def sb(name, shape, dt=F32):
            return ctx.enter_context(nc.sbuf_tensor(name, shape, dt))

        def sem(name):
            return ctx.enter_context(nc.semaphore(name))

        xT = sb("xT", [P, KD, T])
        hHi, hLo = sb("hHi", [P, KD, T], F32R), sb("hLo", [P, KD, T], F32R)
        w_raw = sb("w_raw", [P, RING, CHUNK])
        w_hi, w_lo = sb("w_hi", [P, RING, CHUNK], F32R), sb("w_lo", [P, RING, CHUNK], F32R)
        ident = sb("ident", [P, P])
        ones = sb("ones", [P, P])
        par = sb("par", [P, 3, P])
        par_mix = sb("par_mix", [P, KD])
        pHi, pLo = sb("pHi", [P, 2, T], F32R), sb("pLo", [P, 2, T], F32R)
        rms = sb("rms", [P, 2, T])
        rms_col = sb("rms_col", [P, TT])
        root = sb("root", [P, T + TT])
        sumsq = sb("sumsq", [P, 2, T])
        sq = sb("sq", [P, 2, T])
        eps = sb("eps", [P, 1])
        arena = (nc.sbuf_base + 31) // 32 * 32

        top = [0]

        def at(name, shape, dt=F32, offset=None):
            size = 4 if dt != BF16 else 2
            for n in shape[1:]:
                size *= n
            offset = top[0] if offset is None else offset
            top[0] = max(top[0], (offset + size + 31) // 32 * 32)
            assert arena + top[0] <= nc.sbuf_usable_end, (name, arena + top[0], nc.sbuf_usable_end)
            return nc.alloc_sbuf_tensor_at(name, shape, dt, offset=arena + offset)

        K1 = 1024
        qT = at("qT", [P, WT, T], offset=0)
        kE = at("kE", [P, WT, T], offset=8 * K1)
        kO = at("kO", [P, WT, T], offset=16 * K1)
        v = at("v", [P, TT, W], offset=24 * K1)
        xdt = at("xdt", [P, TT, W], offset=32 * K1)
        z = at("z", [P, TT, W], offset=40 * K1)
        xs = at("xs", [P, TT, W], offset=48 * K1)
        y_fox = at("y_fox", [P, TT, W], offset=56 * K1)
        xsT = at("xsT", [P, WT, T], offset=64 * K1)
        bcT = at("bcT", [P, 2 * G, T], offset=72 * K1)
        cbT = at("cbT", [P, G, 3 * P])
        conv_in = at("conv_in", [P, 2, T + 4])
        conv_out = at("conv_out", [P, 2, 2, T])
        prob = at("prob", [P, 2, 3 * P])
        probT = at("probT", [P, 2, 3 * P])
        decay, mT = prob, probT
        w_fd = at("w_fd", [P, KD, 2 * H])
        cum, ncum = at("cum", [P, T], F32R), at("ncum", [P, T], F32R)
        sel = at("sel", [P, 2 * H], F32R)
        sel_f = at("sel_f", [P, 2 * H])
        ident_bf = at("ident_bf", [P, P], BF16)
        mask_q, mask_s = at("mask_q", [P, P], BF16), at("mask_s", [P, P], BF16)
        dt_tok = at("dt_tok", [P, TT, 2 * H])
        d_all = at("d_all", [P, H])
        neg_max = at("neg_max", [P, H, TT])
        row_sum = at("row_sum", [P, H, TT])
        row_inv = at("row_inv", [P, H, TT])
        ssq, y_root, y_rms = at("ssq", [P, 2, TT]), at("y_root", [P, TT]), at("y_rms", [P, TT])
        fdc = at("fdc", [2 * H, 4])
        xtok = at("xtok", [P, TT, D], offset=40 * K1)
        ptok = at("ptok", [P, TT, DP], offset=56 * K1)
        par_rows = at("par_rows", [P, 3, P], offset=58 * K1)
        mix_rows = at("mix_rows", [KD, P], offset=60 * K1)
        fdw = at("fdw", [2 * H, 8, T], offset=64 * K1)
        mixHi, mixLo = at("mixHi", [P, KD, T], F32R, 0), at("mixLo", [P, KD, T], F32R, 16 * K1)
        actHi, actLo = at("actHi", [P, FT, T], F32R, 0), at("actLo", [P, FT, T], F32R, 4 * FT * T)
        top[0] = 8 * FT * T
        gate_in = at("gate_in", [P, 2, 2, T + 4])
        gate_out = at("gate_out", [P, 2, T])
        silu_g = at("silu_g", [P, 2, T])
        up = at("up", [P, 2, T])
        out_tok = at("out_tok", [P, TT, D], offset=0)
        pg_in = at("pg_in", [P, 2, 2, T], offset=16 * K1)
        pg_sig = at("pg_sig", [P, 2, 2, T], offset=20 * K1)
        finT = at("finT", [P, KD, T], offset=32 * K1)
        ps = ctx.enter_context(nc.psum_tensor("ps", [P, 8, 512], F32))

        par_ffn, par_ple, par_fin = (par[:, 0, i * KD:(i + 1) * KD] for i in range(3))
        o = 3 * KD
        par_ssdn, o = par[:, 0, o:o + WT], o + WT
        par_cb, o = par[:, 0, o:o + CT], o + CT
        par_fb = par[:, 0, o:o + FT]
        par_spans = (o + FT, KC * CT + FT, 2 * FT)
        assert max(par_spans) <= P
        par_cw = [par[:, 1, i * CT:(i + 1) * CT] for i in range(KC)]
        par_fw = [par[:, 1, KC * CT:KC * CT + FT], par[:, 2, 0:FT], par[:, 2, FT:2 * FT]]

        w_landed = [sem(f"w_landed{s}") for s in range(RING)]
        w_hi_made, w_lo_made, w_used = sem("w_hi_made"), sem("w_lo_made"), sem("w_used")
        gain_landed, gain_turned, gain_copied = sem("gain_landed"), sem("gain_turned"), sem("gain_copied")
        par_landed, p_landed = sem("par_landed"), sem("p_landed")
        x_landed = [sem(f"x_landed{j}") for j in range(NDN)]
        fd_landed, small_landed, alog_landed = sem("fd_landed"), sem("small_landed"), sem("alog_landed")
        pool_step, consts_made, masks_made = sem("pool_step"), sem("consts_made"), sem("masks_made")
        par_turned, par_copied, p_turned, p_hi_made, p_lo_made = map(
            sem, ("par_turned", "par_copied", "p_turned", "p_hi_made", "p_lo_made"))
        x_turned, x_new = sem("x_turned"), sem("x_new")
        h_hi_made, h_lo_made = sem("h_hi_made"), sem("h_lo_made")
        squares_made, sums_made, root_made, rms_made = map(sem, ("squares_made", "sums_made", "root_made", "rms_made"))
        dve_evac, act_evac = sem("dve_evac"), sem("act_evac")
        conv_step, conv_made, silu_made = sem("conv_step"), sem("conv_made"), sem("silu_made")
        xs_turned, xs_copied, xdt_made = sem("xs_turned"), sem("xs_copied"), sem("xdt_made")
        cb_ready, cb_copied = sem("cb_ready"), sem("cb_copied")
        wfd_scaled, fd_ready, fd_step, fd_abs, fd_exp, a_exp, a_ready = map(
            sem, ("wfd_scaled", "fd_ready", "fd_step", "fd_abs", "fd_exp", "a_exp", "a_ready"))
        cum_ready, dt_turned, dt_copied = sem("cum_ready"), sem("dt_turned"), sem("dt_copied")
        s_ready, max_made, prob_made, prob_turned, prob_copied, o_ready, inv_made, y_made = map(
            sem, ("s_ready", "max_made", "prob_made", "prob_turned", "prob_copied", "o_ready", "inv_made", "y_made"))
        e_ready, decay_made, m_made, yo_ready, ys_made = map(
            sem, ("e_ready", "decay_made", "m_made", "yo_ready", "ys_made"))
        gated, gated_sq, ssq_made, y_root_made, y_rms_made, y_normed = map(
            sem, ("gated", "gated_sq", "ssq_made", "y_root_made", "y_rms_made", "y_normed"))
        y_turned, mix_hi_made, mix_lo_made = sem("y_turned"), sem("mix_hi_made"), sem("mix_lo_made")
        ffn_done, ffn_step, ffn_conv, ffn_silu, ffn_act, ffn_hi, ffn_lo = map(
            sem, ("ffn_done", "ffn_step", "ffn_conv", "ffn_silu", "ffn_act", "ffn_hi", "ffn_lo"))
        down_done = sem("down_done")
        ffn_out, ple_sig, ple_step, ple_scaled, out_turned, out_copied, out_final, stored = map(
            sem, ("ffn_out", "ple_sig", "ple_step", "ple_scaled", "out_turned", "out_copied", "out_final", "stored"))

        block = ctx.enter_context(nc.Block())

        def load_chunk(sp, n, src, q=0):
            if n >= RING:
                sp.wait_ge(w_lo_made, n + RING * q - RING + 1)
            sp.dma_start(w_raw[:, n % RING, :].rearrange("p (a c) -> p a c", a=2), src).then_inc(w_landed[n % RING], 16)

        def make_hi(act, n, q=0):
            act.wait_ge(w_landed[n % RING], 16 * (n // RING + q + 1))
            if n >= RING:
                act.wait_ge(w_used, n + RING * q - RING + 1)
            act.activation(w_hi[:, n % RING, :], w_raw[:, n % RING, :], ACT.Copy).then_inc(w_hi_made, 1)

        def make_lo(dve, n, q=0):
            dve.wait_ge(w_hi_made, n + RING * q + 1)
            dve.tensor_tensor(w_lo[:, n % RING, :], w_raw[:, n % RING, :], w_hi[:, n % RING, :],
                              ALU.subtract).then_inc(w_lo_made, 1)

        def chunk_of(g, c):
            return g.view[:, 2 * c:2 * c + 2, g.col:g.col + COLS]

        def multiply(pe, n, opHi, opLo, tiles, bank_of, q=0):
            pe.wait_ge(w_lo_made, n + RING * q + 1)
            s = n % RING
            for i, (k, m, start, stop) in enumerate(tiles):
                dst = ps[:, bank_of[m // 2], (m % 2) * T:(m % 2) * T + T]
                hi, lo = w_hi[:, s, i * P:(i + 1) * P], w_lo[:, s, i * P:(i + 1) * P]
                pe.matmul(dst, hi, opHi(k), start=start and m % 2 == 0, stop=False, skip_group_check=True)
                pe.matmul(dst, hi, opLo(k), start=False, stop=False, skip_group_check=True)
                mm = pe.matmul(dst, lo, opHi(k), start=False, stop=stop, skip_group_check=True)
            return mm.then_inc(w_used, 1)

        def pair_tiles(first, last):
            return [(kk, m, first and kk == 0, last and kk == 1) for kk in range(2) for m in range(MT)]

        down_banks = (SET_B, SET_D, SET_C, SET_A)

        def ple_banks(i):
            return ((SET_B, SET_D), (SET_C, SET_A))[i % 2]

        def multiply_group(pe, n, g, c):
            opHi, opLo = {"h": (hHi, hLo), "mix": (mixHi, mixLo), "p": (pHi, pLo)}[g.operand]
            first, last = c == 0, c == g.chunks - 1
            if not g.by_token:
                return multiply(pe, n, lambda k: opHi[:, 2 * c + k, :], lambda k: opLo[:, 2 * c + k, :],
                                pair_tiles(first, last), g.banks)
            pe.wait_ge(w_lo_made, n + 1)
            s = n % RING
            for kk in range(2):
                hi, lo = (w[:, s, kk * COLS:(kk + 1) * COLS] for w in (w_hi, w_lo))
                for t in range(TT):
                    dst = ps[:, g.banks[t], :]
                    a, b = (o_[:, 2 * c + kk, t * P:(t + 1) * P] for o_ in (opHi, opLo))
                    pe.matmul(dst, a, hi, start=first and kk == 0, stop=False)
                    pe.matmul(dst, a, lo, start=False, stop=False)
                    mm = pe.matmul(dst, b, hi, start=False, stop=last and kk == 1)
            return mm.then_inc(w_used, 1)

        evacuated = {n: (dve_evac, i + 1) for i, n in enumerate(("q0", "k0", "q1", "k1"))}
        evacuated |= {n: (act_evac, i + 1) for i, n in enumerate(("v0", "v1", "z0", "z1"))}
        evacuated |= {n: (conv_step, CONV_STEPS * (2 * i + 1) + 1) for i, n in enumerate(("bc", "x0", "x1"))}
        NORM = KD // 2
        evacuated |= {f"o{i}": (x_new, NORM + 2 * i + 2) for i in range(NDN)}
        evacuated |= {f"dn{i}": (x_new, 2 * NORM + 2 * i + 2) for i in range(NDN)}

        bank_user = {}

        def wait_banks(pe, name, banks):
            waits = {}
            for b in banks:
                if b in bank_user:
                    s, val = bank_user[b]
                    waits[s.name] = (s, max(val, waits.get(s.name, (s, 0))[1]))
                bank_user[b] = evacuated[name]
            for s, val in waits.values():
                pe.wait_ge(s, val)

        LEAD = 3
        end = {g.name: done[g.name] for g in in_groups + out_groups}
        pe_after, act_after, dve_after = {}, {}, {}

        def after(table, n, what, *args):
            table.setdefault(n, []).append((what, args))

        def plan():
            def all_after(n, name, *args):
                after(pe_after, n, name, *args)
                after(act_after, n + LEAD, name, *args)
                after(dve_after, n + LEAD, name, *args)

            all_after(end["q0"], "stats0")
            for g in in_groups:
                if g.by_token:
                    after(act_after, end[g.name] + LEAD, "leave", g)
                elif g.name[0] in "qk":
                    after(dve_after, end[g.name] + LEAD, "leave", g)
            for i, g in enumerate(("bc", "x0", "x1")):
                for b in range(2):
                    n = end[g] + LEAD + 3 * b
                    after(dve_after, n, "conv_in_", g, b)
                    after(dve_after, n + 1, "conv_taps", 2 * i + b)
                    after(act_after, n + 2, "conv_silu", 2 * i + b)
            all_after(end["q0"] + 1, "turn_par")
            all_after(end["q0"] + 2, "fd")
            after(dve_after, end["q0"] + 4 + LEAD, "softplus")
            after(dve_after, end["q0"] + 6 + LEAD, "cumulate")
            all_after(end["bc"] + 4, "cums")
            all_after(end["bc"] + 10, "cb", 0)
            all_after(end["bc"] + 13, "cb", 1)
            all_after(end["x0"] + 7, "turn_xs", 0)
            all_after(end["x1"] + 7, "turn_xs", 1)
            b0 = end["x1"] + 8
            for i in range(H + 1):
                all_after(b0 + i * 6 // 5, "ssd", i)
            a0 = end["v0"]
            for i in range(H + 2):
                all_after(a0 + i, "fox", i)
            for b in range(WT // 2):
                all_after(a0 + H + 2 + b, "turn_fox", b)
            z0, z1 = end["z0"] + LEAD, end["z1"] + LEAD
            after(dve_after, z0 + 2, "gate_mul", 0)
            after(act_after, z0 + 3, "gate_square", 0)
            after(dve_after, z1 + 1, "gate_mul", 1)
            after(act_after, z1 + 1, "gate_square", 1)
            after(dve_after, z1 + 2, "gate_norm")
            after(act_after, z1 + 2, "gate_norm")
            for b in range(WT // 2):
                all_after(end["z1"] + 5 + b, "turn_gated", b)
            for g in ("o0", "o1", "o2"):
                i = int(g[1])
                after(act_after, end[g] + LEAD, "leave_out", i)
                after(dve_after, end[g] + LEAD, "leave_out", i)

        plan()

        STATS1_AT = 11
        UNIT_AT = (3, 9)
        U_CONV, U_TAPS, U_SILU, U_ACT, U_HI, U_LO = range(6)
        STATS2_AT = 7
        group_end = [(KP + 1) * (i + 1) - 1 for i in range(NDN - 1)]
        ple_leave_at = {n + LEAD: i for i, n in enumerate(group_end)}
        ple_scale_at = {n + LEAD + 1: i for i, n in enumerate(group_end)}
        turn_out_at = {n + LEAD + 1: i for i, n in enumerate(group_end)}
        copy_out_at = {n + LEAD + 3: i for i, n in enumerate(group_end)}

        def run(table, n, steps):
            for name, args in table.get(n, ()):
                if name in steps:
                    steps[name](*args)

        def flush(table, n, steps):
            for m in sorted(k for k in table if k >= n):
                run(table, m, steps)

        S_BANKS = (0, 1, 7)
        TURN_BANK, SPARE_BANK = 6, 7
        X_BANKS = (0, 1, 6, 7)
        XS_BANKS = (0, 1, 6, 7)
        groups = {g.name: g for g in in_groups + out_groups}
        s_bank = lambda h: S_BANKS[h % 3]

        @block.sync
        def _(sp):
            as_rows = lambda a: a.rearrange("(r p) -> r p", p=P)
            sp.dma_start(mix_rows[:, :], as_rows(mix_norm_w[0])).then_inc(gain_landed, 16)
            x_v = x[0].rearrange("(t p) n -> p t n", p=P)
            for j in range(NDN):
                cols = slice(j * COLS, (j + 1) * COLS)
                sp.dma_start(xtok[:, :, cols], x_v[:, :, cols]).then_inc(x_landed[j], 16)
                load_chunk(sp, j, chunk_of(*front[j]))
            with nc.allow_non_contiguous_dma(reason="the forget and dt columns of w_in are 16 wide"):
                sp.dma_start(w_fd[:, :, 0:H], win_v[:, :, c_f:c_f + H]).then_inc(fd_landed, 16)
                sp.dma_start(w_fd[:, :, H:2 * H], win_v[:, :, c_dt:c_dt + H]).then_inc(fd_landed, 16)
            load_chunk(sp, NDN, chunk_of(*front[NDN]))
            sp.dma_start(ptok[:, :, :], p[0, 0].rearrange("(t p) c -> p t c", p=P)).then_inc(p_landed, 16)
            column = lambda a: a[0].rearrange("(h a) -> h a", a=1)
            sp.dma_start(fdc[0:H, 0:1], column(fox_forget_bias)).then_inc(small_landed, 16)
            sp.dma_start(fdc[H:2 * H, 0:1], column(ssd_dt_bias)).then_inc(small_landed, 16)
            sp.wait_ge(consts_made, 1)
            sp.dma_start(fdc[H:2 * H, 2:3], column(ssd_A_log)).then_inc(alog_landed, 16)
            sp.dma_start(d_all[:, :], ssd_D[0:1, :].to_broadcast([P, H])).then_inc(small_landed, 16)
            load_chunk(sp, NDN + 1, chunk_of(*front[NDN + 1]))

            def param_rows(dst_tile, at_row, src, n):
                sp.dma_start(par_rows[at_row:at_row + n, dst_tile, :], as_rows(src)).then_inc(par_landed, 16)

            row = 0
            for src, n in ((ffn_norm_w[0], KD), (ple_norm_w[0], KD), (final_norm_w, KD),
                           (ssd_norm_w[0], WT), (ssd_conv_b[0], CT), (ffn_conv_b[0], FT)):
                param_rows(0, row, src, n)
                row += n
            for i in range(KC):
                param_rows(1, i * CT, ssd_conv_w[0, i], CT)
            param_rows(1, KC * CT, ffn_conv_w[0, 0], FT)
            param_rows(2, 0, ffn_conv_w[0, 1], FT)
            param_rows(2, FT, ffn_conv_w[0, 2], FT)
            for n in range(NDN + 2, len(front)):
                load_chunk(sp, n, chunk_of(*front[n]))
            gu = wgu_v.rearrange("p k (a n) -> p k a n", a=2)
            for k in range(KD):
                load_chunk(sp, n_ffn + k, gu[:, k, :, 0:COLS])
            with sp.Fori(0, NG // 2) as i:
                for j in range(2):
                    for k in range(KD):
                        load_chunk(sp, n_ffn + (1 + j) * KD + k,
                                   gu[:, k, :, bass.ds(i * (2 * COLS) + (1 + j) * COLS, COLS)], i * (2 * KD // RING))
            for g in range(NDN):
                n0 = n_down + g * KDN
                cols = slice(g * COLS, (g + 1) * COLS)
                for c in range(2):
                    load_chunk(sp, n0 + c, wdn_v[:, 2 * c:2 * c + 2, cols])
                with sp.Fori(0, KDN // RING) as q:
                    for j in range(RING):
                        load_chunk(sp, n0 + 2 + j, wdn_v[:, bass.ds(q * (2 * RING) + 2 * (2 + j), 2), cols], q)
            for i, (g, c) in enumerate(tail):
                load_chunk(sp, n_ple + i, chunk_of(g, c))
            out_v = out[0].rearrange("(t p) n -> p t n", p=P)
            for i in range(TT * NDN):
                t, j = i // NDN, i % NDN
                sp.wait_ge(out_final, i + 1)
                sp.dma_start(out_v[:, t, j * COLS:(j + 1) * COLS], out_tok[:, t, j * COLS:(j + 1) * COLS]).then_inc(stored, 16)
            sp.wait_ge(stored, 16 * TT * NDN)

        @block.gpsimd
        def _(pool):
            steps = [0]

            def link(ins):
                steps[0] += 1
                ins.then_inc(pool_step, 1)

            def linked():
                pool.wait_ge(pool_step, steps[0])

            def select(dst, src, keep, fill, base, per_partition, per_column, n):
                return pool.affine_select(out=dst, in_=src, compare_op=keep, fill=fill, base=base,
                                          pattern=[[per_column, n]], channel_multiplier=per_partition)

            pool.memset(fdc[:, 2:3], 0.0).then_inc(consts_made, 1)
            link(pool.memset(ident[:, :], 0.0))
            link(pool.memset(sel_f[:, :], 0.0))
            link(pool.memset(fdc[:, 1:2], -1.0))
            link(pool.memset(fdw[:, 0, :], 1.0))
            link(pool.memset(mask_q[:, :], 0.0))
            link(pool.memset(mask_s[:, :], 0.0))
            pool.memset(eps[:, :], EPS).then_inc(consts_made, 1)
            linked()
            select(ident[:, :], ident[:, :], ALU.not_equal, 1.0, 0, 1, -1, P).then_inc(consts_made, 1)
            pool.memset(ones[:, :], 1.0).then_inc(consts_made, 1)
            link(select(sel_f[:, :], sel_f[:, :], ALU.not_equal, 1.0, 0, 1, -1, 2 * H))
            linked()
            select(sel_f[:, :], sel_f[:, :], ALU.not_equal, 1.0, -2 * H, 1, -1, 2 * H).then_inc(masks_made, 1)
            select(fdc[:, 1:2], fdc[:, 1:2], ALU.is_ge, 1.0, H - 1, -1, 0, 1).then_inc(masks_made, 1)
            select(fdw[:, 0, P:P + 1], fdw[:, 0, P:P + 1], ALU.is_ge, 0.0, H - 1, -1, 0, 1).then_inc(masks_made, 1)
            select(mask_q[:, :], mask_q[:, :], ALU.is_ge, MASKED, 0, 1, -1, P).then_inc(masks_made, 1)
            select(mask_s[:, :], mask_s[:, :], ALU.is_ge, MASKED, 0, -1, 1, P).then_inc(masks_made, 1)
            pool.wait_ge(masks_made, 5)
            for i, half in enumerate((kE[P // 2:P, :, :], kO[0:P // 2, :, :], conv_in[:, :, 0:4])):
                pool.memset(half, 0.0).then_inc(masks_made, 1)
                pool.wait_ge(masks_made, 6 + i)
            for norm in range(4):
                if norm == 1:
                    pool.wait_ge(a_exp, 1)
                    select(fdc[:, 3:4], fdc[:, 3:4], ALU.is_ge, 1.0, -H, 1, 0, 1).then_inc(a_ready, 1)
                for b in range(KD // 2):
                    pool.wait_ge(x_new, norm * (KD // 2) + b + 1)
                    if b == 0 and norm > 0:
                        pool.wait_ge(sums_made, norm)
                    pair = xT[:, 2 * b:2 * b + 2, :]
                    if b == 0:
                        link(pool.tensor_tensor(sumsq[:, :, :], pair, pair, ALU.mult))
                        continue
                    linked()
                    link(pool.tensor_tensor(sq[:, :, :], pair, pair, ALU.mult))
                    linked()
                    ins = pool.tensor_tensor(sumsq[:, :, :], sumsq[:, :, :], sq[:, :, :], ALU.add)
                    if b == KD // 2 - 1:
                        ins.then_inc(squares_made, 1)
                    else:
                        link(ins)

        @block.tensor
        def _(pe):
            pe.wait_ge(consts_made, 4)
            pe.wait_ge(gain_landed, 16)
            pe.transpose(ps[:, 4, 0:KD], mix_rows[:, :], ident[0:KD, 0:KD]).then_inc(gain_turned, 1)

            def turn_x(b):
                if b % 2 == 0:
                    pe.wait_ge(x_landed[b // 2], 16)
                if b >= len(X_BANKS):
                    pe.wait_ge(x_new, b - len(X_BANKS) + 1)
                for kk in range(2):
                    for t in range(TT):
                        k = 2 * b + kk
                        mm = pe.transpose(ps[:, X_BANKS[b % len(X_BANKS)], kk * T + t * P:kk * T + t * P + P],
                                          xtok[:, t, k * P:(k + 1) * P], ident[:, :])
                mm.then_inc(x_turned, 1)

            for b in range(len(X_BANKS)):
                turn_x(b)

            def turn_par():
                pe.wait_ge(par_landed, 16 * 13)
                pe.wait_ge(x_new, NORM)
                for i, r in enumerate(par_spans):
                    mm = pe.transpose(ps[:, 1, i * P:i * P + r], par_rows[0:r, i, :], ident[0:r, 0:r])
                mm.then_inc(par_turned, 1)

            def turn_p():
                pe.wait_ge(p_landed, 16)
                pe.wait_ge(x_new, NORM - 1)
                for kk in range(2):
                    for t in range(TT):
                        mm = pe.transpose(ps[:, 0, kk * T + t * P:kk * T + t * P + P],
                                          ptok[:, t, kk * P:(kk + 1) * P], ident[:, :])
                mm.then_inc(p_turned, 1)

            def stats(norm, bank, columns=True, rows_=True):
                pe.wait_ge(squares_made, norm + 1)
                if rows_:
                    for j in range(2):
                        mm = pe.matmul(ps[:, bank, 0:T], ones[:, :], sumsq[:, j, :], start=j == 0, stop=j == 1,
                                       skip_group_check=True)
                if columns:
                    for t in range(TT):
                        for j in range(2):
                            mm = pe.matmul(ps[:, bank, T + t:T + t + 1], sumsq[:, j, t * P:(t + 1) * P], ones[:, 0:1],
                                           start=j == 0, stop=j == 1, skip_group_check=True)
                mm.then_inc(sums_made, 1)

            def stats0():
                turn_p()
                pe.wait_ge(x_new, KD // 2)
                stats(0, SPARE_BANK)

            def fd():
                pe.wait_ge(wfd_scaled, 1)
                for k in range(KD):
                    mm = pe.matmul(ps[0:2 * H, TURN_BANK, 0:T], w_fd[:, k, :], xT[:, k, :],
                                   start=k == 0, stop=k == KD - 1)
                mm.then_inc(fd_ready, 1)

            def cums():
                pe.wait_ge(fd_step, SOFTPLUS_STEPS)
                pe.wait_ge(root_made, 1)
                for t in range(TT):
                    mm = pe.transpose(ps[:, SPARE_BANK, t * 2 * H:(t + 1) * 2 * H],
                                      fdw[:, 6, t * P:(t + 1) * P], ident[0:2 * H, 0:2 * H])
                mm.then_inc(dt_turned, 1)

            def cb(g):
                if g == 0:
                    pe.wait_ge(silu_made, 2)
                    pe.wait_ge(dt_copied, 1)
                else:
                    pe.wait_ge(cb_copied, g)
                for s, l0, width, dst in ((0, 0, T, 0), (1, P, P, T)):
                    mm = pe.matmul(ps[:, SPARE_BANK, dst:dst + width], bcT[:, g, s * P:(s + 1) * P],
                                   bcT[:, G + g, l0:l0 + width], start=True, stop=True, skip_group_check=True)
                mm.then_inc(cb_ready, 1)

            def cum_terms(bank, j, by_key):
                one = sel[:, j:j + 1].to_broadcast([P, P])
                row, col = (ncum, cum) if by_key else (cum, ncum)
                blocks = ((0, 0, T, 0), (1, P, P, T)) if by_key else ((0, 0, P, 0), (1, 0, T, P))
                diagonal = (0, T)
                for i, (r, c0, width, dst) in enumerate(blocks):
                    where = ps[:, bank, dst:dst + width]
                    pe.matmul(where, row[:, r * P:(r + 1) * P], sel[:, j:j + 1].to_broadcast([P, width]),
                              start=by_key and i == 0, stop=False, skip_group_check=True)
                    pe.matmul(where, one, col[:, c0:c0 + width], start=False, stop=False, skip_group_check=True)
                if by_key:
                    pe.matmul(ps[:, bank, P:T], one, cum[:, P - 1:P].to_broadcast([P, P]), start=False, stop=False,
                              skip_group_check=True)
                for dst in diagonal:
                    mm = pe.matmul(ps[:, bank, dst:dst + P], ident_bf[:, :], (mask_s if by_key else mask_q)[:, :],
                                   start=False, stop=True, skip_group_check=True)
                return mm

            def fox(i):
                if 1 <= i <= H:
                    h = i - 1
                    pe.wait_ge(prob_made, 2 * h + 2)
                    if h >= 1:
                        pe.wait_ge(prob_copied, h)
                    for b in range(3):
                        mm = pe.transpose(ps[:, TURN_BANK, b * P:(b + 1) * P], prob[:, h % 2, b * P:(b + 1) * P], ident[:, :])
                    mm.then_inc(prob_turned, 1)
                if i >= 2:
                    h = i - 2
                    pe.wait_ge(prob_copied, h + 1)
                    if h % (H // 2) == 0:
                        pe.wait_ge(*evacuated[f"v{h // (H // 2)}"])
                    pT = lambda b: probT[:, h % 2, b * P:(b + 1) * P]
                    val = lambda t: v[:, t, h * HD:(h + 1) * HD]
                    o0, o1 = (ps[:, s_bank(h), 3 * P + t * HD:3 * P + (t + 1) * HD] for t in range(2))
                    pe.matmul(o0, pT(0), val(0), start=True, stop=True, skip_group_check=True)
                    pe.matmul(o1, pT(1), val(0), start=False, stop=False, skip_group_check=True)
                    pe.matmul(o1, pT(2), val(1), start=False, stop=True, skip_group_check=True).then_inc(o_ready, 1)
                if i < H:
                    h = i
                    bank = s_bank(h)
                    if h == 0:
                        pe.wait_ge(*evacuated["k1"])
                        pe.wait_ge(ys_made, H)
                    if h >= 3:
                        pe.wait_ge(y_made, h - 2)
                    keys = (kE, kO)[h % 2]
                    pe.matmul(ps[:, bank, 0:P], qT[:, h // 2, 0:P], keys[:, h // 2, 0:P],
                              start=True, stop=False, skip_group_check=True)
                    pe.matmul(ps[:, bank, P:3 * P], qT[:, h // 2, P:T], keys[:, h // 2, :],
                              start=False, stop=False, skip_group_check=True)
                    cum_terms(bank, h, by_key=False).then_inc(s_ready, 1)

            def ssd(i):
                if i >= 1:
                    h = i - 1
                    pe.wait_ge(m_made, h + 1)
                    m = lambda b: mT[:, h % 2, b * P:(b + 1) * P]
                    val = lambda t: xdt[:, t, h * HD:(h + 1) * HD]
                    o0, o1 = (ps[:, s_bank(h), 3 * P + t * HD:3 * P + (t + 1) * HD] for t in range(2))
                    pe.matmul(o0, m(0), val(0), start=True, stop=True, skip_group_check=True)
                    pe.matmul(o1, m(1), val(0), start=False, stop=False, skip_group_check=True)
                    pe.matmul(o1, m(2), val(1), start=False, stop=True, skip_group_check=True).then_inc(yo_ready, 1)
                if i < H:
                    h = i
                    if h == 0:
                        pe.wait_ge(cum_ready, 1)
                        pe.wait_ge(xdt_made, 2 * TT)
                    if h >= 3:
                        pe.wait_ge(ys_made, h - 2)
                    cum_terms(s_bank(h), H + h, by_key=True).then_inc(e_ready, 1)

            def turn_xs(half):
                pe.wait_ge(silu_made, 4 + 2 * half)
                if half == 0:
                    pe.wait_ge(par_copied, 1)
                    pe.wait_ge(p_lo_made, 1)
                else:
                    pe.wait_ge(cum_ready, 1)
                    pe.wait_ge(cb_copied, G)
                for t in range(TT):
                    for j in range(WT // 2):
                        mm = pe.transpose(ps[:, XS_BANKS[TT * half + t], j * P:(j + 1) * P],
                                          xsT[:, WT // 2 * half + j, t * P:(t + 1) * P], ident[:, :])
                    mm.then_inc(xs_turned, 1)

            def turn_y(src, n):
                if n >= 2:
                    pe.wait_ge(mix_lo_made, n - 1)
                for kk in range(2):
                    for t in range(TT):
                        k = 2 * (n % (WT // 2)) + kk
                        mm = pe.transpose(ps[:, 6 + n % 2, kk * T + t * P:kk * T + t * P + P],
                                          src[:, t, k * P:(k + 1) * P], ident[:, :])
                mm.then_inc(y_turned, 1)

            def turn_fox(b):
                pe.wait_ge(y_made, H)
                turn_y(y_fox, b)

            def turn_gated(b):
                pe.wait_ge(y_normed, TT)
                turn_y(z, WT // 2 + b)

            steps = dict(turn_par=turn_par, stats0=stats0, fd=fd, cums=cums, cb=cb, fox=fox, ssd=ssd, turn_xs=turn_xs,
                         turn_fox=turn_fox, turn_gated=turn_gated)
            for n, (g, c) in enumerate(front):
                if c == 0:
                    wait_banks(pe, g.name, g.banks)
                    if g.name == "o2":
                        pe.wait_ge(y_made, H)
                    if g.name == "o3":
                        pe.wait_ge(mix_lo_made, WT)
                if g.name == "q0":
                    pe.wait_ge(h_lo_made, 2 * c + 2)
                if g.name == "bc" and c == 0:
                    pe.wait_ge(gain_copied, 1)
                if g.name == "o0":
                    pe.wait_ge(mix_lo_made, c + 1)
                multiply_group(pe, n, g, c)
                if n + len(X_BANKS) < NORM:
                    turn_x(n + len(X_BANKS))
                run(pe_after, n, steps)
            flush(pe_after, len(front), steps)

            def ffn_chunk(n, k, half, q=0):
                return multiply(pe, n, lambda _: hHi[:, k, :], lambda _: hLo[:, k, :],
                                [(k, m, k == 0, k == KD - 1) for m in range(2 * MT)],
                                [4 * half + b for b in range(4)], q)

            for k in range(KD):
                if k == 0:
                    for name in ("o1", "o2"):
                        pe.wait_ge(*evacuated[name])
                pe.wait_ge(h_lo_made, KD + k + 1)
                ffn_chunk(n_ffn + k, k, 0)
                if k == KD // 2:
                    pe.wait_ge(*evacuated["o0"])
                if k == STATS1_AT:
                    stats(1, 4, columns=False)
            pe.wait_ge(root_made, 2)
            with pe.Fori(0, NG // 2) as i:
                for j in range(2):
                    for k in range(KD):
                        if k == 0:
                            pe.wait_ge(ffn_out, i * 4 + (1, 3)[j])
                        ffn_chunk(n_ffn + (1 + j) * KD + k, k, 1 - j, i * (2 * KD // RING))

            for g in range(NDN):
                n0 = n_down + g * KDN

                def chunk(j, q, first=False, last=False):
                    at_ = (lambda t, k: t[:, 2 * j + k, :]) if isinstance(q, int) else \
                        (lambda t, k: t[:, bass.ds(q * (2 * RING) + (2 * j + k), 1), :])
                    return multiply(pe, n0 + j, lambda k: at_(actHi, k), lambda k: at_(actLo, k),
                                    pair_tiles(first, last), down_banks[g], q)

                pe.wait_ge(ffn_lo, 2 * (NG - 1) if g == 0 else 2 * NG)
                for j in range(2):
                    chunk(j, 0, first=j == 0)
                with pe.Fori(0, KDN // RING - 1) as q:
                    for j in range(2, 2 + RING):
                        chunk(j, q)
                if g == 0:
                    pe.wait_ge(ffn_lo, 2 * NG)
                for j in range(KDN - RING, KDN):
                    chunk(j, 0, last=j == KDN - 1)

            def turn_out(i):
                gate_banks, _ = ple_banks(i)
                pe.wait_ge(ple_scaled, MT * (i + 1))
                pe.wait_ge(ple_step, 4 * (i + 1))
                for t in range(TT):
                    for m in range(MT):
                        mm = pe.transpose(ps[:, gate_banks[t], m * P:(m + 1) * P],
                                          finT[:, MT * i + m, t * P:(t + 1) * P], ident[:, :])
                    mm.then_inc(out_turned, 1)

            for i, (g, c) in enumerate(tail):
                if g.name == "pp0":
                    pe.wait_ge(*evacuated["dn1"])
                elif g.name == "pp1":
                    pe.wait_ge(*evacuated["dn3"])
                    pe.wait_ge(root_made, 3)
                elif c == 0 and int(g.name[2]) >= 2:
                    j = int(g.name[2]) - 2
                    pe.wait_ge(ple_step, 4 * (j + 1))
                    pe.wait_ge(out_copied, TT * (j + 1))
                if g.name == "pg0":
                    pe.wait_ge(h_lo_made, 2 * KD + 2 * c + 2)
                multiply_group(pe, n_ple + i, g, c)
                if i == STATS2_AT:
                    stats(2, 0, columns=False)
                if i in turn_out_at:
                    turn_out(turn_out_at[i])
            turn_out(NDN - 1)
            pe.wait_ge(out_copied, TT * NDN)
            stats(3, 0, rows_=False)

        @block.scalar
        def _(act):
            def copy(dst, src, scale=1.0):
                return act.activation(dst, src, ACT.Copy, scale=scale)

            def make_h(norm, k, gain):
                act.wait_ge(x_new, norm * NORM + k // 2 + 1)
                copy(hHi[:, k, :], xT[:, k, :], gain[:, k:k + 1]).then_inc(h_hi_made, 1)

            def stats(norm, bank, a=0, b=T):
                act.wait_ge(sums_made, norm + 1)
                act.activation(root[:, a:b], ps[:, bank, a:b], ACT.Sqrt, bias=eps[:, :], scale=1.0 / D).then_inc(root_made, 1)

            def conv_silu(u):
                act.wait_ge(conv_step, CONV_STEPS * (u + 1))
                dst = bcT[:, 2 * u:2 * u + 2, :] if u < 2 else xsT[:, 2 * (u - 2):2 * (u - 2) + 2, :]
                act.activation(dst, conv_out[:, u % 2, :, :], ACT.Silu).then_inc(silu_made, 1)

            def leave(g):
                act.wait_ge(w_used, done[g.name] + 1)
                half = int(g.name[1])
                for t in range(TT):
                    dst = (v if g.name[0] == "v" else z)[:, t, half * COLS:(half + 1) * COLS]
                    ins = act.activation(dst, ps[:, g.banks[t], :], ACT.Copy if g.name[0] == "v" else ACT.Silu,
                                         scale=rms_col[:, t:t + 1])
                ins.then_inc(act_evac, 1)

            def p_hi():
                act.wait_ge(p_turned, 1)
                copy(pHi[:, :, :], ps[:, 0, :]).then_inc(p_hi_made, 1)

            def stats0():
                p_hi()
                stats(0, SPARE_BANK, 0, T + TT)

            def fd():
                act.wait_ge(fd_step, 2)
                act.activation(fdw[:, 2, :], fdw[:, 1, :], ACT.Abs).then_inc(fd_abs, 1)
                act.wait_ge(fd_abs, 1)
                act.activation(fdw[:, 3, :], fdw[:, 2, :], ACT.Exp, scale=-1.0).then_inc(fd_exp, 1)
                act.wait_ge(alog_landed, 16)
                act.activation(fdc[:, 3:4], fdc[:, 2:3], ACT.Exp).then_inc(a_exp, 1)

            def fox(i):
                if i >= 1 and i <= H:
                    h = i - 1
                    act.wait_ge(prob_turned, h + 1)
                    if h >= 2:
                        act.wait_ge(o_ready, h - 1)
                    copy(probT[:, h % 2, :], ps[:, TURN_BANK, 0:3 * P]).then_inc(prob_copied, 1)
                if i < H:
                    h = i
                    act.wait_ge(max_made, 2 * h + 2)
                    if h >= 2:
                        act.wait_ge(prob_turned, h - 1)
                    for t, (a, b) in enumerate(((0, P), (P, 3 * P))):
                        act.activation(prob[:, h % 2, a:b], ps[:, s_bank(h), a:b], ACT.Exp,
                                       bias=neg_max[:, h, t:t + 1], accum_out=row_sum[:, h, t:t + 1]).then_inc(prob_made, 1)

            def ssd(i):
                if i < H:
                    h = i
                    act.wait_ge(e_ready, h + 1)
                    if h >= 2:
                        act.wait_ge(m_made, h - 1)
                    act.activation(decay[:, h % 2, :], ps[:, s_bank(h), 0:3 * P], ACT.Exp).then_inc(decay_made, 1)

            def turn_fox(b):
                act.wait_ge(y_turned, b + 1)
                copy(mixHi[:, 2 * b:2 * b + 2, :], ps[:, 6 + b % 2, :]).then_inc(mix_hi_made, 1)

            def gate_square(half):
                act.wait_ge(gated, half + 1)
                cols = slice(half * COLS, (half + 1) * COLS)
                for t in range(TT):
                    act.activation(xdt[:, t, cols], z[:, t, cols], ACT.Square,
                                   accum_out=ssq[:, half, t:t + 1]).then_inc(gated_sq, 1)

            def gate_norm():
                act.wait_ge(ssq_made, 1)
                act.activation(y_root[:, :], ssq[:, 0, :], ACT.Sqrt, bias=eps[:, :], scale=1.0 / W).then_inc(y_root_made, 1)

            def turn_gated(b):
                act.wait_ge(y_turned, WT // 2 + b + 1)
                for kk in range(2):
                    k = 2 * b + kk
                    copy(mixHi[:, WT + k, :], ps[:, 6 + b % 2, kk * T:(kk + 1) * T],
                         par_ssdn[:, k:k + 1]).then_inc(mix_hi_made, 1)

            def leave_out(i):
                for k in range(MT * i, MT * (i + 1)):
                    make_h(1, k, par_ffn)

            steps = dict(leave=leave, stats0=stats0, fd=fd, fox=fox, ssd=ssd, turn_fox=turn_fox, conv_silu=conv_silu,
                         gate_square=gate_square, gate_norm=gate_norm, turn_gated=turn_gated, leave_out=leave_out)
            act.wait_ge(gain_copied, 1)
            act.wait_ge(consts_made, 4)
            for n in range(len(front)):
                if n < NORM:
                    for k in (2 * n, 2 * n + 1):
                        make_h(0, k, par_mix)
                make_hi(act, n)
                run(act_after, n, steps)
            for k in range(KD):
                make_hi(act, n_ffn + k)
                run(act_after, n_ffn + k, steps)
                if k == LEAD:
                    leave_out(NDN - 1)
                if k == STATS1_AT + LEAD:
                    stats(1, 4)

            def ffn_unit_silu(u):
                act.wait_ge(ffn_step, u * GATE_STEPS + GATE_STEPS)
                act.activation(silu_g[:, :, :], gate_out[:, :, :], ACT.Silu).then_inc(ffn_silu, 1)

            def ffn_unit_hi(u):
                act.wait_ge(ffn_act, u + 1)
                dst = actHi[:, 2 * u:2 * u + 2, :] if isinstance(u, int) else actHi[:, bass.ds(u * 2, 2), :]
                copy(dst, gate_out[:, :, :]).then_inc(ffn_hi, 1)

            with act.Fori(0, NG // 2) as i:
                for j in range(2):
                    for k in range(KD):
                        make_hi(act, n_ffn + (1 + j) * KD + k, i * (2 * KD // RING))
                        for b in range(2):
                            if k == UNIT_AT[b] + U_SILU:
                                ffn_unit_silu(i * 4 + (2 * j + b))
                            if k == UNIT_AT[b] + U_HI:
                                ffn_unit_hi(i * 4 + (2 * j + b))
            for g in range(NDN):
                n0 = n_down + g * KDN
                peeled = 18 if g == 0 else 6
                for c in range(peeled):
                    make_hi(act, n0 + c)
                    if g == 0:
                        for b in range(2):
                            if c == UNIT_AT[b] + U_SILU:
                                ffn_unit_silu(2 * (NG - 1) + b)
                            if c == UNIT_AT[b] + U_HI:
                                ffn_unit_hi(2 * (NG - 1) + b)
                    elif c == LEAD:
                        for k in range(MT * (g - 1), MT * g):
                            make_h(2, k, par_ple)
                with act.Fori(0, (KDN - peeled) // RING) as q:
                    for j in range(RING):
                        make_hi(act, n0 + peeled + j, q)

            def ple_sigmoid(i):
                for b in range(2):
                    act.wait_ge(ple_step, 4 * i + b + 1)
                    act.activation(pg_sig[:, b, :, :], pg_in[:, b, :, :], ACT.Sigmoid).then_inc(ple_sig, 1)

            def ple_scale(i):
                for k in range(MT * i, MT * (i + 1)):
                    act.wait_ge(x_new, 3 * NORM + k // 2 + 1)
                    copy(finT[:, k, :], xT[:, k, :], par_fin[:, k:k + 1]).then_inc(ple_scaled, 1)

            def copy_out(i):
                gate_banks, _ = ple_banks(i)
                for t in range(TT):
                    act.wait_ge(out_turned, TT * i + t + 1)
                    copy(out_tok[:, t, i * COLS:(i + 1) * COLS], ps[:, gate_banks[t], :]).then_inc(out_copied, 1)

            for i in range(len(tail)):
                make_hi(act, n_ple + i)
                if i == LEAD:
                    for k in range(MT * (NDN - 1), KD):
                        make_h(2, k, par_ple)
                if i == STATS2_AT + LEAD - 1:
                    stats(2, 0)
                for table, what in ((ple_leave_at, ple_sigmoid), (ple_scale_at, ple_scale), (copy_out_at, copy_out)):
                    if i in table:
                        what(table[i])
            ple_sigmoid(NDN - 1)
            ple_scale(NDN - 1)
            copy_out(NDN - 1)
            stats(3, 0, T, T + TT)

        @block.vector
        def _(dve):
            def make_h(norm, k, gain):
                dve.wait_ge(h_hi_made, norm * KD + k + 1)
                dve.scalar_tensor_tensor(hLo[:, k, :], xT[:, k, :], gain[:, k:k + 1], hHi[:, k, :],
                                         ALU.mult, ALU.subtract).then_inc(h_lo_made, 1)

            def add_to_residual(norm, i, banks):
                for b in range(2):
                    k = MT * i + 2 * b
                    dve.tensor_tensor(xT[:, k:k + 2, :], ps[:, banks[b], :].rearrange("p (a t) -> p a t", a=2),
                                      xT[:, k:k + 2, :], ALU.add).then_inc(x_new, 1)

            def stats(norm):
                dve.wait_ge(root_made, norm + 1)
                if norm == 0:
                    dve.reciprocal(rms_col[:, :], root[:, T:T + TT])
                if norm == 3:
                    dve.reciprocal(rms_col[:, :], root[:, T:T + TT]).then_inc(rms_made, 1)
                    return
                for j in range(2):
                    ins = dve.reciprocal(rms[:, j, :], root[:, 0:T])
                ins.then_inc(rms_made, 1)
                dve.wait_ge(rms_made, norm + 1)

            pair = lambda bank: ps[:, bank, :].rearrange("p (a t) -> p a t", a=2)

            def conv_channel(u):
                return WT + 2 * u if u < 2 else 2 * (u - 2)

            def conv_tap(u, back):
                for e in range(2):
                    dst, src = conv_out[:, u % 2, e, :], conv_in[:, e, 4 - back:4 - back + T]
                    ch = conv_channel(u) + e
                    weight = par_cw[KC - 1 - back][:, ch:ch + 1]
                    if back == 0:
                        ins = dve.tensor_scalar(dst, src, weight, par_cb[:, ch:ch + 1], ALU.mult, ALU.add)
                    else:
                        dve.wait_ge(conv_step, CONV_STEPS * u + 2 * back + e)
                        ins = dve.scalar_tensor_tensor(dst, src, weight, dst, ALU.mult, ALU.add)
                    ins.then_inc(conv_step, 1)

            def conv_in_(name, b):
                u = 2 * ("bc", "x0", "x1").index(name) + b
                dve.wait_ge(w_used, done[name] + 1)
                if u == 0:
                    dve.wait_ge(par_copied, 1)
                    dve.wait_ge(masks_made, 8)
                else:
                    dve.wait_ge(conv_step, CONV_STEPS * u)
                bank = groups[name].banks[b]
                dve.tensor_tensor(conv_in[:, :, 4:4 + T], pair(bank), rms[:, :, :], ALU.mult).then_inc(conv_step, 1)
                if u >= 2:
                    dve.wait_ge(silu_made, u - 1)
                dve.wait_ge(conv_step, CONV_STEPS * u + 1)
                for back in range(0, 2):
                    conv_tap(u, back)

            def conv_taps(u):
                for back in range(2, KC):
                    conv_tap(u, back)

            def leave(g):
                dve.wait_ge(w_used, done[g.name] + 1)
                for b in range(2):
                    bank = g.banks[b]
                    k = MT * int(g.name[1]) + 2 * b
                    if g.name[0] == "q":
                        ins = dve.scalar_tensor_tensor(qT[:, k:k + 2, :], pair(bank), HD ** -0.5, rms[:, :, :],
                                                       ALU.mult, ALU.mult)
                    else:
                        for keys, a in ((kE, 0), (kO, P // 2)):
                            r = slice(a, a + P // 2)
                            ins = dve.tensor_tensor(keys[r, k:k + 2, :], ps[r, bank, :].rearrange("p (a t) -> p a t", a=2),
                                                    rms[r, :, :], ALU.mult)
                    if b == 1:
                        ins.then_inc(dve_evac, 1)

            def stats0():
                dve.wait_ge(p_hi_made, 1)
                dve.tensor_tensor(pLo[:, :, :], pair(0), pHi[:, :, :], ALU.subtract).then_inc(p_lo_made, 1)
                stats(0)

            fd_count = [0]
            fdr = lambda i: fdw[:, i, :]

            def link(ins):
                fd_count[0] += 1
                ins.then_inc(fd_step, 1)
                dve.wait_ge(fd_step, fd_count[0])

            def fd():
                dve.wait_ge(fd_ready, 1)
                link(dve.tensor_tensor(fdr(1), ps[0:2 * H, TURN_BANK, 0:T], rms[0:2 * H, 0, :], ALU.mult))
                dve.wait_ge(small_landed, 48)
                dve.wait_ge(masks_made, 8)
                link(dve.tensor_scalar(fdr(1), fdr(1), fdc[:, 0:1], fdc[:, 1:2], ALU.add, ALU.mult))

            def softplus():
                dve.wait_ge(fd_exp, 1)
                link(dve.tensor_scalar(fdr(4), fdr(3), 2.0, None, ALU.add))
                link(dve.reciprocal(fdr(4), fdr(4)))
                link(dve.tensor_tensor(fdr(4), fdr(3), fdr(4), ALU.mult))
                link(dve.tensor_tensor(fdr(5), fdr(4), fdr(4), ALU.mult))
                link(dve.tensor_scalar(fdr(6), fdr(5), 1.0 / 15, None, ALU.mult))
                for n in (13, 11, 9):
                    link(dve.scalar_tensor_tensor(fdr(6), fdr(6), 1.0 / n, fdr(5), ALU.add, ALU.mult))

            def cumulate():
                for n in (7, 5, 3):
                    link(dve.scalar_tensor_tensor(fdr(6), fdr(6), 1.0 / n, fdr(5), ALU.add, ALU.mult))
                link(dve.scalar_tensor_tensor(fdr(6), fdr(6), 1.0, fdr(4), ALU.add, ALU.mult))
                link(dve.tensor_scalar(fdr(5), fdr(1), 0.0, None, ALU.max))
                link(dve.scalar_tensor_tensor(fdr(6), fdr(6), 2.0, fdr(5), ALU.mult, ALU.add))
                assert fd_count[0] == SOFTPLUS_STEPS
                dve.wait_ge(a_ready, 1)
                link(dve.tensor_scalar(fdr(7), fdr(6), fdc[:, 3:4], -1.0, ALU.mult, ALU.mult))
                link(dve.tensor_tensor_scan(fdr(1), fdr(0), fdr(7), 0.0, ALU.mult, ALU.add))
                n = 2 * H
                dve.memset(cum[2 * n:P, :].bitcast(F32), 0.0)
                dve.memset(ncum[2 * n:P, :].bitcast(F32), 0.0)
                link(dve.tensor_copy(cum[0:n, :], fdr(1)))
                link(dve.tensor_tensor(cum[n:2 * n, :], fdr(1), cum[0:n, :], ALU.subtract))
                dve.tensor_copy(sel[:, :], sel_f[:, :])
                dve.tensor_copy(ident_bf[:, :], ident[:, :])
                dve.tensor_scalar(ncum[0:2 * n, :], cum[0:2 * n, :], -1.0, None, ALU.mult).then_inc(cum_ready, 1)

            def cums():
                dve.wait_ge(dt_turned, 1)
                dve.tensor_copy(dt_tok[:, :, :], ps[:, SPARE_BANK, 0:TT * 2 * H].rearrange("p (t h) -> p t h", t=TT)).then_inc(dt_copied, 1)

            def cb(g):
                dve.wait_ge(cb_ready, g + 1)
                dve.tensor_copy(cbT[:, g, :], ps[:, SPARE_BANK, 0:3 * P]).then_inc(cb_copied, 1)

            def fox(i):
                if i >= 2:
                    h = i - 2
                    dve.wait_ge(prob_made, 2 * h + 2)
                    dve.reciprocal(row_inv[:, h, :], row_sum[:, h, :]).then_inc(inv_made, 1)
                    dve.wait_ge(inv_made, h + 1)
                    dve.wait_ge(o_ready, h + 1)
                    o_ = ps[:, s_bank(h), 3 * P:3 * P + TT * HD].rearrange("p (t d) -> p t d", t=TT)
                    dve.tensor_tensor(y_fox[:, :, h * HD:(h + 1) * HD], o_,
                                      row_inv[:, h, :].unsqueeze(2).to_broadcast([P, TT, HD]), ALU.mult).then_inc(y_made, 1)
                if i < H:
                    h = i
                    dve.wait_ge(s_ready, h + 1)
                    for t, (a, b) in enumerate(((0, P), (P, 3 * P))):
                        dve.reduce_max(neg_max[:, h, t:t + 1], ps[:, s_bank(h), a:b], AX_X, negate=True).then_inc(max_made, 1)

            def ssd(i):
                if i >= 1:
                    h = i - 1
                    dve.wait_ge(yo_ready, h + 1)
                    o_ = ps[:, s_bank(h), 3 * P:3 * P + TT * HD].rearrange("p (t d) -> p t d", t=TT)
                    cols = xs[:, :, h * HD:(h + 1) * HD]
                    dve.scalar_tensor_tensor(cols, cols, d_all[:, h:h + 1], o_, ALU.mult, ALU.add).then_inc(ys_made, 1)
                if i < H:
                    h = i
                    dve.wait_ge(decay_made, h + 1)
                    if h >= 2:
                        dve.wait_ge(yo_ready, h - 1)
                    dve.tensor_tensor(mT[:, h % 2, :], decay[:, h % 2, :], cbT[:, h * G // H, :], ALU.mult).then_inc(m_made, 1)

            def turn_xs(half):
                for t in range(TT):
                    i = TT * half + t
                    dve.wait_ge(xs_turned, i + 1)
                    cols = xs[:, t, half * COLS:(half + 1) * COLS]
                    dve.tensor_copy(cols, ps[:, XS_BANKS[i], :]).then_inc(xs_copied, 1)
                    if i == 0:
                        dve.wait_ge(dt_copied, 1)
                    dve.wait_ge(xs_copied, i + 1)
                    h0 = H + half * (H // 2)
                    dve.tensor_tensor(xdt[:, t, half * COLS:(half + 1) * COLS].rearrange("p (h d) -> p h d", d=HD),
                                      cols.rearrange("p (h d) -> p h d", d=HD),
                                      dt_tok[:, t, h0:h0 + H // 2].unsqueeze(2).to_broadcast([P, H // 2, HD]),
                                      ALU.mult).then_inc(xdt_made, 1)

            def turn_fox(b):
                dve.wait_ge(mix_hi_made, b + 1)
                dve.tensor_tensor(mixLo[:, 2 * b:2 * b + 2, :], pair(6 + b % 2), mixHi[:, 2 * b:2 * b + 2, :],
                                  ALU.subtract).then_inc(mix_lo_made, 1)

            def gate_mul(half):
                dve.wait_ge(ys_made, H)
                dve.wait_ge(*evacuated[f"z{half}"])
                cols = slice(half * COLS, (half + 1) * COLS)
                dve.tensor_tensor(z[:, :, cols], z[:, :, cols], xs[:, :, cols], ALU.mult).then_inc(gated, 1)

            def gate_norm():
                dve.wait_ge(gated_sq, 2 * TT)
                dve.tensor_tensor(ssq[:, 0, :], ssq[:, 0, :], ssq[:, 1, :], ALU.add).then_inc(ssq_made, 1)
                dve.wait_ge(y_root_made, 1)
                dve.reciprocal(y_rms[:, :], y_root[:, :]).then_inc(y_rms_made, 1)
                dve.wait_ge(y_rms_made, 1)
                for t in range(TT):
                    dve.tensor_scalar(z[:, t, :], z[:, t, :], y_rms[:, t:t + 1], None, ALU.mult).then_inc(y_normed, 1)

            def turn_gated(b):
                dve.wait_ge(mix_hi_made, WT // 2 + 2 * b + 2)
                for kk in range(2):
                    k = 2 * b + kk
                    ins = dve.scalar_tensor_tensor(mixLo[:, WT + k, :], ps[:, 6 + b % 2, kk * T:(kk + 1) * T],
                                                   par_ssdn[:, k:k + 1], mixHi[:, WT + k, :], ALU.mult, ALU.subtract)
                ins.then_inc(mix_lo_made, 1)

            def leave_out(i):
                dve.wait_ge(w_used, done[f"o{i}"] + 1)
                add_to_residual(1, i, out_groups[i].banks)
                for k in range(MT * i, MT * (i + 1)):
                    make_h(1, k, par_ffn)

            def turn_par():
                dve.wait_ge(par_turned, 1)
                for i, r in enumerate(par_spans):
                    ins = dve.tensor_copy(par[:, i, 0:r], ps[:, 1, i * P:i * P + r])
                ins.then_inc(par_copied, 1)

            def copy_x(b):
                dve.wait_ge(x_turned, b + 1)
                dve.tensor_copy(xT[:, 2 * b:2 * b + 2, :], pair(X_BANKS[b % len(X_BANKS)])).then_inc(x_new, 1)

            steps = dict(leave=leave, turn_par=turn_par, stats0=stats0, fd=fd, softplus=softplus, cumulate=cumulate,
                         cums=cums, cb=cb, conv_in_=conv_in_, conv_taps=conv_taps, fox=fox, ssd=ssd, turn_xs=turn_xs,
                         turn_fox=turn_fox, gate_mul=gate_mul, gate_norm=gate_norm, turn_gated=turn_gated,
                         leave_out=leave_out)
            dve.wait_ge(gain_turned, 1)
            dve.tensor_copy(par_mix[:, :], ps[:, 4, 0:KD]).then_inc(gain_copied, 1)
            dve.wait_ge(gain_copied, 1)
            copy_x(0)
            copy_x(1)
            for n in range(len(front)):
                if n < NORM:
                    for k in (2 * n, 2 * n + 1):
                        make_h(0, k, par_mix)
                make_lo(dve, n)
                if n + 2 < NORM:
                    copy_x(n + 2)
                if n == NORM:
                    dve.wait_ge(fd_landed, 32)
                    dve.tensor_tensor(w_fd[:, :, :], w_fd[:, :, :], par_mix[:, :].unsqueeze(2).to_broadcast([P, KD, 2 * H]),
                                      ALU.mult).then_inc(wfd_scaled, 1)
                run(dve_after, n, steps)
            for k in range(KD):
                make_lo(dve, n_ffn + k)
                run(dve_after, n_ffn + k, steps)
                if k == LEAD:
                    leave_out(NDN - 1)
                    dve.memset(gate_in[:, :, :, 0:4], 0.0).then_inc(ffn_out, 1)
                if k == STATS1_AT + LEAD:
                    stats(1)

            def ffn_unit_conv(u, half, b):
                reg = not isinstance(u, int)
                ch = lambda t, e: t[:, bass.ds(u * 2 + e, 1)] if reg else t[:, 2 * u + e:2 * u + e + 1]
                base = u * GATE_STEPS
                buf = gate_in[:, b, :, :]
                dve.tensor_tensor(buf[:, :, 4:4 + T], pair(4 * half + b), rms[:, :, :], ALU.mult).then_inc(ffn_step, 1)
                dve.wait_ge(ffn_step, base + 1)
                for e in range(2):
                    dve.tensor_scalar(gate_out[:, e, :], buf[:, e, 4:4 + T], ch(par_fw[KF - 1], e), ch(par_fb, e),
                                      ALU.mult, ALU.add).then_inc(ffn_step, 1)

            def ffn_unit_taps(u, b):
                reg = not isinstance(u, int)
                ch = lambda t, e: t[:, bass.ds(u * 2 + e, 1)] if reg else t[:, 2 * u + e:2 * u + e + 1]
                base = u * GATE_STEPS
                buf = gate_in[:, b, :, :]
                for back in range(1, KF):
                    for e in range(2):
                        dve.wait_ge(ffn_step, base + (2 * back + e))
                        dve.scalar_tensor_tensor(gate_out[:, e, :], buf[:, e, 4 - back:4 - back + T],
                                                 ch(par_fw[KF - 1 - back], e), gate_out[:, e, :],
                                                 ALU.mult, ALU.add).then_inc(ffn_step, 1)

            def ffn_unit_act(u, half, b):
                dve.tensor_tensor(up[:, :, :], pair(4 * half + 2 + b), rms[:, :, :], ALU.mult).then_inc(ffn_out, 1)
                dve.wait_ge(ffn_out, u + 2)
                dve.wait_ge(ffn_silu, u + 1)
                dve.tensor_tensor(gate_out[:, :, :], up[:, :, :], silu_g[:, :, :], ALU.mult).then_inc(ffn_act, 1)

            def ffn_unit_lo(u):
                dve.wait_ge(ffn_hi, u + 1)
                sl = slice(2 * u, 2 * u + 2) if isinstance(u, int) else bass.ds(u * 2, 2)
                dve.tensor_tensor(actLo[:, sl, :], gate_out[:, :, :], actHi[:, sl, :], ALU.subtract).then_inc(ffn_lo, 1)

            def ffn_steps(k, u0, half, group_end):
                for b in range(2):
                    u = u0 + b
                    if k == UNIT_AT[b]:
                        if b == 0:
                            dve.wait_ge(w_used, group_end)
                        ffn_unit_conv(u, half, b)
                    if k == UNIT_AT[b] + U_TAPS:
                        ffn_unit_taps(u, b)
                    if k == UNIT_AT[b] + U_ACT:
                        ffn_unit_act(u, half, b)
                    if k == UNIT_AT[b] + U_LO:
                        ffn_unit_lo(u)

            with dve.Fori(0, NG // 2) as i:
                for j in range(2):
                    for k in range(KD):
                        make_lo(dve, n_ffn + (1 + j) * KD + k, i * (2 * KD // RING))
                        ffn_steps(k, i * 4 + 2 * j, j, i * (2 * KD) + (n_ffn + (1 + j) * KD))
            for g in range(NDN):
                n0 = n_down + g * KDN
                peeled = 18 if g == 0 else 6
                for c in range(peeled):
                    make_lo(dve, n0 + c)
                    if g == 0:
                        ffn_steps(c, 2 * (NG - 1), 0, n_down)
                    elif c == LEAD:
                        dve.wait_ge(w_used, n0)
                        add_to_residual(2, g - 1, down_banks[g - 1])
                        for k in range(MT * (g - 1), MT * g):
                            make_h(2, k, par_ple)
                with dve.Fori(0, (KDN - peeled) // RING) as q:
                    for j in range(RING):
                        make_lo(dve, n0 + peeled + j, q)

            def ple_leave(i):
                gate_banks, _ = ple_banks(i)
                dve.wait_ge(w_used, n_ple + (KP + 1) * (i + 1))
                for b in range(2):
                    dve.tensor_tensor(pg_in[:, b, :, :], pair(gate_banks[b]), rms[:, :, :], ALU.mult).then_inc(ple_step, 1)

            def ple_add(i):
                _, proj_banks = ple_banks(i)
                for b in range(2):
                    dve.wait_ge(ple_sig, 2 * i + b + 1)
                    dve.tensor_tensor(pg_in[:, b, :, :], pair(proj_banks[b]), pg_sig[:, b, :, :], ALU.mult).then_inc(ple_step, 1)
                for b in range(2):
                    k = MT * i + 2 * b
                    dve.wait_ge(ple_step, 4 * i + 2 + b + 1)
                    dve.tensor_tensor(xT[:, k:k + 2, :], xT[:, k:k + 2, :], pg_in[:, b, :, :], ALU.add).then_inc(x_new, 1)

            for i in range(len(tail)):
                make_lo(dve, n_ple + i)
                if i == LEAD:
                    dve.wait_ge(w_used, n_ple)
                    add_to_residual(2, NDN - 1, down_banks[NDN - 1])
                    for k in range(MT * (NDN - 1), KD):
                        make_h(2, k, par_ple)
                if i == STATS2_AT + LEAD - 1:
                    stats(2)
                if i in ple_leave_at:
                    ple_leave(ple_leave_at[i])
                if i in ple_scale_at:
                    ple_add(ple_scale_at[i])
            ple_leave(NDN - 1)
            ple_add(NDN - 1)
            stats(3)
            dve.wait_ge(rms_made, 4)
            dve.wait_ge(out_copied, TT * NDN)
            for i in range(TT * NDN):
                t, j = i // NDN, i % NDN
                piece = out_tok[:, t, j * COLS:(j + 1) * COLS]
                dve.tensor_scalar(piece, piece, rms_col[:, t:t + 1], None, ALU.mult).then_inc(out_final, 1)


_INS = ["x", "p", "mix_norm_w", "w_in", "fox_forget_bias", "ssd_conv_w", "ssd_conv_b", "ssd_dt_bias", "ssd_A_log",
        "ssd_D", "ssd_norm_w", "w_out", "ffn_norm_w", "w_gate_up", "ffn_conv_w", "ffn_conv_b", "w_down",
        "ple_norm_w", "w_ple_gate", "w_ple_proj", "final_norm_w"]


def kernel(**inputs):
    import numpy as np
    import concourse.bacc as bacc
    from concourse.bass_utils import run_bass_kernel_spmd

    nc = bacc.Bacc("TRN2", target_bir_lowering=False, num_devices=1)
    arrays, args = {}, []
    for name in _INS:
        a = np.ascontiguousarray(inputs[name])
        arrays[f"in_{name}"] = a
        args.append(nc.dram_tensor(f"in_{name}", a.shape, mybir.dt.from_np(a.dtype), kind="ExternalInput").ap())
    out = nc.dram_tensor("out_x", arrays["in_x"].shape, F32, kind="ExternalOutput").ap()
    build(nc, *args, out)
    r = run_bass_kernel_spmd(nc, [arrays], core_ids=[0])
    return r.results[0]["out_x"]
```

```python
from contextlib import ExitStack

import concourse.bass as bass
from concourse import mybir

F32 = mybir.dt.float32
F32R = mybir.dt.float32r
BF16 = mybir.dt.bfloat16
ALU = mybir.AluOpType
ACT = mybir.ActivationFunctionType
AX_X = mybir.AxisListType.X

P = 128
EPS = 1e-6
MASKED = -1e30
RING = 4
CHUNK = 1024
COLS = 512
MT = COLS // P
CONV_STEPS = 9
GATE_STEPS = 7
SOFTPLUS_STEPS = 18
CUMULATE_STEPS = SOFTPLUS_STEPS + 2


def build(nc, x, p, mix_norm_w, w_in, fox_forget_bias, ssd_conv_w, ssd_conv_b, ssd_dt_bias, ssd_A_log,
          ssd_D, ssd_norm_w, w_out, ffn_norm_w, w_gate_up, ffn_conv_w, ffn_conv_b, w_down, ple_norm_w,
          w_ple_gate, w_ple_proj, final_norm_w, out):
    _, T, D = x.shape
    TT = T // P
    KD = D // P
    DP = p.shape[3]
    H = fox_forget_bias.shape[1]
    W = ssd_norm_w.shape[1]
    HD = W // H
    WT = W // P
    CW = ssd_conv_w.shape[2]
    GN = (CW - W) // 2
    G = GN // P
    CT = CW // P
    F = ffn_conv_w.shape[2]
    FT = F // P
    KC = ssd_conv_w.shape[1]
    KF = ffn_conv_w.shape[1]
    assert T == 256 and TT == 2 and DP == 2 * P and HD == 64 and KC == 4 and KF == 3 and G == 2

    c_q, c_k, c_v = 0, W, 2 * W
    c_f = 3 * W
    c_x = c_f + H
    c_b = c_x + W
    c_z = c_b + 2 * GN
    c_dt = c_z + W

    rows = lambda w: w[0].rearrange("(k p) n -> p k n", p=P)
    win_v, wout_v, wgu_v, wdn_v, wpg_v, wpp_v = map(rows, (w_in, w_out, w_gate_up, w_down, w_ple_gate, w_ple_proj))

    class Group:

        def __init__(self, name, view, col, operand, banks, chunks, by_token=False):
            self.name, self.view, self.col, self.operand = name, view, col, operand
            self.banks, self.chunks, self.by_token = banks, chunks, by_token

    SET_A, SET_B, SET_C, SET_D = (2, 3), (4, 5), (0, 1), (6, 7)
    KP = KD // 2
    in_cols = [("q0", c_q), ("bc", c_b), ("x0", c_x), ("x1", c_x + COLS), ("k0", c_k), ("q1", c_q + COLS),
               ("k1", c_k + COLS), ("v0", c_v), ("v1", c_v + COLS), ("z0", c_z), ("z1", c_z + COLS)]
    in_groups = [Group(n, win_v, c, "h", (SET_A, SET_B)[i % 2], KP, n[0] in "vz") for i, (n, c) in enumerate(in_cols)]
    out_groups = [Group(f"o{i}", wout_v, COLS * i, "mix", b, KP) for i, b in enumerate((SET_B, SET_A, SET_C, SET_D))]
    halves = [(0, 0, KP // 2), (1, 0, KP // 2), (0, KP // 2, KP), (1, KP // 2, KP), (2, 0, KP), (3, 0, KP)]
    front = [(g, c) for g in in_groups for c in range(KP)]
    front += [(out_groups[g], c) for g, a, b in halves for c in range(a, b)]
    NG = F // COLS
    n_ffn = len(front)
    n_down = n_ffn + NG * KD
    KDN = FT // 2
    NDN = D // COLS
    n_ple = n_down + NDN * KDN
    PROJ_AT = 6
    GATE_BANKS, PROJ_BANKS, XTOK_BANKS = (SET_B, SET_D), SET_C, SET_A
    tail = []
    for i in range(NDN):
        pg = Group(f"pg{i}", wpg_v, COLS * i, "h", GATE_BANKS[i % 2], KP, by_token=True)
        tail += [(pg, c) for c in range(KP)]
        tail.insert(-(KP - PROJ_AT), (Group(f"pp{i}", wpp_v, COLS * i, "p", PROJ_BANKS, 1, by_token=True), 0))
    n_last = n_ple + (NDN - 1) * (KP + 1)
    assert n_ffn % RING == 0 and n_down % RING == 0 and n_ple % RING == 0 and NG % 2 == 1 and KDN % RING == 2

    def last_of(steps, base):
        return {g.name: base + i for i, (g, c) in enumerate(steps)}

    done = last_of(front, 0) | last_of(tail, n_ple)

    ctx = ExitStack()
    with ctx:
        def sb(name, shape, dt=F32):
            return ctx.enter_context(nc.sbuf_tensor(name, shape, dt))

        def sem(name):
            return ctx.enter_context(nc.semaphore(name))

        xT = sb("xT", [P, KD, T])
        hHi, hLo = sb("hHi", [P, KD, T], F32R), sb("hLo", [P, KD, T], F32R)
        w_raw = sb("w_raw", [P, RING, CHUNK])
        w_hi, w_lo = sb("w_hi", [P, RING, CHUNK], F32R), sb("w_lo", [P, RING, CHUNK], F32R)
        ident = sb("ident", [P, P])
        ones = sb("ones", [P, P])
        par = sb("par", [P, 3, P])
        par_mix = sb("par_mix", [P, KD])
        pHi, pLo = sb("pHi", [P, 2, T], F32R), sb("pLo", [P, 2, T], F32R)
        rms = sb("rms", [P, 2, T])
        rms_col = sb("rms_col", [P, TT])
        root = sb("root", [P, T + TT])
        sumsq = sb("sumsq", [P, 2, T])
        sq = sb("sq", [P, 2, T])
        eps = sb("eps", [P, 1])
        arena = (nc.sbuf_base + 31) // 32 * 32

        top = [0]

        def at(name, shape, dt=F32, offset=None):
            size = 4 if dt != BF16 else 2
            for n in shape[1:]:
                size *= n
            offset = top[0] if offset is None else offset
            top[0] = max(top[0], (offset + size + 31) // 32 * 32)
            assert arena + top[0] <= nc.sbuf_usable_end, (name, arena + top[0], nc.sbuf_usable_end)
            return nc.alloc_sbuf_tensor_at(name, shape, dt, offset=arena + offset)

        K1 = 1024
        qT = at("qT", [P, WT, T], offset=0)
        kE = at("kE", [P, WT, T], offset=8 * K1)
        kO = at("kO", [P, WT, T], offset=16 * K1)
        v = at("v", [P, TT, W], offset=24 * K1)
        xdt = at("xdt", [P, TT, W], offset=32 * K1)
        z = at("z", [P, TT, W], offset=40 * K1)
        xs = at("xs", [P, TT, W], offset=48 * K1)
        y_fox = at("y_fox", [P, TT, W], offset=56 * K1)
        xsT = at("xsT", [P, WT, T], offset=64 * K1)
        bcT = at("bcT", [P, 2 * G, T], offset=72 * K1)
        cbT = at("cbT", [P, G, 3 * P])
        conv_in = at("conv_in", [P, 2, T + 4])
        conv_out = at("conv_out", [P, 2, 2, T])
        prob = at("prob", [P, 2, 3 * P])
        probT = at("probT", [P, 2, 3 * P])
        decay, mT = prob, probT
        w_fd = at("w_fd", [P, KD, 2 * H], offset=24 * K1)
        w_fd_parts = at("w_fd_parts", [P, KD, 4 * H], F32R, offset=26 * K1)
        ssd_row, fox_row = at("ssd_row", [4 * H, 3 * P], F32R), at("fox_row", [4 * H, 3 * P], F32R)
        sel = at("sel", [P, 2 * H], F32R)
        sel_f = at("sel_f", [P, 2 * H])
        ident_bf = at("ident_bf", [P, P], BF16)
        mask_q, mask_s = at("mask_q", [P, P], BF16), at("mask_s", [P, P], BF16)
        dt_tok = at("dt_tok", [P, TT, 2 * H])
        ncum_tok = at("ncum_tok", [P, TT, 2 * H])
        d_all = at("d_all", [P, H])
        neg_max = at("neg_max", [P, H, TT])
        row_sum = at("row_sum", [P, H, TT])
        row_inv = at("row_inv", [P, H, TT])
        ssq, y_root, y_rms = at("ssq", [P, 2, TT]), at("y_root", [P, TT]), at("y_rms", [P, TT])
        fdc = at("fdc", [2 * H, 4])
        xtok = at("xtok", [P, TT, D], offset=40 * K1)
        ptok = at("ptok", [P, TT, DP], offset=56 * K1)
        par_rows = at("par_rows", [P, 3, P], offset=58 * K1)
        mix_rows = at("mix_rows", [KD, P], offset=60 * K1)
        fdw = at("fdw", [2 * H, 8, T], offset=64 * K1)
        mixHi, mixLo = at("mixHi", [P, KD, T], F32R, 0), at("mixLo", [P, KD, T], F32R, 16 * K1)
        actHi, actLo = at("actHi", [P, FT, T], F32R, 0), at("actLo", [P, FT, T], F32R, 4 * FT * T)
        top[0] = 8 * FT * T
        gate_in = at("gate_in", [P, 2, 2, T + 4])
        gate_out = at("gate_out", [P, 2, T])
        silu_g = at("silu_g", [P, 2, T])
        up = at("up", [P, 2, T])
        out_tok = at("out_tok", [P, TT, D], offset=0)
        gate_x = at("gate_x", [P, TT, COLS], offset=16 * K1)
        pg_sig = at("pg_sig", [P, TT, COLS], offset=20 * K1)
        gain_fin = at("gain_fin", [P, D], offset=24 * K1)
        squares = at("squares", [P, COLS], offset=32 * K1)
        out_ssq = at("out_ssq", [P, TT, NDN], offset=34 * K1)
        last_hi, last_lo = (at(n, [P, KP - 1, CHUNK], F32R, offset=36 * K1 + 4 * CHUNK * (KP - 1) * i)
                            for i, n in enumerate(("last_hi", "last_lo")))
        out_sum, out_root, out_rms = (at(n, [P, TT], offset=34 * K1 + 128 * (i + 1))
                                      for i, n in enumerate(("out_sum", "out_root", "out_rms")))
        out_ssq_spare = at("out_ssq_spare", [P, 1], offset=34 * K1 + 512)
        ps = ctx.enter_context(nc.psum_tensor("ps", [P, 8, 512], F32))

        par_ffn, par_ple = (par[:, 0, i * KD:(i + 1) * KD] for i in range(2))
        o = 2 * KD
        par_ssdn, o = par[:, 0, o:o + WT], o + WT
        par_cb, o = par[:, 0, o:o + CT], o + CT
        par_fb = par[:, 0, o:o + FT]
        par_spans = (o + FT, KC * CT + FT, 2 * FT)
        assert max(par_spans) <= P
        par_cw = [par[:, 1, i * CT:(i + 1) * CT] for i in range(KC)]
        par_fw = [par[:, 1, KC * CT:KC * CT + FT], par[:, 2, 0:FT], par[:, 2, FT:2 * FT]]

        w_landed = [sem(f"w_landed{s}") for s in range(RING)]
        w_hi_made, w_lo_made, w_used = sem("w_hi_made"), sem("w_lo_made"), sem("w_used")
        gain_landed, gain_turned, gain_copied = sem("gain_landed"), sem("gain_turned"), sem("gain_copied")
        par_landed, p_landed = sem("par_landed"), sem("p_landed")
        tables_loaded = sem("tables_loaded")
        x_landed = [sem(f"x_landed{j}") for j in range(NDN)]
        fd_landed, small_landed, alog_landed = sem("fd_landed"), sem("small_landed"), sem("alog_landed")
        pool_step, consts_made, masks_made = sem("pool_step"), sem("consts_made"), sem("masks_made")
        par_turned, par_copied, p_turned, p_hi_made, p_lo_made = map(
            sem, ("par_turned", "par_copied", "p_turned", "p_hi_made", "p_lo_made"))
        x_turned, x_new = sem("x_turned"), sem("x_new")
        h_hi_made, h_lo_made = sem("h_hi_made"), sem("h_lo_made")
        squares_made, sums_made, root_made, rms_made = map(sem, ("squares_made", "sums_made", "root_made", "rms_made"))
        dve_evac, act_evac = sem("dve_evac"), sem("act_evac")
        conv_step, conv_made, silu_made = sem("conv_step"), sem("conv_made"), sem("silu_made")
        xs_turned, xs_copied, xdt_made = sem("xs_turned"), sem("xs_copied"), sem("xdt_made")
        cb_ready, cb_copied = sem("cb_ready"), sem("cb_copied")
        wfd_hi_made, wfd_lo_made, fd_ready, fd_step, fd_abs, fd_exp, a_exp, a_ready = map(
            sem, ("wfd_hi_made", "wfd_lo_made", "fd_ready", "fd_step", "fd_abs", "fd_exp", "a_exp", "a_ready"))
        cum_ready, dt_turned, dt_copied = sem("cum_ready"), sem("dt_turned"), sem("dt_copied")
        s_ready, max_made, prob_made, prob_turned, prob_copied, o_ready, inv_made, y_made = map(
            sem, ("s_ready", "max_made", "prob_made", "prob_turned", "prob_copied", "o_ready", "inv_made", "y_made"))
        e_ready, decay_made, m_made, yo_ready, ys_made = map(
            sem, ("e_ready", "decay_made", "m_made", "yo_ready", "ys_made"))
        gated, gated_sq, ssq_made, y_root_made, y_rms_made, y_normed = map(
            sem, ("gated", "gated_sq", "ssq_made", "y_root_made", "y_rms_made", "y_normed"))
        y_turned, mix_hi_made, mix_lo_made = sem("y_turned"), sem("mix_hi_made"), sem("mix_lo_made")
        ffn_done, ffn_step, ffn_conv, ffn_silu, ffn_act, ffn_hi, ffn_lo = map(
            sem, ("ffn_done", "ffn_step", "ffn_conv", "ffn_silu", "ffn_act", "ffn_hi", "ffn_lo"))
        down_done = sem("down_done")
        ffn_out, gain_fin_landed, stored = map(sem, ("ffn_out", "gain_fin_landed", "stored"))
        gate_first, ple_sig, ple_mul, xtok_turned, xtok_copied, out_added, out_squared, out_gained = map(
            sem, ("gate_first", "ple_sig", "ple_mul", "xtok_turned", "xtok_copied", "out_added", "out_squared", "out_gained"))
        out_sum_made, out_root_made, out_rms_made = map(sem, ("out_sum_made", "out_root_made", "out_rms_made"))
        out_final, out_final_act = sem("out_final"), sem("out_final_act")

        block = ctx.enter_context(nc.Block())

        def load_chunk(sp, n, src, q=0):
            if n >= RING:
                sp.wait_ge(w_lo_made, n + RING * q - RING + 1)
            sp.dma_start(w_raw[:, n % RING, :].rearrange("p (a c) -> p a c", a=2), src).then_inc(w_landed[n % RING], 16)

        def parts(n):
            if n_last <= n < n_last + KP - 1:
                return last_hi[:, n - n_last, :], last_lo[:, n - n_last, :]
            return w_hi[:, n % RING, :], w_lo[:, n % RING, :]

        def make_hi(act, n, q=0):
            act.wait_ge(w_landed[n % RING], 16 * (n // RING + q + 1))
            if RING <= n < n_last:
                act.wait_ge(w_used, n + RING * q - RING + 1)
            elif n >= n_last + KP - 1:
                act.wait_ge(w_used, n_last)
            act.activation(parts(n)[0], w_raw[:, n % RING, :], ACT.Copy).then_inc(w_hi_made, 1)

        def make_lo(dve, n, q=0):
            dve.wait_ge(w_hi_made, n + RING * q + 1)
            hi, lo = parts(n)
            dve.tensor_tensor(lo, w_raw[:, n % RING, :], hi, ALU.subtract).then_inc(w_lo_made, 1)

        def chunk_of(g, c):
            return g.view[:, 2 * c:2 * c + 2, g.col:g.col + COLS]

        def multiply(pe, n, opHi, opLo, tiles, bank_of, q=0):
            pe.wait_ge(w_lo_made, n + RING * q + 1)
            s = n % RING
            for i, (k, m, start, stop) in enumerate(tiles):
                dst = ps[:, bank_of[m // 2], (m % 2) * T:(m % 2) * T + T]
                hi, lo = w_hi[:, s, i * P:(i + 1) * P], w_lo[:, s, i * P:(i + 1) * P]
                pe.matmul(dst, hi, opHi(k), start=start and m % 2 == 0, stop=False, skip_group_check=True)
                pe.matmul(dst, hi, opLo(k), start=False, stop=False, skip_group_check=True)
                mm = pe.matmul(dst, lo, opHi(k), start=False, stop=stop, skip_group_check=True)
            return mm.then_inc(w_used, 1)

        def pair_tiles(first, last):
            return [(kk, m, first and kk == 0, last and kk == 1) for kk in range(2) for m in range(MT)]

        down_banks = (SET_B, SET_D, SET_C, SET_A)

        def multiply_group(pe, n, g, c, only=(0, 1)):
            opHi, opLo = {"h": (hHi, hLo), "mix": (mixHi, mixLo), "p": (pHi, pLo)}[g.operand]
            first, last = c == 0, c == g.chunks - 1
            if not g.by_token:
                return multiply(pe, n, lambda k: opHi[:, 2 * c + k, :], lambda k: opLo[:, 2 * c + k, :],
                                pair_tiles(first, last), g.banks)
            pe.wait_ge(w_lo_made, n + 1)
            order = [(kk, t) for t in range(TT) for kk in range(2)] if last else [(kk, t) for kk in range(2) for t in range(TT)]
            for i, (kk, t) in enumerate(order):
                if t not in only:
                    continue
                hi, lo = (w[:, kk * COLS:(kk + 1) * COLS] for w in parts(n))
                dst = ps[:, g.banks[t], :]
                a, b = (o_[:, 2 * c + kk, t * P:(t + 1) * P] for o_ in (opHi, opLo))
                pe.matmul(dst, a, hi, start=first and kk == 0, stop=False)
                pe.matmul(dst, a, lo, start=False, stop=False)
                mm = pe.matmul(dst, b, hi, start=False, stop=last and kk == 1)
                if g.name[:2] == "pg" and last and i == 1:
                    mm.then_inc(gate_first, 1)
            if n < n_last or (last and only == (1,)):
                mm.then_inc(w_used, 1)

        evacuated = {n: (dve_evac, i + 1) for i, n in enumerate(("q0", "k0", "q1", "k1"))}
        evacuated |= {n: (act_evac, i + 1) for i, n in enumerate(("v0", "v1", "z0", "z1"))}
        evacuated |= {n: (conv_step, CONV_STEPS * (2 * i + 1) + 1) for i, n in enumerate(("bc", "x0", "x1"))}
        NORM = KD // 2
        evacuated |= {f"o{i}": (x_new, NORM + 2 * i + 2) for i in range(NDN)}
        evacuated |= {f"dn{i}": (x_new, 2 * NORM + 2 * i + 2) for i in range(NDN)}

        bank_user = {}

        def wait_banks(pe, name, banks):
            waits = {}
            for b in banks:
                if b in bank_user:
                    s, val = bank_user[b]
                    waits[s.name] = (s, max(val, waits.get(s.name, (s, 0))[1]))
                bank_user[b] = evacuated[name]
            for s, val in waits.values():
                pe.wait_ge(s, val)

        LEAD = 3
        end = {g.name: done[g.name] for g in in_groups + out_groups}
        pe_after, act_after, dve_after = {}, {}, {}

        def after(table, n, what, *args):
            table.setdefault(n, []).append((what, args))

        def plan():
            def all_after(n, name, *args):
                after(pe_after, n, name, *args)
                after(act_after, n + LEAD, name, *args)
                after(dve_after, n + LEAD, name, *args)

            all_after(end["q0"], "stats0")
            for g in in_groups:
                if g.by_token:
                    after(act_after, end[g.name] + LEAD, "leave", g)
                elif g.name[0] in "qk":
                    after(dve_after, end[g.name] + LEAD, "leave", g)
            for i, g in enumerate(("bc", "x0", "x1")):
                for b in range(2):
                    n = end[g] + LEAD + 3 * b
                    after(dve_after, n, "conv_in_", g, b)
                    after(dve_after, n + 1, "conv_taps", 2 * i + b)
                    after(act_after, n + 2, "conv_silu", 2 * i + b)
            all_after(end["q0"] + 1, "turn_par")
            all_after(end["q0"] + 2, "fd")
            after(dve_after, end["q0"] + 4 + LEAD, "softplus")
            after(dve_after, end["q0"] + 6 + LEAD, "cumulate")
            after(dve_after, end["bc"] + 2 + LEAD, "make_row", 0)
            after(dve_after, end["bc"] + 5 + LEAD, "make_row", 1)
            all_after(end["bc"] + 4, "cums")
            all_after(end["bc"] + 10, "cb", 0)
            all_after(end["bc"] + 13, "cb", 1)
            all_after(end["x0"] + 7, "turn_xs", 0)
            all_after(end["x1"] + 7, "turn_xs", 1)
            b0 = end["x1"] + 8
            for i in range(H + 1):
                all_after(b0 + i * 6 // 5, "ssd", i)
            a0 = end["v0"]
            for i in range(H + 2):
                all_after(a0 + i, "fox", i)
            for b in range(WT // 2):
                all_after(a0 + H + 2 + b, "turn_fox", b)
            z0, z1 = end["z0"] + LEAD, end["z1"] + LEAD
            after(dve_after, z0 + 2, "gate_mul", 0)
            after(act_after, z0 + 3, "gate_square", 0)
            after(dve_after, z1 + 1, "gate_mul", 1)
            after(act_after, z1 + 1, "gate_square", 1)
            after(dve_after, z1 + 2, "gate_norm")
            after(act_after, z1 + 2, "gate_norm")
            for b in range(WT // 2):
                all_after(end["z1"] + 5 + b, "turn_gated", b)
            for g in ("o0", "o1", "o2"):
                i = int(g[1])
                after(act_after, end[g] + LEAD, "leave_out", i)
                after(dve_after, end[g] + LEAD, "leave_out", i)

        plan()

        STATS1_AT = 11
        UNIT_AT = (3, 9)
        U_CONV, U_TAPS, U_SILU, U_ACT, U_HI, U_LO = range(6)
        STATS2_AT = 7
        GROUP = KP + 1
        XTURN_AT, XCOPY_AT = 5, 5 + LEAD
        SIG_AT, MUL_AT, ADD_AT, SQUARE_AT, GAIN_AT = (GROUP - 1 + LEAD + j for j in range(5))

        def run(table, n, steps):
            for name, args in table.get(n, ()):
                if name in steps:
                    steps[name](*args)

        def flush(table, n, steps):
            for m in sorted(k for k in table if k >= n):
                run(table, m, steps)

        S_BANKS = (0, 1, 7)
        TURN_BANK, SPARE_BANK = 6, 7
        X_BANKS = (0, 1, 6, 7)
        XS_BANKS = (0, 1, 6, 7)
        groups = {g.name: g for g in in_groups + out_groups}
        s_bank = lambda h: S_BANKS[h % 3]

        @block.sync
        def _(sp):
            as_rows = lambda a: a.rearrange("(r p) -> r p", p=P)
            sp.dma_start(mix_rows[:, :], as_rows(mix_norm_w[0])).then_inc(gain_landed, 16)
            x_v = x[0].rearrange("(t p) n -> p t n", p=P)
            for j in range(NDN):
                cols = slice(j * COLS, (j + 1) * COLS)
                sp.dma_start(xtok[:, :, cols], x_v[:, :, cols]).then_inc(x_landed[j], 16)
                load_chunk(sp, j, chunk_of(*front[j]))
            with nc.allow_non_contiguous_dma(reason="the forget and dt columns of w_in are 16 wide"):
                sp.dma_start(w_fd[:, :, 0:H], win_v[:, :, c_f:c_f + H]).then_inc(fd_landed, 16)
                sp.dma_start(w_fd[:, :, H:2 * H], win_v[:, :, c_dt:c_dt + H]).then_inc(fd_landed, 16)
            load_chunk(sp, NDN, chunk_of(*front[NDN]))
            sp.dma_start(ptok[:, :, :], p[0, 0].rearrange("(t p) c -> p t c", p=P)).then_inc(p_landed, 16)
            column = lambda a: a[0].rearrange("(h a) -> h a", a=1)
            sp.dma_start(fdc[0:H, 0:1], column(fox_forget_bias)).then_inc(small_landed, 16)
            sp.dma_start(fdc[H:2 * H, 0:1], column(ssd_dt_bias)).then_inc(small_landed, 16)
            sp.wait_ge(consts_made, 1)
            sp.dma_start(fdc[H:2 * H, 2:3], column(ssd_A_log)).then_inc(alog_landed, 16)
            sp.dma_start(d_all[:, :], ssd_D[0:1, :].to_broadcast([P, H])).then_inc(small_landed, 16)
            load_chunk(sp, NDN + 1, chunk_of(*front[NDN + 1]))

            def param_rows(dst_tile, at_row, src, n):
                sp.dma_start(par_rows[at_row:at_row + n, dst_tile, :], as_rows(src)).then_inc(par_landed, 16)

            row = 0
            for src, n in ((ffn_norm_w[0], KD), (ple_norm_w[0], KD),
                           (ssd_norm_w[0], WT), (ssd_conv_b[0], CT), (ffn_conv_b[0], FT)):
                param_rows(0, row, src, n)
                row += n
            for i in range(KC):
                param_rows(1, i * CT, ssd_conv_w[0, i], CT)
            param_rows(1, KC * CT, ffn_conv_w[0, 0], FT)
            param_rows(2, 0, ffn_conv_w[0, 1], FT)
            param_rows(2, FT, ffn_conv_w[0, 2], FT)
            for n in range(NDN + 2, len(front)):
                load_chunk(sp, n, chunk_of(*front[n]))
            gu = wgu_v.rearrange("p k (a n) -> p k a n", a=2)
            for k in range(KD):
                load_chunk(sp, n_ffn + k, gu[:, k, :, 0:COLS])
            with sp.Fori(0, NG // 2) as i:
                for j in range(2):
                    for k in range(KD):
                        load_chunk(sp, n_ffn + (1 + j) * KD + k,
                                   gu[:, k, :, bass.ds(i * (2 * COLS) + (1 + j) * COLS, COLS)], i * (2 * KD // RING))
            for g in range(NDN):
                n0 = n_down + g * KDN
                cols = slice(g * COLS, (g + 1) * COLS)
                for c in range(2):
                    load_chunk(sp, n0 + c, wdn_v[:, 2 * c:2 * c + 2, cols])
                with sp.Fori(0, KDN // RING) as q:
                    for j in range(RING):
                        load_chunk(sp, n0 + 2 + j, wdn_v[:, bass.ds(q * (2 * RING) + 2 * (2 + j), 2), cols], q)
            for i, (g, c) in enumerate(tail):
                load_chunk(sp, n_ple + i, chunk_of(g, c))
                if i == RING:
                    sp.dma_start(gain_fin[:, :], final_norm_w.rearrange("(a n) -> a n", a=1).to_broadcast([P, D])).then_inc(gain_fin_landed, 16)
            out_v = out[0].rearrange("(t p) n -> p t n", p=P)
            for t in range(TT):
                for i in range(NDN // 2):
                    for finished, j in ((out_final, NDN // 2 + i), (out_final_act, i)):
                        sp.wait_ge(finished, t * (NDN // 2) + i + 1)
                        cols = slice(j * COLS, (j + 1) * COLS)
                        sp.dma_start(out_v[:, t, cols], out_tok[:, t, cols]).then_inc(stored, 16)
            sp.wait_ge(stored, 16 * TT * NDN)

        @block.gpsimd
        def _(pool):
            steps = [0]

            def link(ins):
                steps[0] += 1
                ins.then_inc(pool_step, 1)

            def linked():
                pool.wait_ge(pool_step, steps[0])

            def select(dst, src, keep, fill, base, per_partition, per_column, n):
                return pool.affine_select(out=dst, in_=src, compare_op=keep, fill=fill, base=base,
                                          pattern=[[per_column, n]], channel_multiplier=per_partition)

            pool.memset(fdc[:, 2:3], 0.0).then_inc(consts_made, 1)
            link(pool.memset(ident[:, :], 0.0))
            link(pool.memset(sel_f[:, :], 0.0))
            link(pool.memset(fdc[:, 1:2], -1.0))
            link(pool.memset(fdw[:, 0, :], 1.0))
            link(pool.memset(mask_q[:, :], 0.0))
            link(pool.memset(mask_s[:, :], 0.0))
            pool.memset(eps[:, :], EPS).then_inc(consts_made, 1)
            linked()
            select(ident[:, :], ident[:, :], ALU.not_equal, 1.0, 0, 1, -1, P).then_inc(consts_made, 1)
            pool.memset(ones[:, :], 1.0).then_inc(consts_made, 1)
            link(select(sel_f[:, :], sel_f[:, :], ALU.not_equal, 1.0, 0, 1, -1, 2 * H))
            linked()
            select(sel_f[:, :], sel_f[:, :], ALU.not_equal, 1.0, -2 * H, 1, -1, 2 * H).then_inc(masks_made, 1)
            select(fdc[:, 1:2], fdc[:, 1:2], ALU.is_ge, 1.0, H - 1, -1, 0, 1).then_inc(masks_made, 1)
            select(fdw[:, 0, P:P + 1], fdw[:, 0, P:P + 1], ALU.is_ge, 0.0, H - 1, -1, 0, 1).then_inc(masks_made, 1)
            select(mask_q[:, :], mask_q[:, :], ALU.is_ge, MASKED, 0, 1, -1, P).then_inc(masks_made, 1)
            select(mask_s[:, :], mask_s[:, :], ALU.is_ge, MASKED, 0, -1, 1, P).then_inc(masks_made, 1)
            pool.wait_ge(masks_made, 5)
            for i, half in enumerate((kE[P // 2:P, :, :], kO[0:P // 2, :, :], conv_in[:, :, 0:4])):
                pool.memset(half, 0.0).then_inc(masks_made, 1)
                pool.wait_ge(masks_made, 6 + i)
            for norm in range(3):
                if norm == 1:
                    pool.wait_ge(a_exp, 1)
                    select(fdc[:, 3:4], fdc[:, 3:4], ALU.is_ge, 1.0, -H, 1, 0, 1).then_inc(a_ready, 1)
                for b in range(KD // 2):
                    pool.wait_ge(x_new, norm * (KD // 2) + b + 1)
                    if b == 0 and norm > 0:
                        pool.wait_ge(sums_made, norm)
                    pair = xT[:, 2 * b:2 * b + 2, :]
                    if b == 0:
                        link(pool.tensor_tensor(sumsq[:, :, :], pair, pair, ALU.mult))
                        continue
                    linked()
                    link(pool.tensor_tensor(sq[:, :, :], pair, pair, ALU.mult))
                    linked()
                    ins = pool.tensor_tensor(sumsq[:, :, :], sumsq[:, :, :], sq[:, :, :], ALU.add)
                    if b == KD // 2 - 1:
                        ins.then_inc(squares_made, 1)
                    else:
                        link(ins)

        @block.tensor
        def _(pe):
            pe.wait_ge(consts_made, 4)
            pe.wait_ge(gain_landed, 16)
            pe.transpose(ps[:, 4, 0:KD], mix_rows[:, :], ident[0:KD, 0:KD]).then_inc(gain_turned, 1)

            def turn_x(b):
                if b % 2 == 0:
                    pe.wait_ge(x_landed[b // 2], 16)
                if b >= len(X_BANKS):
                    pe.wait_ge(x_new, b - len(X_BANKS) + 1)
                for kk in range(2):
                    for t in range(TT):
                        k = 2 * b + kk
                        mm = pe.transpose(ps[:, X_BANKS[b % len(X_BANKS)], kk * T + t * P:kk * T + t * P + P],
                                          xtok[:, t, k * P:(k + 1) * P], ident[:, :])
                mm.then_inc(x_turned, 1)

            for b in range(len(X_BANKS)):
                turn_x(b)

            def turn_par():
                pe.wait_ge(par_landed, 16 * 12)
                pe.wait_ge(x_new, NORM)
                for i, r in enumerate(par_spans):
                    mm = pe.transpose(ps[:, 1, i * P:i * P + r], par_rows[0:r, i, :], ident[0:r, 0:r])
                mm.then_inc(par_turned, 1)

            def turn_p():
                pe.wait_ge(p_landed, 16)
                pe.wait_ge(x_new, NORM - 1)
                for kk in range(2):
                    for t in range(TT):
                        mm = pe.transpose(ps[:, 0, kk * T + t * P:kk * T + t * P + P],
                                          ptok[:, t, kk * P:(kk + 1) * P], ident[:, :])
                mm.then_inc(p_turned, 1)

            def stats(norm, bank, columns=True, rows_=True):
                pe.wait_ge(squares_made, norm + 1)
                if rows_:
                    for j in range(2):
                        mm = pe.matmul(ps[:, bank, 0:T], ones[:, :], sumsq[:, j, :], start=j == 0, stop=j == 1,
                                       skip_group_check=True)
                if columns:
                    for t in range(TT):
                        for j in range(2):
                            mm = pe.matmul(ps[:, bank, T + t:T + t + 1], sumsq[:, j, t * P:(t + 1) * P], ones[:, 0:1],
                                           start=j == 0, stop=j == 1, skip_group_check=True)
                mm.then_inc(sums_made, 1)

            def stats0():
                turn_p()
                pe.wait_ge(x_new, KD // 2)
                stats(0, SPARE_BANK)

            def fd():
                pe.wait_ge(wfd_lo_made, 1)
                for k in range(KD):
                    pe.matmul(ps[0:4 * H, TURN_BANK, 0:T], w_fd_parts[:, k, :], hHi[:, k, :],
                              start=k == 0, stop=False, skip_group_check=True)
                    mm = pe.matmul(ps[0:2 * H, TURN_BANK, 0:T], w_fd_parts[:, k, 0:2 * H], hLo[:, k, :],
                                   start=False, stop=k == KD - 1, skip_group_check=True)
                mm.then_inc(fd_ready, 1)

            def cums():
                pe.wait_ge(fd_step, CUMULATE_STEPS)
                pe.wait_ge(root_made, 1)
                for i, row in enumerate((6, 1)):
                    for t in range(TT):
                        mm = pe.transpose(ps[:, SPARE_BANK, (i * TT + t) * 2 * H:(i * TT + t + 1) * 2 * H],
                                          fdw[:, row, t * P:(t + 1) * P], ident[0:2 * H, 0:2 * H])
                mm.then_inc(dt_turned, 1)

            def cb(g):
                if g == 0:
                    pe.wait_ge(silu_made, 2)
                    pe.wait_ge(dt_copied, 2)
                else:
                    pe.wait_ge(cb_copied, g)
                for s, l0, width, dst in ((0, 0, T, 0), (1, P, P, T)):
                    mm = pe.matmul(ps[:, SPARE_BANK, dst:dst + width], bcT[:, g, s * P:(s + 1) * P],
                                   bcT[:, G + g, l0:l0 + width], start=True, stop=True, skip_group_check=True)
                mm.then_inc(cb_ready, 1)

            def exponent_terms(bank, j, row, mask, start):
                both = 4 * H
                pe.matmul(ps[:, bank, 0:3 * P], sel[0:both, j:j + 1].to_broadcast([both, P]), row[:, :],
                          start=start, stop=False, skip_group_check=True)
                for dst in (0, T):
                    mm = pe.matmul(ps[:, bank, dst:dst + P], ident_bf[:, :], mask[:, :],
                                   start=False, stop=True, skip_group_check=True)
                return mm

            def fox(i):
                if 1 <= i <= H:
                    h = i - 1
                    pe.wait_ge(prob_made, 2 * h + 2)
                    if h >= 1:
                        pe.wait_ge(prob_copied, h)
                    for b in range(3):
                        mm = pe.transpose(ps[:, TURN_BANK, b * P:(b + 1) * P], prob[:, h % 2, b * P:(b + 1) * P], ident[:, :])
                    mm.then_inc(prob_turned, 1)
                if i >= 2:
                    h = i - 2
                    pe.wait_ge(prob_copied, h + 1)
                    if h % (H // 2) == 0:
                        pe.wait_ge(*evacuated[f"v{h // (H // 2)}"])
                    pT = lambda b: probT[:, h % 2, b * P:(b + 1) * P]
                    val = lambda t: v[:, t, h * HD:(h + 1) * HD]
                    o0, o1 = (ps[:, s_bank(h), 3 * P + t * HD:3 * P + (t + 1) * HD] for t in range(2))
                    pe.matmul(o0, pT(0), val(0), start=True, stop=True, skip_group_check=True)
                    pe.matmul(o1, pT(1), val(0), start=False, stop=False, skip_group_check=True)
                    pe.matmul(o1, pT(2), val(1), start=False, stop=True, skip_group_check=True).then_inc(o_ready, 1)
                if i < H:
                    h = i
                    bank = s_bank(h)
                    if h == 0:
                        pe.wait_ge(*evacuated["k1"])
                        pe.wait_ge(ys_made, H)
                    if h >= 3:
                        pe.wait_ge(y_made, h - 2)
                    keys = (kE, kO)[h % 2]
                    pe.matmul(ps[:, bank, 0:P], qT[:, h // 2, 0:P], keys[:, h // 2, 0:P],
                              start=True, stop=False, skip_group_check=True)
                    pe.matmul(ps[:, bank, P:3 * P], qT[:, h // 2, P:T], keys[:, h // 2, :],
                              start=False, stop=False, skip_group_check=True)
                    exponent_terms(bank, h, fox_row, mask_q, start=False).then_inc(s_ready, 1)

            def ssd(i):
                if i >= 1:
                    h = i - 1
                    pe.wait_ge(m_made, h + 1)
                    m = lambda b: mT[:, h % 2, b * P:(b + 1) * P]
                    val = lambda t: xdt[:, t, h * HD:(h + 1) * HD]
                    o0, o1 = (ps[:, s_bank(h), 3 * P + t * HD:3 * P + (t + 1) * HD] for t in range(2))
                    pe.matmul(o0, m(0), val(0), start=True, stop=True, skip_group_check=True)
                    pe.matmul(o1, m(1), val(0), start=False, stop=False, skip_group_check=True)
                    pe.matmul(o1, m(2), val(1), start=False, stop=True, skip_group_check=True).then_inc(yo_ready, 1)
                if i < H:
                    h = i
                    if h == 0:
                        pe.wait_ge(cum_ready, 2)
                        pe.wait_ge(xdt_made, 2 * TT)
                    if h >= 3:
                        pe.wait_ge(ys_made, h - 2)
                    exponent_terms(s_bank(h), H + h, ssd_row, mask_s, start=True).then_inc(e_ready, 1)

            def turn_xs(half):
                pe.wait_ge(silu_made, 4 + 2 * half)
                if half == 0:
                    pe.wait_ge(par_copied, 1)
                    pe.wait_ge(p_lo_made, 1)
                else:
                    pe.wait_ge(fd_step, CUMULATE_STEPS)
                    pe.wait_ge(cb_copied, G)
                for t in range(TT):
                    for j in range(WT // 2):
                        mm = pe.transpose(ps[:, XS_BANKS[TT * half + t], j * P:(j + 1) * P],
                                          xsT[:, WT // 2 * half + j, t * P:(t + 1) * P], ident[:, :])
                    mm.then_inc(xs_turned, 1)

            def turn_y(src, n):
                if n >= 2:
                    pe.wait_ge(mix_lo_made, n - 1)
                for kk in range(2):
                    for t in range(TT):
                        k = 2 * (n % (WT // 2)) + kk
                        mm = pe.transpose(ps[:, 6 + n % 2, kk * T + t * P:kk * T + t * P + P],
                                          src[:, t, k * P:(k + 1) * P], ident[:, :])
                mm.then_inc(y_turned, 1)

            def turn_fox(b):
                pe.wait_ge(y_made, H)
                turn_y(y_fox, b)

            def turn_gated(b):
                pe.wait_ge(y_normed, TT)
                turn_y(z, WT // 2 + b)

            steps = dict(turn_par=turn_par, stats0=stats0, fd=fd, cums=cums, cb=cb, fox=fox, ssd=ssd, turn_xs=turn_xs,
                         turn_fox=turn_fox, turn_gated=turn_gated)
            for n, (g, c) in enumerate(front):
                if c == 0:
                    wait_banks(pe, g.name, g.banks)
                    if g.name == "o2":
                        pe.wait_ge(y_made, H)
                    if g.name == "o3":
                        pe.wait_ge(mix_lo_made, WT)
                if g.name == "q0":
                    pe.wait_ge(h_lo_made, 2 * c + 2)
                if g.name == "bc" and c == 0:
                    pe.wait_ge(gain_copied, 1)
                if g.name == "o0":
                    pe.wait_ge(mix_lo_made, c + 1)
                multiply_group(pe, n, g, c)
                if n + len(X_BANKS) < NORM:
                    turn_x(n + len(X_BANKS))
                run(pe_after, n, steps)
            flush(pe_after, len(front), steps)

            def ffn_chunk(n, k, half, q=0):
                return multiply(pe, n, lambda _: hHi[:, k, :], lambda _: hLo[:, k, :],
                                [(k, m, k == 0, k == KD - 1) for m in range(2 * MT)],
                                [4 * half + b for b in range(4)], q)

            for k in range(KD):
                if k == 0:
                    for name in ("o1", "o2"):
                        pe.wait_ge(*evacuated[name])
                pe.wait_ge(h_lo_made, KD + k + 1)
                ffn_chunk(n_ffn + k, k, 0)
                if k == KD // 2:
                    pe.wait_ge(*evacuated["o0"])
                if k == STATS1_AT:
                    stats(1, 4, columns=False)
            pe.wait_ge(root_made, 2)
            with pe.Fori(0, NG // 2) as i:
                for j in range(2):
                    for k in range(KD):
                        if k == 0:
                            pe.wait_ge(ffn_out, i * 4 + (1, 3)[j])
                        ffn_chunk(n_ffn + (1 + j) * KD + k, k, 1 - j, i * (2 * KD // RING))

            for g in range(NDN):
                n0 = n_down + g * KDN

                def chunk(j, q, first=False, last=False):
                    at_ = (lambda t, k: t[:, 2 * j + k, :]) if isinstance(q, int) else \
                        (lambda t, k: t[:, bass.ds(q * (2 * RING) + (2 * j + k), 1), :])
                    return multiply(pe, n0 + j, lambda k: at_(actHi, k), lambda k: at_(actLo, k),
                                    pair_tiles(first, last), down_banks[g], q)

                pe.wait_ge(ffn_lo, 2 * (NG - 1) if g == 0 else 2 * NG)
                for j in range(2):
                    chunk(j, 0, first=j == 0)
                with pe.Fori(0, KDN // RING - 1) as q:
                    for j in range(2, 2 + RING):
                        chunk(j, q)
                if g == 0:
                    pe.wait_ge(ffn_lo, 2 * NG)
                for j in range(KDN - RING, KDN):
                    chunk(j, 0, last=j == KDN - 1)

            def turn_residual(i):
                pe.wait_ge(x_new, 3 * NORM - 2 * (NDN - 1 - i) if i < NDN - 1 else 3 * NORM)
                if i == 0:
                    pe.wait_ge(*evacuated["dn3"])
                else:
                    pe.wait_ge(xtok_copied, TT * i)
                for t in range(TT):
                    for m in range(MT):
                        mm = pe.transpose(ps[:, XTOK_BANKS[t], m * P:(m + 1) * P],
                                          xT[:, MT * i + m, t * P:(t + 1) * P], ident[:, :])
                    mm.then_inc(xtok_turned, 1)

            for n, (g, c) in enumerate(tail):
                i = n // GROUP
                if g.name[:2] == "pg" and c == 0:
                    if i < 2:
                        pe.wait_ge(*evacuated[f"dn{i}"])
                        if i == 1:
                            pe.wait_ge(root_made, 3)
                    else:
                        pe.wait_ge(ple_sig, TT * (i - 1))
                if g.name[:2] == "pp":
                    if i == 0:
                        pe.wait_ge(*evacuated["dn2"])
                    else:
                        pe.wait_ge(ple_mul, TT * i)
                if g.name == "pg0":
                    pe.wait_ge(h_lo_made, 2 * KD + 2 * c + 2)
                multiply_group(pe, n_ple + n, g, c, (0, 1) if i < NDN - 1 or g.name[:2] == "pp" else (0,))
                if n == STATS2_AT:
                    stats(2, GATE_BANKS[1][0], rows_=False)
                if n % GROUP == XTURN_AT:
                    turn_residual(i)
            for n, (g, c) in enumerate(tail):
                if n >= len(tail) - GROUP and g.name[:2] == "pg":
                    multiply_group(pe, n_ple + n, g, c, (1,))

        @block.scalar
        def _(act):
            def copy(dst, src, scale=1.0):
                return act.activation(dst, src, ACT.Copy, scale=scale)

            def make_h(norm, k, gain):
                act.wait_ge(x_new, norm * NORM + k // 2 + 1)
                copy(hHi[:, k, :], xT[:, k, :], gain[:, k:k + 1]).then_inc(h_hi_made, 1)

            def stats(norm, bank, a=0, b=T):
                act.wait_ge(sums_made, norm + 1)
                act.wait_ge(tables_loaded, 1)
                act.activation(root[:, a:b], ps[:, bank, a:b], ACT.Sqrt, bias=eps[:, :], scale=1.0 / D).then_inc(root_made, 1)

            def conv_silu(u):
                act.wait_ge(conv_step, CONV_STEPS * (u + 1))
                dst = bcT[:, 2 * u:2 * u + 2, :] if u < 2 else xsT[:, 2 * (u - 2):2 * (u - 2) + 2, :]
                act.activation(dst, conv_out[:, u % 2, :, :], ACT.Silu).then_inc(silu_made, 1)

            def leave(g):
                act.wait_ge(w_used, done[g.name] + 1)
                half = int(g.name[1])
                for t in range(TT):
                    dst = (v if g.name[0] == "v" else z)[:, t, half * COLS:(half + 1) * COLS]
                    ins = act.activation(dst, ps[:, g.banks[t], :], ACT.Copy if g.name[0] == "v" else ACT.Silu,
                                         scale=rms_col[:, t:t + 1])
                ins.then_inc(act_evac, 1)

            def p_hi():
                act.wait_ge(p_turned, 1)
                copy(pHi[:, :, :], ps[:, 0, :]).then_inc(p_hi_made, 1)

            def stats0():
                p_hi()
                stats(0, SPARE_BANK, 0, T + TT)

            def fd():
                act.wait_ge(fd_step, 4)
                act.activation(fdw[:, 2, :], fdw[:, 1, :], ACT.Abs).then_inc(fd_abs, 1)
                act.wait_ge(fd_abs, 1)
                act.activation(fdw[:, 3, :], fdw[:, 2, :], ACT.Exp, scale=-1.0).then_inc(fd_exp, 1)
                act.wait_ge(alog_landed, 16)
                act.activation(fdc[:, 3:4], fdc[:, 2:3], ACT.Exp).then_inc(a_exp, 1)

            def fox(i):
                if i >= 1 and i <= H:
                    h = i - 1
                    act.wait_ge(prob_turned, h + 1)
                    if h >= 2:
                        act.wait_ge(o_ready, h - 1)
                    copy(probT[:, h % 2, :], ps[:, TURN_BANK, 0:3 * P]).then_inc(prob_copied, 1)
                if i < H:
                    h = i
                    act.wait_ge(max_made, 2 * h + 2)
                    if h >= 2:
                        act.wait_ge(prob_turned, h - 1)
                    for t, (a, b) in enumerate(((0, P), (P, 3 * P))):
                        act.activation(prob[:, h % 2, a:b], ps[:, s_bank(h), a:b], ACT.Exp,
                                       bias=neg_max[:, h, t:t + 1], accum_out=row_sum[:, h, t:t + 1]).then_inc(prob_made, 1)

            def ssd(i):
                if i < H:
                    h = i
                    act.wait_ge(e_ready, h + 1)
                    if h >= 2:
                        act.wait_ge(m_made, h - 1)
                    if h == 0:
                        act.wait_ge(dt_copied, 2)
                    for t, (a, b) in enumerate(((0, T), (T, 3 * P))):
                        act.activation(decay[:, h % 2, a:b], ps[:, s_bank(h), a:b], ACT.Exp,
                                       bias=ncum_tok[:, t, H + h:H + h + 1]).then_inc(decay_made, 1)

            def turn_fox(b):
                act.wait_ge(y_turned, b + 1)
                copy(mixHi[:, 2 * b:2 * b + 2, :], ps[:, 6 + b % 2, :]).then_inc(mix_hi_made, 1)

            def gate_square(half):
                act.wait_ge(gated, half + 1)
                cols = slice(half * COLS, (half + 1) * COLS)
                for t in range(TT):
                    act.activation(xdt[:, t, cols], z[:, t, cols], ACT.Square,
                                   accum_out=ssq[:, half, t:t + 1]).then_inc(gated_sq, 1)

            def gate_norm():
                act.wait_ge(ssq_made, 1)
                act.activation(y_root[:, :], ssq[:, 0, :], ACT.Sqrt, bias=eps[:, :], scale=1.0 / W).then_inc(y_root_made, 1)

            def turn_gated(b):
                act.wait_ge(y_turned, WT // 2 + b + 1)
                for kk in range(2):
                    k = 2 * b + kk
                    copy(mixHi[:, WT + k, :], ps[:, 6 + b % 2, kk * T:(kk + 1) * T],
                         par_ssdn[:, k:k + 1]).then_inc(mix_hi_made, 1)

            def leave_out(i):
                for k in range(MT * i, MT * (i + 1)):
                    make_h(1, k, par_ffn)

            steps = dict(leave=leave, stats0=stats0, fd=fd, fox=fox, ssd=ssd, turn_fox=turn_fox, conv_silu=conv_silu,
                         gate_square=gate_square, gate_norm=gate_norm, turn_gated=turn_gated, leave_out=leave_out)
            act.wait_ge(consts_made, 4)
            copy(root[:, 0:1], eps[:, :]).then_inc(tables_loaded, 1)
            act.wait_ge(gain_copied, 1)
            for n in range(len(front)):
                if n < NORM:
                    for k in (2 * n, 2 * n + 1):
                        make_h(0, k, par_mix)
                make_hi(act, n)
                if n == NORM - 1:
                    act.wait_ge(fd_landed, 32)
                    copy(w_fd_parts[:, :, 0:2 * H], w_fd[:, :, :]).then_inc(wfd_hi_made, 1)
                run(act_after, n, steps)
            for k in range(KD):
                make_hi(act, n_ffn + k)
                run(act_after, n_ffn + k, steps)
                if k == LEAD:
                    leave_out(NDN - 1)
                if k == STATS1_AT + LEAD:
                    stats(1, 4)

            def ffn_unit_silu(u):
                act.wait_ge(ffn_step, u * GATE_STEPS + GATE_STEPS)
                act.activation(silu_g[:, :, :], gate_out[:, :, :], ACT.Silu).then_inc(ffn_silu, 1)

            def ffn_unit_hi(u):
                act.wait_ge(ffn_act, u + 1)
                dst = actHi[:, 2 * u:2 * u + 2, :] if isinstance(u, int) else actHi[:, bass.ds(u * 2, 2), :]
                copy(dst, gate_out[:, :, :]).then_inc(ffn_hi, 1)

            with act.Fori(0, NG // 2) as i:
                for j in range(2):
                    for k in range(KD):
                        make_hi(act, n_ffn + (1 + j) * KD + k, i * (2 * KD // RING))
                        for b in range(2):
                            if k == UNIT_AT[b] + U_SILU:
                                ffn_unit_silu(i * 4 + (2 * j + b))
                            if k == UNIT_AT[b] + U_HI:
                                ffn_unit_hi(i * 4 + (2 * j + b))
            for g in range(NDN):
                n0 = n_down + g * KDN
                peeled = 18 if g == 0 else 6
                for c in range(peeled):
                    make_hi(act, n0 + c)
                    if g == 0:
                        for b in range(2):
                            if c == UNIT_AT[b] + U_SILU:
                                ffn_unit_silu(2 * (NG - 1) + b)
                            if c == UNIT_AT[b] + U_HI:
                                ffn_unit_hi(2 * (NG - 1) + b)
                    elif c == LEAD:
                        for k in range(MT * (g - 1), MT * g):
                            make_h(2, k, par_ple)
                with act.Fori(0, (KDN - peeled) // RING) as q:
                    for j in range(RING):
                        make_hi(act, n0 + peeled + j, q)

            def ple_sigmoid(i, only=(0, 1)):
                for t in only:
                    if t == 0:
                        act.wait_ge(gate_first, i + 1)
                        act.wait_ge(rms_made, 3)
                    else:
                        act.wait_ge(w_used, n_ple + GROUP * (i + 1) if i < NDN - 1 else n_last + 1)
                    if i > 0:
                        act.wait_ge(ple_mul, TT * (i - 1) + t + 1)
                    act.activation(pg_sig[:, t, :], ps[:, GATE_BANKS[i % 2][t], :], ACT.Sigmoid,
                                   scale=rms_col[:, t:t + 1]).then_inc(ple_sig, 1)

            def copy_residual(i):
                for t in range(TT):
                    act.wait_ge(xtok_turned, TT * i + t + 1)
                    copy(out_tok[:, t, i * COLS:(i + 1) * COLS], ps[:, XTOK_BANKS[t], :]).then_inc(xtok_copied, 1)

            def square(i, t):
                act.wait_ge(out_added, TT * i + t + 1)
                if i + t > 0:
                    act.wait_ge(out_squared, TT * i + t)
                act.activation(squares[:, :], out_tok[:, t, i * COLS:(i + 1) * COLS], ACT.Square,
                               accum_out=out_ssq[:, t, i:i + 1]).then_inc(out_squared, 1)

            for n in range(len(tail)):
                make_hi(act, n_ple + n)
                if n == LEAD:
                    for k in range(MT * (NDN - 1), KD):
                        make_h(2, k, par_ple)
                if n == STATS2_AT + LEAD - 1:
                    stats(2, GATE_BANKS[1][0], T, T + TT)
                if n % GROUP == XCOPY_AT:
                    copy_residual(n // GROUP)
                for i in range(NDN - 1):
                    if n == i * GROUP + SIG_AT:
                        ple_sigmoid(i)
                    if n == i * GROUP + SQUARE_AT:
                        for t in range(TT):
                            square(i, t)
            for t in range(TT):
                ple_sigmoid(NDN - 1, (t,))
                act.activation(out_root[:, t:t + 1], eps[:, :], ACT.Sqrt).then_inc(tables_loaded, 1)
                square(NDN - 1, t)
                act.wait_ge(out_sum_made, t + 1)
                act.wait_ge(tables_loaded, 2 + 2 * t)
                act.activation(out_root[:, t:t + 1], out_sum[:, t:t + 1], ACT.Sqrt, bias=eps[:, :], scale=1.0 / D).then_inc(out_root_made, 1)
                act.wait_ge(out_gained, TT * (NDN - 1))
                act.wait_ge(out_rms_made, t + 1)
                for i in range(NDN // 2):
                    piece = out_tok[:, t, i * COLS:(i + 1) * COLS]
                    copy(piece, piece, out_rms[:, t:t + 1]).then_inc(out_final_act, 1)
                if t == 0:
                    act.activation(out_ssq_spare[:, :], eps[:, :], ACT.Sigmoid).then_inc(tables_loaded, 1)

        @block.vector
        def _(dve):
            def make_h(norm, k, gain):
                dve.wait_ge(h_hi_made, norm * KD + k + 1)
                dve.scalar_tensor_tensor(hLo[:, k, :], xT[:, k, :], gain[:, k:k + 1], hHi[:, k, :],
                                         ALU.mult, ALU.subtract).then_inc(h_lo_made, 1)

            def add_to_residual(norm, i, banks):
                for b in range(2):
                    k = MT * i + 2 * b
                    dve.tensor_tensor(xT[:, k:k + 2, :], ps[:, banks[b], :].rearrange("p (a t) -> p a t", a=2),
                                      xT[:, k:k + 2, :], ALU.add).then_inc(x_new, 1)

            def stats(norm):
                dve.wait_ge(root_made, norm + 1)
                if norm == 0:
                    dve.reciprocal(rms_col[:, :], root[:, T:T + TT])
                if norm == 3:
                    dve.reciprocal(rms_col[:, :], root[:, T:T + TT]).then_inc(rms_made, 1)
                    return
                for j in range(2):
                    ins = dve.reciprocal(rms[:, j, :], root[:, 0:T])
                ins.then_inc(rms_made, 1)
                dve.wait_ge(rms_made, norm + 1)

            pair = lambda bank: ps[:, bank, :].rearrange("p (a t) -> p a t", a=2)

            def conv_channel(u):
                return WT + 2 * u if u < 2 else 2 * (u - 2)

            def conv_tap(u, back):
                for e in range(2):
                    dst, src = conv_out[:, u % 2, e, :], conv_in[:, e, 4 - back:4 - back + T]
                    ch = conv_channel(u) + e
                    weight = par_cw[KC - 1 - back][:, ch:ch + 1]
                    if back == 0:
                        ins = dve.tensor_scalar(dst, src, weight, par_cb[:, ch:ch + 1], ALU.mult, ALU.add)
                    else:
                        dve.wait_ge(conv_step, CONV_STEPS * u + 2 * back + e)
                        ins = dve.scalar_tensor_tensor(dst, src, weight, dst, ALU.mult, ALU.add)
                    ins.then_inc(conv_step, 1)

            def conv_in_(name, b):
                u = 2 * ("bc", "x0", "x1").index(name) + b
                dve.wait_ge(w_used, done[name] + 1)
                if u == 0:
                    dve.wait_ge(par_copied, 1)
                    dve.wait_ge(masks_made, 8)
                else:
                    dve.wait_ge(conv_step, CONV_STEPS * u)
                bank = groups[name].banks[b]
                dve.tensor_tensor(conv_in[:, :, 4:4 + T], pair(bank), rms[:, :, :], ALU.mult).then_inc(conv_step, 1)
                if u >= 2:
                    dve.wait_ge(silu_made, u - 1)
                dve.wait_ge(conv_step, CONV_STEPS * u + 1)
                for back in range(0, 2):
                    conv_tap(u, back)

            def conv_taps(u):
                for back in range(2, KC):
                    conv_tap(u, back)

            def leave(g):
                dve.wait_ge(w_used, done[g.name] + 1)
                for b in range(2):
                    bank = g.banks[b]
                    k = MT * int(g.name[1]) + 2 * b
                    if g.name[0] == "q":
                        ins = dve.scalar_tensor_tensor(qT[:, k:k + 2, :], pair(bank), HD ** -0.5, rms[:, :, :],
                                                       ALU.mult, ALU.mult)
                    else:
                        for keys, a in ((kE, 0), (kO, P // 2)):
                            r = slice(a, a + P // 2)
                            ins = dve.tensor_tensor(keys[r, k:k + 2, :], ps[r, bank, :].rearrange("p (a t) -> p a t", a=2),
                                                    rms[r, :, :], ALU.mult)
                    if b == 1:
                        ins.then_inc(dve_evac, 1)

            def stats0():
                dve.wait_ge(p_hi_made, 1)
                dve.tensor_tensor(pLo[:, :, :], pair(0), pHi[:, :, :], ALU.subtract).then_inc(p_lo_made, 1)
                stats(0)

            fd_count = [0]
            fdr = lambda i: fdw[:, i, :]

            def link(ins):
                fd_count[0] += 1
                ins.then_inc(fd_step, 1)
                dve.wait_ge(fd_step, fd_count[0])

            def fd():
                dve.wait_ge(fd_ready, 1)
                link(dve.tensor_copy(fdr(1), ps[2 * H:4 * H, TURN_BANK, 0:T]))
                link(dve.tensor_tensor(fdr(1), ps[0:2 * H, TURN_BANK, 0:T], fdr(1), ALU.add))
                link(dve.tensor_tensor(fdr(1), fdr(1), rms[0:2 * H, 0, :], ALU.mult))
                dve.wait_ge(small_landed, 48)
                dve.wait_ge(masks_made, 8)
                link(dve.tensor_scalar(fdr(1), fdr(1), fdc[:, 0:1], fdc[:, 1:2], ALU.add, ALU.mult))

            def softplus():
                dve.wait_ge(fd_exp, 1)
                link(dve.tensor_scalar(fdr(4), fdr(3), 2.0, None, ALU.add))
                link(dve.reciprocal(fdr(4), fdr(4)))
                link(dve.tensor_tensor(fdr(4), fdr(3), fdr(4), ALU.mult))
                link(dve.tensor_tensor(fdr(5), fdr(4), fdr(4), ALU.mult))
                link(dve.tensor_scalar(fdr(6), fdr(5), 1.0 / 15, None, ALU.mult))
                for n in (13, 11, 9):
                    link(dve.scalar_tensor_tensor(fdr(6), fdr(6), 1.0 / n, fdr(5), ALU.add, ALU.mult))

            def cumulate():
                for n in (7, 5, 3):
                    link(dve.scalar_tensor_tensor(fdr(6), fdr(6), 1.0 / n, fdr(5), ALU.add, ALU.mult))
                link(dve.scalar_tensor_tensor(fdr(6), fdr(6), 1.0, fdr(4), ALU.add, ALU.mult))
                link(dve.tensor_scalar(fdr(5), fdr(1), 0.0, None, ALU.max))
                link(dve.scalar_tensor_tensor(fdr(6), fdr(6), 2.0, fdr(5), ALU.mult, ALU.add))
                assert fd_count[0] == SOFTPLUS_STEPS
                dve.wait_ge(a_ready, 1)
                link(dve.tensor_scalar(fdr(7), fdr(6), fdc[:, 3:4], -1.0, ALU.mult, ALU.mult))
                link(dve.tensor_tensor_scan(fdr(1), fdr(0), fdr(7), 0.0, ALU.mult, ALU.add))
                assert fd_count[0] == CUMULATE_STEPS

            def make_row(attention):
                n, c = 2 * H, fdr(1)
                src = fdw[:, 2 + 2 * attention:4 + 2 * attention, :].rearrange("h a t -> h (a t)")[:, 0:3 * P]
                if attention:
                    dst = fox_row
                    link(dve.tensor_scalar(src[:, 0:P], c[:, 0:P], -1.0, None, ALU.mult))
                    link(dve.tensor_scalar(src[:, P:3 * P], c, -1.0, None, ALU.mult))
                    dve.tensor_copy(ident_bf[:, :], ident[:, :])
                else:
                    dst = ssd_row
                    link(dve.tensor_copy(src[:, 0:P], c[:, 0:P]))
                    link(dve.tensor_scalar(src[:, P:T], c[:, P:T], c[:, P - 1:P], None, ALU.add))
                    link(dve.tensor_copy(src[:, T:3 * P], c[:, P:T]))
                    dve.tensor_copy(sel[:, :], sel_f[:, :])
                link(dve.tensor_copy(dst[0:n, :], src))
                dve.tensor_tensor(dst[n:2 * n, :], src, dst[0:n, :], ALU.subtract).then_inc(cum_ready, 1)

            def cums():
                dve.wait_ge(dt_turned, 1)
                tok = lambda i: ps[:, SPARE_BANK, i * TT * 2 * H:(i + 1) * TT * 2 * H].rearrange("p (t h) -> p t h", t=TT)
                dve.tensor_copy(dt_tok[:, :, :], tok(0)).then_inc(dt_copied, 1)
                dve.tensor_scalar(ncum_tok[:, :, :], tok(1), -1.0, None, ALU.mult).then_inc(dt_copied, 1)

            def cb(g):
                dve.wait_ge(cb_ready, g + 1)
                dve.tensor_copy(cbT[:, g, :], ps[:, SPARE_BANK, 0:3 * P]).then_inc(cb_copied, 1)

            def fox(i):
                if i >= 2:
                    h = i - 2
                    dve.wait_ge(prob_made, 2 * h + 2)
                    dve.reciprocal(row_inv[:, h, :], row_sum[:, h, :]).then_inc(inv_made, 1)
                    dve.wait_ge(inv_made, h + 1)
                    dve.wait_ge(o_ready, h + 1)
                    o_ = ps[:, s_bank(h), 3 * P:3 * P + TT * HD].rearrange("p (t d) -> p t d", t=TT)
                    dve.tensor_tensor(y_fox[:, :, h * HD:(h + 1) * HD], o_,
                                      row_inv[:, h, :].unsqueeze(2).to_broadcast([P, TT, HD]), ALU.mult).then_inc(y_made, 1)
                if i < H:
                    h = i
                    dve.wait_ge(s_ready, h + 1)
                    for t, (a, b) in enumerate(((0, P), (P, 3 * P))):
                        dve.reduce_max(neg_max[:, h, t:t + 1], ps[:, s_bank(h), a:b], AX_X, negate=True).then_inc(max_made, 1)

            def ssd(i):
                if i >= 1:
                    h = i - 1
                    dve.wait_ge(yo_ready, h + 1)
                    o_ = ps[:, s_bank(h), 3 * P:3 * P + TT * HD].rearrange("p (t d) -> p t d", t=TT)
                    cols = xs[:, :, h * HD:(h + 1) * HD]
                    dve.scalar_tensor_tensor(cols, cols, d_all[:, h:h + 1], o_, ALU.mult, ALU.add).then_inc(ys_made, 1)
                if i < H:
                    h = i
                    dve.wait_ge(decay_made, 2 * h + 2)
                    if h >= 2:
                        dve.wait_ge(yo_ready, h - 1)
                    dve.tensor_tensor(mT[:, h % 2, :], decay[:, h % 2, :], cbT[:, h * G // H, :], ALU.mult).then_inc(m_made, 1)

            def turn_xs(half):
                for t in range(TT):
                    i = TT * half + t
                    dve.wait_ge(xs_turned, i + 1)
                    cols = xs[:, t, half * COLS:(half + 1) * COLS]
                    dve.tensor_copy(cols, ps[:, XS_BANKS[i], :]).then_inc(xs_copied, 1)
                    if i == 0:
                        dve.wait_ge(dt_copied, 1)
                    dve.wait_ge(xs_copied, i + 1)
                    h0 = H + half * (H // 2)
                    dve.tensor_tensor(xdt[:, t, half * COLS:(half + 1) * COLS].rearrange("p (h d) -> p h d", d=HD),
                                      cols.rearrange("p (h d) -> p h d", d=HD),
                                      dt_tok[:, t, h0:h0 + H // 2].unsqueeze(2).to_broadcast([P, H // 2, HD]),
                                      ALU.mult).then_inc(xdt_made, 1)

            def turn_fox(b):
                dve.wait_ge(mix_hi_made, b + 1)
                dve.tensor_tensor(mixLo[:, 2 * b:2 * b + 2, :], pair(6 + b % 2), mixHi[:, 2 * b:2 * b + 2, :],
                                  ALU.subtract).then_inc(mix_lo_made, 1)

            def gate_mul(half):
                dve.wait_ge(ys_made, H)
                dve.wait_ge(*evacuated[f"z{half}"])
                cols = slice(half * COLS, (half + 1) * COLS)
                dve.tensor_tensor(z[:, :, cols], z[:, :, cols], xs[:, :, cols], ALU.mult).then_inc(gated, 1)

            def gate_norm():
                dve.wait_ge(gated_sq, 2 * TT)
                dve.tensor_tensor(ssq[:, 0, :], ssq[:, 0, :], ssq[:, 1, :], ALU.add).then_inc(ssq_made, 1)
                dve.wait_ge(y_root_made, 1)
                dve.reciprocal(y_rms[:, :], y_root[:, :]).then_inc(y_rms_made, 1)
                dve.wait_ge(y_rms_made, 1)
                for t in range(TT):
                    dve.tensor_scalar(z[:, t, :], z[:, t, :], y_rms[:, t:t + 1], None, ALU.mult).then_inc(y_normed, 1)

            def turn_gated(b):
                dve.wait_ge(mix_hi_made, WT // 2 + 2 * b + 2)
                for kk in range(2):
                    k = 2 * b + kk
                    ins = dve.scalar_tensor_tensor(mixLo[:, WT + k, :], ps[:, 6 + b % 2, kk * T:(kk + 1) * T],
                                                   par_ssdn[:, k:k + 1], mixHi[:, WT + k, :], ALU.mult, ALU.subtract)
                ins.then_inc(mix_lo_made, 1)

            def leave_out(i):
                dve.wait_ge(w_used, done[f"o{i}"] + 1)
                add_to_residual(1, i, out_groups[i].banks)
                for k in range(MT * i, MT * (i + 1)):
                    make_h(1, k, par_ffn)

            def turn_par():
                dve.wait_ge(par_turned, 1)
                for i, r in enumerate(par_spans):
                    ins = dve.tensor_copy(par[:, i, 0:r], ps[:, 1, i * P:i * P + r])
                ins.then_inc(par_copied, 1)

            def copy_x(b):
                dve.wait_ge(x_turned, b + 1)
                dve.tensor_copy(xT[:, 2 * b:2 * b + 2, :], pair(X_BANKS[b % len(X_BANKS)])).then_inc(x_new, 1)

            steps = dict(leave=leave, turn_par=turn_par, stats0=stats0, fd=fd, softplus=softplus, cumulate=cumulate, make_row=make_row,
                         cums=cums, cb=cb, conv_in_=conv_in_, conv_taps=conv_taps, fox=fox, ssd=ssd, turn_xs=turn_xs,
                         turn_fox=turn_fox, gate_mul=gate_mul, gate_norm=gate_norm, turn_gated=turn_gated,
                         leave_out=leave_out)
            dve.wait_ge(gain_turned, 1)
            dve.tensor_copy(par_mix[:, :], ps[:, 4, 0:KD]).then_inc(gain_copied, 1)
            dve.wait_ge(gain_copied, 1)
            copy_x(0)
            copy_x(1)
            for n in range(len(front)):
                if n < NORM:
                    for k in (2 * n, 2 * n + 1):
                        make_h(0, k, par_mix)
                make_lo(dve, n)
                if n + 2 < NORM:
                    copy_x(n + 2)
                if n == NORM:
                    dve.wait_ge(wfd_hi_made, 1)
                    dve.tensor_tensor(w_fd_parts[:, :, 2 * H:4 * H], w_fd[:, :, :], w_fd_parts[:, :, 0:2 * H],
                                      ALU.subtract).then_inc(wfd_lo_made, 1)
                run(dve_after, n, steps)
            for k in range(KD):
                make_lo(dve, n_ffn + k)
                run(dve_after, n_ffn + k, steps)
                if k == LEAD:
                    leave_out(NDN - 1)
                    dve.memset(gate_in[:, :, :, 0:4], 0.0).then_inc(ffn_out, 1)
                if k == STATS1_AT + LEAD:
                    stats(1)

            def ffn_unit_conv(u, half, b):
                reg = not isinstance(u, int)
                ch = lambda t, e: t[:, bass.ds(u * 2 + e, 1)] if reg else t[:, 2 * u + e:2 * u + e + 1]
                base = u * GATE_STEPS
                buf = gate_in[:, b, :, :]
                dve.tensor_tensor(buf[:, :, 4:4 + T], pair(4 * half + b), rms[:, :, :], ALU.mult).then_inc(ffn_step, 1)
                dve.wait_ge(ffn_step, base + 1)
                for e in range(2):
                    dve.tensor_scalar(gate_out[:, e, :], buf[:, e, 4:4 + T], ch(par_fw[KF - 1], e), ch(par_fb, e),
                                      ALU.mult, ALU.add).then_inc(ffn_step, 1)

            def ffn_unit_taps(u, b):
                reg = not isinstance(u, int)
                ch = lambda t, e: t[:, bass.ds(u * 2 + e, 1)] if reg else t[:, 2 * u + e:2 * u + e + 1]
                base = u * GATE_STEPS
                buf = gate_in[:, b, :, :]
                for back in range(1, KF):
                    for e in range(2):
                        dve.wait_ge(ffn_step, base + (2 * back + e))
                        dve.scalar_tensor_tensor(gate_out[:, e, :], buf[:, e, 4 - back:4 - back + T],
                                                 ch(par_fw[KF - 1 - back], e), gate_out[:, e, :],
                                                 ALU.mult, ALU.add).then_inc(ffn_step, 1)

            def ffn_unit_act(u, half, b):
                dve.tensor_tensor(up[:, :, :], pair(4 * half + 2 + b), rms[:, :, :], ALU.mult).then_inc(ffn_out, 1)
                dve.wait_ge(ffn_out, u + 2)
                dve.wait_ge(ffn_silu, u + 1)
                dve.tensor_tensor(gate_out[:, :, :], up[:, :, :], silu_g[:, :, :], ALU.mult).then_inc(ffn_act, 1)

            def ffn_unit_lo(u):
                dve.wait_ge(ffn_hi, u + 1)
                sl = slice(2 * u, 2 * u + 2) if isinstance(u, int) else bass.ds(u * 2, 2)
                dve.tensor_tensor(actLo[:, sl, :], gate_out[:, :, :], actHi[:, sl, :], ALU.subtract).then_inc(ffn_lo, 1)

            def ffn_steps(k, u0, half, group_end):
                for b in range(2):
                    u = u0 + b
                    if k == UNIT_AT[b]:
                        if b == 0:
                            dve.wait_ge(w_used, group_end)
                        ffn_unit_conv(u, half, b)
                    if k == UNIT_AT[b] + U_TAPS:
                        ffn_unit_taps(u, b)
                    if k == UNIT_AT[b] + U_ACT:
                        ffn_unit_act(u, half, b)
                    if k == UNIT_AT[b] + U_LO:
                        ffn_unit_lo(u)

            with dve.Fori(0, NG // 2) as i:
                for j in range(2):
                    for k in range(KD):
                        make_lo(dve, n_ffn + (1 + j) * KD + k, i * (2 * KD // RING))
                        ffn_steps(k, i * 4 + 2 * j, j, i * (2 * KD) + (n_ffn + (1 + j) * KD))
            for g in range(NDN):
                n0 = n_down + g * KDN
                peeled = 18 if g == 0 else 6
                for c in range(peeled):
                    make_lo(dve, n0 + c)
                    if g == 0:
                        ffn_steps(c, 2 * (NG - 1), 0, n_down)
                    elif c == LEAD:
                        dve.wait_ge(w_used, n0)
                        add_to_residual(2, g - 1, down_banks[g - 1])
                        for k in range(MT * (g - 1), MT * g):
                            make_h(2, k, par_ple)
                with dve.Fori(0, (KDN - peeled) // RING) as q:
                    for j in range(RING):
                        make_lo(dve, n0 + peeled + j, q)

            def ple_mul_(i, t):
                dve.wait_ge(ple_sig, TT * i + t + 1)
                if i > 0:
                    dve.wait_ge(out_added, TT * (i - 1) + t + 1)
                dve.tensor_tensor(gate_x[:, t, :], ps[:, PROJ_BANKS[t], :], pg_sig[:, t, :], ALU.mult).then_inc(ple_mul, 1)

            def ple_add(i, t):
                dve.wait_ge(ple_mul, TT * i + t + 1)
                dve.wait_ge(xtok_copied, TT * i + t + 1)
                cols = out_tok[:, t, i * COLS:(i + 1) * COLS]
                dve.tensor_tensor(cols, cols, gate_x[:, t, :], ALU.add).then_inc(out_added, 1)

            def ple_gain(i, t):
                dve.wait_ge(out_squared, TT * i + t + 1)
                if i + t == 0:
                    dve.wait_ge(gain_fin_landed, 16)
                cols = out_tok[:, t, i * COLS:(i + 1) * COLS]
                dve.tensor_tensor(cols, cols, gain_fin[:, i * COLS:(i + 1) * COLS], ALU.mult).then_inc(out_gained, 1)

            for n in range(len(tail)):
                make_lo(dve, n_ple + n)
                if n == LEAD:
                    dve.wait_ge(w_used, n_ple)
                    add_to_residual(2, NDN - 1, down_banks[NDN - 1])
                    for k in range(MT * (NDN - 1), KD):
                        make_h(2, k, par_ple)
                if n == STATS2_AT + LEAD - 1:
                    dve.wait_ge(root_made, 3)
                    dve.reciprocal(rms_col[:, :], root[:, T:T + TT]).then_inc(rms_made, 1)
                for i in range(NDN - 1):
                    for place, step in ((MUL_AT, ple_mul_), (ADD_AT, ple_add), (GAIN_AT, ple_gain)):
                        if n == i * GROUP + place:
                            for t in range(TT):
                                step(i, t)
            for t in range(TT):
                ple_mul_(NDN - 1, t)
                ple_add(NDN - 1, t)
                dve.wait_ge(out_gained, TT * (NDN - 1))
                dve.wait_ge(out_squared, TT * (NDN - 1) + t + 1)
                dve.reduce_sum(out_sum[:, t:t + 1], out_ssq[:, t, :], AX_X).then_inc(out_sum_made, 1)
                dve.wait_ge(out_root_made, t + 1)
                dve.reciprocal(out_rms[:, t:t + 1], out_root[:, t:t + 1]).then_inc(out_rms_made, 1)
                dve.wait_ge(out_rms_made, t + 1)
                for i in range(NDN // 2, NDN):
                    piece = out_tok[:, t, i * COLS:(i + 1) * COLS]
                    if i < NDN - 1:
                        ins = dve.tensor_scalar(piece, piece, out_rms[:, t:t + 1], None, ALU.mult)
                    else:
                        ins = dve.scalar_tensor_tensor(piece, piece, out_rms[:, t:t + 1], gain_fin[:, i * COLS:D],
                                                       ALU.mult, ALU.mult)
                    ins.then_inc(out_final, 1)


_INS = ["x", "p", "mix_norm_w", "w_in", "fox_forget_bias", "ssd_conv_w", "ssd_conv_b", "ssd_dt_bias", "ssd_A_log",
        "ssd_D", "ssd_norm_w", "w_out", "ffn_norm_w", "w_gate_up", "ffn_conv_w", "ffn_conv_b", "w_down",
        "ple_norm_w", "w_ple_gate", "w_ple_proj", "final_norm_w"]


def kernel(**inputs):
    import numpy as np
    import concourse.bacc as bacc
    from concourse.bass_utils import run_bass_kernel_spmd

    nc = bacc.Bacc("TRN2", target_bir_lowering=False, num_devices=1)
    arrays, args = {}, []
    for name in _INS:
        a = np.ascontiguousarray(inputs[name])
        arrays[f"in_{name}"] = a
        args.append(nc.dram_tensor(f"in_{name}", a.shape, mybir.dt.from_np(a.dtype), kind="ExternalInput").ap())
    out = nc.dram_tensor("out_x", arrays["in_x"].shape, F32, kind="ExternalOutput").ap()
    build(nc, *args, out)
    r = run_bass_kernel_spmd(nc, [arrays], core_ids=[0])
    return r.results[0]["out_x"]
```

```python
from contextlib import ExitStack

import concourse.bass as bass
from concourse import mybir

F32 = mybir.dt.float32
F32R = mybir.dt.float32r
BF16 = mybir.dt.bfloat16
ALU = mybir.AluOpType
ACT = mybir.ActivationFunctionType
AX_X = mybir.AxisListType.X

P = 128
EPS = 1e-6
MASKED = -1e30
RING = 4
CHUNK = 1024
COLS = 512
MT = COLS // P
CONV_STEPS = 9
GATE_STEPS = 7
SOFTPLUS_STEPS = 18
CUMULATE_STEPS = SOFTPLUS_STEPS + 2


def build(nc, x, p, mix_norm_w, w_in, fox_forget_bias, ssd_conv_w, ssd_conv_b, ssd_dt_bias, ssd_A_log,
          ssd_D, ssd_norm_w, w_out, ffn_norm_w, w_gate_up, ffn_conv_w, ffn_conv_b, w_down, ple_norm_w,
          w_ple_gate, w_ple_proj, final_norm_w, out):
    _, T, D = x.shape
    TT = T // P
    KD = D // P
    DP = p.shape[3]
    H = fox_forget_bias.shape[1]
    W = ssd_norm_w.shape[1]
    HD = W // H
    WT = W // P
    CW = ssd_conv_w.shape[2]
    GN = (CW - W) // 2
    G = GN // P
    CT = CW // P
    F = ffn_conv_w.shape[2]
    FT = F // P
    KC = ssd_conv_w.shape[1]
    KF = ffn_conv_w.shape[1]
    assert T == 256 and TT == 2 and DP == 2 * P and HD == 64 and KC == 4 and KF == 3 and G == 2

    c_q, c_k, c_v = 0, W, 2 * W
    c_f = 3 * W
    c_x = c_f + H
    c_b = c_x + W
    c_z = c_b + 2 * GN
    c_dt = c_z + W

    rows = lambda w: w[0].rearrange("(k p) n -> p k n", p=P)
    win_v, wout_v, wgu_v, wdn_v, wpg_v, wpp_v = map(rows, (w_in, w_out, w_gate_up, w_down, w_ple_gate, w_ple_proj))

    class Group:

        def __init__(self, name, view, col, operand, banks, chunks, by_token=False):
            self.name, self.view, self.col, self.operand = name, view, col, operand
            self.banks, self.chunks, self.by_token = banks, chunks, by_token

    SET_A, SET_B, SET_C, SET_D = (2, 3), (4, 5), (0, 1), (6, 7)
    KP = KD // 2
    in_cols = [("q0", c_q), ("bc", c_b), ("x0", c_x), ("x1", c_x + COLS), ("k0", c_k), ("q1", c_q + COLS),
               ("k1", c_k + COLS), ("v0", c_v), ("v1", c_v + COLS), ("z0", c_z), ("z1", c_z + COLS)]
    in_groups = [Group(n, win_v, c, "h", (SET_A, SET_B)[i % 2], KP, n[0] == "v") for i, (n, c) in enumerate(in_cols)]
    out_groups = [Group(f"o{i}", wout_v, COLS * i, "mix", b, KP) for i, b in enumerate((SET_B, SET_A, SET_C, SET_D))]
    halves = [(g, 0, KP // 2) for g in range(3)] + [(g, KP // 2, KP) for g in range(3)] + [(3, 0, KP)]
    front = [(g, c) for g in in_groups for c in range(KP)]
    front += [(out_groups[g], c) for g, a, b in halves for c in range(a, b)]
    NG = F // COLS
    n_ffn = len(front)
    n_down = n_ffn + NG * KD
    KDN = FT // 2
    NDN = D // COLS
    n_ple = n_down + NDN * KDN
    PROJ_AT = 6
    GATE_BANKS, PROJ_BANKS, XTOK_BANKS = (SET_B, SET_D), SET_C, SET_A
    tail = []
    for i in range(NDN):
        pg = Group(f"pg{i}", wpg_v, COLS * i, "h", GATE_BANKS[i % 2], KP, by_token=True)
        tail += [(pg, c) for c in range(KP)]
        tail.insert(-(KP - PROJ_AT), (Group(f"pp{i}", wpp_v, COLS * i, "p", PROJ_BANKS, 1, by_token=True), 0))
    n_last = n_ple + (NDN - 1) * (KP + 1)
    assert n_ffn % RING == 0 and n_down % RING == 0 and n_ple % RING == 0 and NG % 2 == 1 and KDN % RING == 2

    X_PIECES = [(0, 1), (1, 2)] + [(a, a + 2) for a in range(2, KD // 2, 2)]

    def last_of(steps, base):
        return {g.name: base + i for i, (g, c) in enumerate(steps)}

    done = last_of(front, 0) | last_of(tail, n_ple)

    ctx = ExitStack()
    with ctx:
        def sb(name, shape, dt=F32):
            return ctx.enter_context(nc.sbuf_tensor(name, shape, dt))

        def sem(name):
            return ctx.enter_context(nc.semaphore(name))

        xT = sb("xT", [P, KD, T])
        hHi, hLo = sb("hHi", [P, KD, T], F32R), sb("hLo", [P, KD, T], F32R)
        w_raw = sb("w_raw", [P, RING, CHUNK])
        w_hi, w_lo = sb("w_hi", [P, RING, CHUNK], F32R), sb("w_lo", [P, RING, CHUNK], F32R)
        ident = sb("ident", [P, P])
        ones = sb("ones", [P, P])
        par = sb("par", [P, 3, P])
        par_mix = sb("par_mix", [P, KD])
        pHi, pLo = sb("pHi", [P, 2, T], F32R), sb("pLo", [P, 2, T], F32R)
        rms = sb("rms", [P, 2, T])
        rms_col = sb("rms_col", [P, TT])
        root = sb("root", [P, T + TT])
        sumsq = sb("sumsq", [P, 2, T])
        sq = sb("sq", [P, 2, T])
        eps = sb("eps", [P, 1])
        arena = (nc.sbuf_base + 31) // 32 * 32

        top = [0]

        def at(name, shape, dt=F32, offset=None):
            size = 4 if dt != BF16 else 2
            for n in shape[1:]:
                size *= n
            offset = top[0] if offset is None else offset
            top[0] = max(top[0], (offset + size + 31) // 32 * 32)
            assert arena + top[0] <= nc.sbuf_usable_end, (name, arena + top[0], nc.sbuf_usable_end)
            return nc.alloc_sbuf_tensor_at(name, shape, dt, offset=arena + offset)

        K1 = 1024
        qT = at("qT", [P, WT, T], offset=0)
        kE = at("kE", [P, WT, T], offset=8 * K1)
        kO = at("kO", [P, WT, T], offset=16 * K1)
        probT_hi, probT_lo = (at(f"probT_{n}", [P, 2, 3 * P], F32R, offset=(24 + 3 * i) * K1) for i, n in enumerate(("hi", "lo")))
        y_part = at("y_part", [HD, 2, T], offset=30 * K1)
        v_parts = at("v_parts", [P, TT, H, 2 * HD], F32R, offset=40 * K1)
        xdt = at("xdt", [P, TT, W], offset=32 * K1)
        xdt_parts = at("xdt_parts", [P, TT, H, 2 * HD], F32R, offset=40 * K1)
        zT = at("zT", [P, WT, T], offset=32 * K1)
        y_foxT = at("y_foxT", [P, WT, T], offset=56 * K1)
        xsT = at("xsT", [P, WT, T], offset=64 * K1)
        bcT = at("bcT", [P, 2 * G, T], offset=72 * K1)
        cbT = at("cbT", [P, G, 3 * P], offset=76 * K1)
        conv_in = at("conv_in", [P, 2, T + 4])
        conv_out = at("conv_out", [P, 2, 2, T])
        prob = at("prob", [P, 2, 3 * P])
        mT = at("mT", [P, 2, 3 * P])
        decay, mT_hi, mT_lo = prob, probT_hi, probT_lo
        w_fd = at("w_fd", [P, KD, 2 * H], offset=24 * K1)
        w_fd_parts = at("w_fd_parts", [P, KD, 4 * H], F32R, offset=26 * K1)
        ssd_row, fox_row = at("ssd_row", [4 * H, 3 * P], F32R), at("fox_row", [4 * H, 3 * P], F32R)
        sel = at("sel", [P, 2 * H], F32R)
        sel_f = at("sel_f", [P, 2 * H])
        ident_bf = at("ident_bf", [P, P], BF16)
        mask_q, mask_s = at("mask_q", [P, P], BF16), at("mask_s", [P, P], BF16)
        dt_tok = at("dt_tok", [P, TT, 2 * H])
        ncum_tok = at("ncum_tok", [P, TT, 2 * H])
        d_all = at("d_all", [P, H])
        neg_max = at("neg_max", [P, H, TT])
        row_sum = at("row_sum", [P, H, TT])
        row_inv = at("row_inv", [P, H, TT])
        y_sum = at("y_sum", [P, T])
        y_rms = at("y_rms", [P, T])
        fdc = at("fdc", [2 * H, 4])
        xtok = at("xtok", [P, TT, D], offset=40 * K1)
        ptok = at("ptok", [P, TT, DP], offset=56 * K1)
        par_rows = at("par_rows", [P, 3, P], offset=58 * K1)
        mix_rows = at("mix_rows", [KD, P], offset=60 * K1)
        fdw = at("fdw", [2 * H, 8, T], offset=64 * K1)
        idle_in = at("idle_in", [P, COLS], BF16, offset=72 * K1)
        mixHi, mixLo = at("mixHi", [P, KD, T], F32R, 0), at("mixLo", [P, KD, T], F32R, 16 * K1)
        actHi, actLo = at("actHi", [P, FT, T], F32R, 0), at("actLo", [P, FT, T], F32R, 4 * FT * T)
        top[0] = 8 * FT * T
        gate_in = at("gate_in", [P, 2, 2, T + 4])
        gate_out = at("gate_out", [P, 2, T])
        silu_g = at("silu_g", [P, 2, T])
        up = at("up", [P, 2, T])
        out_tok = at("out_tok", [P, TT, D], offset=0)
        gate_x = at("gate_x", [P, TT, COLS], offset=16 * K1)
        pg_sig = at("pg_sig", [P, TT, COLS], offset=20 * K1)
        gain_fin = at("gain_fin", [P, D], offset=24 * K1)
        squares = at("squares", [P, COLS], offset=32 * K1)
        out_ssq = at("out_ssq", [P, TT, NDN], offset=34 * K1)
        last_hi, last_lo = (at(n, [P, KP - 1, CHUNK], F32R, offset=36 * K1 + 4 * CHUNK * (KP - 1) * i)
                            for i, n in enumerate(("last_hi", "last_lo")))
        out_sum, out_root, out_rms = (at(n, [P, TT], offset=34 * K1 + 128 * (i + 1))
                                      for i, n in enumerate(("out_sum", "out_root", "out_rms")))
        unread = at("unread", [P, 1], offset=34 * K1 + 512)
        ps = ctx.enter_context(nc.psum_tensor("ps", [P, 8, 512], F32))

        par_ffn, par_ple = (par[:, 0, i * KD:(i + 1) * KD] for i in range(2))
        o = 2 * KD
        par_ssdn, o = par[:, 0, o:o + WT], o + WT
        par_cb, o = par[:, 0, o:o + CT], o + CT
        par_fb = par[:, 0, o:o + FT]
        par_spans = (o + FT, KC * CT + FT, 2 * FT)
        assert max(par_spans) <= P
        par_cw = [par[:, 1, i * CT:(i + 1) * CT] for i in range(KC)]
        par_fw = [par[:, 1, KC * CT:KC * CT + FT], par[:, 2, 0:FT], par[:, 2, FT:2 * FT]]

        w_landed = [sem(f"w_landed{s}") for s in range(RING)]
        w_hi_made, w_lo_made, w_used = sem("w_hi_made"), sem("w_lo_made"), sem("w_used")
        gain_landed, gain_turned, gain_copied = sem("gain_landed"), sem("gain_turned"), sem("gain_copied")
        par_landed, p_landed = sem("par_landed"), sem("p_landed")
        tables_loaded, idle_in_made = sem("tables_loaded"), sem("idle_in_made")
        x_landed = [sem(f"x_landed{j}") for j in range(len(X_PIECES))]
        fd_landed, small_landed, alog_landed = sem("fd_landed"), sem("small_landed"), sem("alog_landed")
        pool_step, consts_made, masks_made = sem("pool_step"), sem("consts_made"), sem("masks_made")
        par_turned, par_copied, p_turned, p_hi_made, p_lo_made = map(
            sem, ("par_turned", "par_copied", "p_turned", "p_hi_made", "p_lo_made"))
        x_turned, x_new = sem("x_turned"), sem("x_new")
        h_hi_made, h_lo_made = sem("h_hi_made"), sem("h_lo_made")
        squares_made, sums_made, root_made, rms_made = map(sem, ("squares_made", "sums_made", "root_made", "rms_made"))
        dve_evac = sem("dve_evac")
        conv_step, silu_made = sem("conv_step"), sem("silu_made")
        xs_turned, xdt_made, xdt_hi_made, xdt_lo_made = map(sem, ("xs_turned", "xdt_made", "xdt_hi_made", "xdt_lo_made"))
        cb_ready, cb_copied = sem("cb_ready"), sem("cb_copied")
        wfd_hi_made, wfd_lo_made, fd_ready, fd_step, fd_abs, fd_exp, a_exp, a_ready = map(
            sem, ("wfd_hi_made", "wfd_lo_made", "fd_ready", "fd_step", "fd_abs", "fd_exp", "a_exp", "a_ready"))
        cum_ready, dt_turned, dt_copied = sem("cum_ready"), sem("dt_turned"), sem("dt_copied")
        v_hi_made, v_lo_made = sem("v_hi_made"), sem("v_lo_made")
        s_ready, max_made, prob_made, inv_made, prob_normed, prob_turned, prob_hi_made, prob_lo_made = map(
            sem, ("s_ready", "max_made", "prob_made", "inv_made", "prob_normed", "prob_turned", "prob_hi_made", "prob_lo_made"))
        o_ready, y_part_made, y_made = map(sem, ("o_ready", "y_part_made", "y_made"))
        e_ready, decay_made, m_made, m_hi_made, m_lo_made, yo_ready, yo_part_made, y_summed, ys_made = map(
            sem, ("e_ready", "decay_made", "m_made", "m_hi_made", "m_lo_made", "yo_ready", "yo_part_made", "y_summed", "ys_made"))
        z_scaled, z_made, gated, y_squared, y_sums_made, y_root_made, y_rms_made, y_normed = map(
            sem, ("z_scaled", "z_made", "gated", "y_squared", "y_sums_made", "y_root_made", "y_rms_made", "y_normed"))
        mix_hi_made, mix_lo_made = sem("mix_hi_made"), sem("mix_lo_made")
        ffn_step, ffn_silu, ffn_act, ffn_hi, ffn_lo = map(
            sem, ("ffn_step", "ffn_silu", "ffn_act", "ffn_hi", "ffn_lo"))
        ffn_out, gain_fin_landed, stored = map(sem, ("ffn_out", "gain_fin_landed", "stored"))
        gate_first, ple_sig, ple_mul, xtok_turned, xtok_copied, out_added, out_squared, out_gained = map(
            sem, ("gate_first", "ple_sig", "ple_mul", "xtok_turned", "xtok_copied", "out_added", "out_squared", "out_gained"))
        out_sum_made, out_root_made, out_rms_made = map(sem, ("out_sum_made", "out_root_made", "out_rms_made"))
        out_final, out_final_act = sem("out_final"), sem("out_final_act")

        block = ctx.enter_context(nc.Block())

        def load_chunk(sp, n, src, q=0):
            if n >= RING:
                sp.wait_ge(w_lo_made, n + RING * q - RING + 1)
            sp.dma_start(w_raw[:, n % RING, :].rearrange("p (a c) -> p a c", a=2), src).then_inc(w_landed[n % RING], 16)

        def parts(n):
            if n_last <= n < n_last + KP - 1:
                return last_hi[:, n - n_last, :], last_lo[:, n - n_last, :]
            return w_hi[:, n % RING, :], w_lo[:, n % RING, :]

        def make_hi(act, n, q=0):
            act.wait_ge(w_landed[n % RING], 16 * (n // RING + q + 1))
            if RING <= n < n_last:
                act.wait_ge(w_used, n + RING * q - RING + 1)
            elif n >= n_last + KP - 1:
                act.wait_ge(w_used, n_last)
            act.activation(parts(n)[0], w_raw[:, n % RING, :], ACT.Copy).then_inc(w_hi_made, 1)

        def make_lo(dve, n, q=0):
            dve.wait_ge(w_hi_made, n + RING * q + 1)
            hi, lo = parts(n)
            dve.tensor_tensor(lo, w_raw[:, n % RING, :], hi, ALU.subtract).then_inc(w_lo_made, 1)

        def chunk_of(g, c):
            return g.view[:, 2 * c:2 * c + 2, g.col:g.col + COLS]

        def multiply(pe, n, opHi, opLo, tiles, bank_of, q=0, between=None):
            pe.wait_ge(w_lo_made, n + RING * q + 1)
            s = n % RING
            for i, (k, m, start, stop) in enumerate(tiles):
                if between and i == len(tiles) // 2:
                    between()
                dst = ps[:, bank_of[m // 2], (m % 2) * T:(m % 2) * T + T]
                hi, lo = w_hi[:, s, i * P:(i + 1) * P], w_lo[:, s, i * P:(i + 1) * P]
                pe.matmul(dst, hi, opHi(k), start=start and m % 2 == 0, stop=False, skip_group_check=True)
                pe.matmul(dst, hi, opLo(k), start=False, stop=False, skip_group_check=True)
                mm = pe.matmul(dst, lo, opHi(k), start=False, stop=stop, skip_group_check=True)
            return mm.then_inc(w_used, 1)

        def pair_tiles(first, last):
            return [(kk, m, first and kk == 0, last and kk == 1) for kk in range(2) for m in range(MT)]

        down_banks = (SET_B, SET_D, SET_C, SET_A)

        def multiply_group(pe, n, g, c, only=(0, 1), between=None):
            opHi, opLo = {"h": (hHi, hLo), "mix": (mixHi, mixLo), "p": (pHi, pLo)}[g.operand]
            first, last = c == 0, c == g.chunks - 1
            if not g.by_token:
                return multiply(pe, n, lambda k: opHi[:, 2 * c + k, :], lambda k: opLo[:, 2 * c + k, :],
                                pair_tiles(first, last), g.banks, between=between)
            pe.wait_ge(w_lo_made, n + 1)
            order = [(kk, t) for t in range(TT) for kk in range(2)] if last else [(kk, t) for kk in range(2) for t in range(TT)]
            for i, (kk, t) in enumerate(order):
                if t not in only:
                    continue
                hi, lo = (w[:, kk * COLS:(kk + 1) * COLS] for w in parts(n))
                dst = ps[:, g.banks[t], :]
                a, b = (o_[:, 2 * c + kk, t * P:(t + 1) * P] for o_ in (opHi, opLo))
                pe.matmul(dst, a, hi, start=first and kk == 0, stop=False)
                pe.matmul(dst, a, lo, start=False, stop=False)
                mm = pe.matmul(dst, b, hi, start=False, stop=last and kk == 1)
                if g.name[:2] == "pg" and last and i == 1:
                    mm.then_inc(gate_first, 1)
            if n < n_last or (last and only == (1,)):
                mm.then_inc(w_used, 1)

        evacuated = {n: (dve_evac, i + 1) for i, n in enumerate(("q0", "k0", "q1", "k1"))}
        evacuated |= {f"v{i}": (v_lo_made, TT * (i + 1)) for i in range(2)}
        evacuated |= {f"z{i}": (z_scaled, 2 * (i + 1)) for i in range(2)}
        evacuated |= {n: (conv_step, CONV_STEPS * (2 * i + 1) + 1) for i, n in enumerate(("bc", "x0", "x1"))}
        NORM = KD // 2
        evacuated |= {f"o{i}": (x_new, NORM + 2 * i + 2) for i in range(NDN)}
        evacuated |= {f"dn{i}": (x_new, 2 * NORM + 2 * i + 2) for i in range(NDN)}

        bank_user = {}

        def wait_banks(pe, name, banks):
            waits = {}
            for b in banks:
                if b in bank_user:
                    s, val = bank_user[b]
                    waits[s.name] = (s, max(val, waits.get(s.name, (s, 0))[1]))
                bank_user[b] = evacuated[name]
            for s, val in waits.values():
                pe.wait_ge(s, val)

        LEAD = 3
        end = {g.name: done[g.name] for g in in_groups + out_groups}
        pe_after, act_after, dve_after = {}, {}, {}

        def after(table, n, what, *args):
            table.setdefault(n, []).append((what, args))

        def plan():
            def all_after(n, name, *args):
                after(pe_after, n, name, *args)
                after(act_after, n + LEAD, name, *args)
                after(dve_after, n + LEAD, name, *args)

            all_after(end["q0"], "stats0")
            for g in in_groups:
                if g.by_token:
                    after(act_after, end[g.name] + LEAD, "leave_v", g)
                    after(dve_after, end[g.name] + LEAD, "leave_v", g)
                elif g.name[0] in "qk":
                    after(dve_after, end[g.name] + LEAD, "leave", g)
            for i, g in enumerate(("bc", "x0", "x1")):
                for b in range(2):
                    n = end[g] + LEAD + 3 * b
                    after(dve_after, n, "conv_start", g, b)
                    after(dve_after, n + 1, "conv_taps", 2 * i + b)
                    after(act_after, n + 2, "conv_silu", 2 * i + b)
            all_after(end["q0"] + 1, "turn_par")
            all_after(end["q0"] + 2, "fd")
            after(dve_after, end["q0"] + 4 + LEAD, "softplus")
            after(dve_after, end["q0"] + 7 + LEAD, "cumulate")
            after(dve_after, end["bc"] + 6 + LEAD, "make_row", 0)
            after(dve_after, end["bc"] + 7 + LEAD, "make_row", 1)
            all_after(end["bc"] + 4, "cums")
            all_after(end["bc"] + 10, "cb", 0)
            all_after(end["bc"] + 13, "cb", 1)
            all_after(end["x0"] + 7, "turn_xs", 0)
            all_after(end["x1"] + 7, "turn_xs", 1)
            b0 = end["x1"] + 9
            for i in range(H + 2):
                all_after(b0 + i * 6 // 5, "ssd", i)
            a0 = end["v0"] - 1
            for i in range(H + 3):
                all_after(a0 + i, "fox", i)
            for b in range(WT // 2):
                all_after(a0 + H + 3 + b, "split_fox", b)
            for half in range(2):
                n = end[f"z{half}"] + LEAD
                after(dve_after, n, "leave_z", half)
                after(act_after, n, "leave_z", half)
                after(dve_after, n + 1, "gate_mul", half)
            all_after(end["z1"] + 6, "gate_norm")
            for b in range(WT // 2):
                n = end["z1"] + 7 + b + LEAD
                after(dve_after, n, "scale_ssd", b)
                after(act_after, n + 1, "split_ssd", b)
                after(dve_after, n + 2, "split_ssd", b)
            for g in ("o0", "o1", "o2"):
                i = int(g[1])
                after(act_after, end[g] + LEAD, "leave_out", i)
                after(dve_after, end[g] + LEAD, "leave_out", i)

        plan()

        STATS1_AT = 11
        UNIT_AT = (3, 9)
        U_IN, U_TAPS, U_SILU, U_ACT, U_HI, U_LO = range(6)
        STATS2_AT = 7
        GROUP = KP + 1
        XTURN_AT, XCOPY_AT = 5, 5 + LEAD
        SIG_AT, MUL_AT, ADD_AT, SQUARE_AT, GAIN_AT = (GROUP - 1 + LEAD + j for j in (0, 1, 4, 5, 6))

        def run(table, n, steps):
            for name, args in table.get(n, ()):
                if name in steps:
                    steps[name](*args)

        def flush(table, n, steps):
            for m in sorted(k for k in table if k >= n):
                run(table, m, steps)

        S_BANKS = (0, 1, 7)
        TURN_BANK, SPARE_BANK = 6, 7
        X_BANKS = (0, 1, 6, 7)
        XS_BANKS = (0, 1, 6, 7)
        groups = {g.name: g for g in in_groups + out_groups}
        s_bank = lambda h: S_BANKS[h % 3]

        @block.sync
        def _(sp):
            as_rows = lambda a: a.rearrange("(r p) -> r p", p=P)
            sp.dma_start(mix_rows[:, :], as_rows(mix_norm_w[0])).then_inc(gain_landed, 16)
            x_v = x[0].rearrange("(t p) n -> p t n", p=P)
            for j, (a, b) in enumerate(X_PIECES):
                cols = slice(2 * a * P, 2 * b * P)
                sp.dma_start(xtok[:, :, cols], x_v[:, :, cols]).then_inc(x_landed[j], 16)
                if j < RING:
                    load_chunk(sp, j, chunk_of(*front[j]))
            with nc.allow_non_contiguous_dma(reason="the forget and dt columns of w_in are 16 wide"):
                sp.dma_start(w_fd[:, :, 0:H], win_v[:, :, c_f:c_f + H]).then_inc(fd_landed, 16)
                sp.dma_start(w_fd[:, :, H:2 * H], win_v[:, :, c_dt:c_dt + H]).then_inc(fd_landed, 16)
            load_chunk(sp, RING, chunk_of(*front[RING]))
            sp.dma_start(ptok[:, :, :], p[0, 0].rearrange("(t p) c -> p t c", p=P)).then_inc(p_landed, 16)
            column = lambda a: a[0].rearrange("(h a) -> h a", a=1)
            sp.dma_start(fdc[0:H, 0:1], column(fox_forget_bias)).then_inc(small_landed, 16)
            sp.dma_start(fdc[H:2 * H, 0:1], column(ssd_dt_bias)).then_inc(small_landed, 16)
            sp.wait_ge(consts_made, 1)
            sp.dma_start(fdc[H:2 * H, 2:3], column(ssd_A_log)).then_inc(alog_landed, 16)
            sp.dma_start(d_all[:, :], ssd_D[0:1, :].to_broadcast([P, H])).then_inc(small_landed, 16)
            load_chunk(sp, RING + 1, chunk_of(*front[RING + 1]))

            def param_rows(dst_tile, at_row, src, n):
                sp.dma_start(par_rows[at_row:at_row + n, dst_tile, :], as_rows(src)).then_inc(par_landed, 16)

            row = 0
            for src, n in ((ffn_norm_w[0], KD), (ple_norm_w[0], KD),
                           (ssd_norm_w[0], WT), (ssd_conv_b[0], CT), (ffn_conv_b[0], FT)):
                param_rows(0, row, src, n)
                row += n
            for i in range(KC):
                param_rows(1, i * CT, ssd_conv_w[0, i], CT)
            param_rows(1, KC * CT, ffn_conv_w[0, 0], FT)
            param_rows(2, 0, ffn_conv_w[0, 1], FT)
            param_rows(2, FT, ffn_conv_w[0, 2], FT)
            for n in range(RING + 2, len(front)):
                load_chunk(sp, n, chunk_of(*front[n]))
            gu = wgu_v.rearrange("p k (a n) -> p k a n", a=2)
            for k in range(KD):
                load_chunk(sp, n_ffn + k, gu[:, k, :, 0:COLS])
            with sp.Fori(0, NG // 2) as i:
                for j in range(2):
                    for k in range(KD):
                        load_chunk(sp, n_ffn + (1 + j) * KD + k,
                                   gu[:, k, :, bass.ds(i * (2 * COLS) + (1 + j) * COLS, COLS)], i * (2 * KD // RING))
            for g in range(NDN):
                n0 = n_down + g * KDN
                cols = slice(g * COLS, (g + 1) * COLS)
                for c in range(2):
                    load_chunk(sp, n0 + c, wdn_v[:, 2 * c:2 * c + 2, cols])
                with sp.Fori(0, KDN // RING) as q:
                    for j in range(RING):
                        load_chunk(sp, n0 + 2 + j, wdn_v[:, bass.ds(q * (2 * RING) + 2 * (2 + j), 2), cols], q)
            for i, (g, c) in enumerate(tail):
                load_chunk(sp, n_ple + i, chunk_of(g, c))
                if i == RING:
                    sp.dma_start(gain_fin[:, :], final_norm_w.rearrange("(a n) -> a n", a=1).to_broadcast([P, D])).then_inc(gain_fin_landed, 16)
            out_v = out[0].rearrange("(t p) n -> p t n", p=P)
            for t in range(TT):
                for i in range(NDN // 2):
                    for finished, j in ((out_final, NDN // 2 + i), (out_final_act, i)):
                        sp.wait_ge(finished, t * (NDN // 2) + i + 1)
                        cols = slice(j * COLS, (j + 1) * COLS)
                        sp.dma_start(out_v[:, t, cols], out_tok[:, t, cols]).then_inc(stored, 16)
            sp.wait_ge(stored, 16 * TT * NDN)

        @block.gpsimd
        def _(pool):
            steps = [0]

            def link(ins):
                steps[0] += 1
                ins.then_inc(pool_step, 1)

            def linked():
                pool.wait_ge(pool_step, steps[0])

            def select(dst, src, keep, fill, base, per_partition, per_column, n):
                return pool.affine_select(out=dst, in_=src, compare_op=keep, fill=fill, base=base,
                                          pattern=[[per_column, n]], channel_multiplier=per_partition)

            pool.memset(fdc[:, 2:3], 0.0).then_inc(consts_made, 1)
            link(pool.memset(ident[:, :], 0.0))
            link(pool.memset(sel_f[:, :], 0.0))
            link(pool.memset(fdc[:, 1:2], -1.0))
            link(pool.memset(fdw[:, 0, :], 1.0))
            link(pool.memset(mask_q[:, :], 0.0))
            link(pool.memset(mask_s[:, :], 0.0))
            pool.memset(eps[:, :], EPS).then_inc(consts_made, 1)
            linked()
            select(ident[:, :], ident[:, :], ALU.not_equal, 1.0, 0, 1, -1, P).then_inc(consts_made, 1)
            pool.memset(ones[:, :], 1.0).then_inc(consts_made, 1)
            link(select(sel_f[:, :], sel_f[:, :], ALU.not_equal, 1.0, 0, 1, -1, 2 * H))
            linked()
            select(sel_f[:, :], sel_f[:, :], ALU.not_equal, 1.0, -2 * H, 1, -1, 2 * H).then_inc(masks_made, 1)
            select(fdc[:, 1:2], fdc[:, 1:2], ALU.is_ge, 1.0, H - 1, -1, 0, 1).then_inc(masks_made, 1)
            select(fdw[:, 0, P:P + 1], fdw[:, 0, P:P + 1], ALU.is_ge, 0.0, H - 1, -1, 0, 1).then_inc(masks_made, 1)
            select(mask_q[:, :], mask_q[:, :], ALU.is_ge, MASKED, 0, 1, -1, P).then_inc(masks_made, 1)
            select(mask_s[:, :], mask_s[:, :], ALU.is_ge, MASKED, 0, -1, 1, P).then_inc(masks_made, 1)
            pool.wait_ge(masks_made, 5)
            for i, half in enumerate((kE[P // 2:P, :, :], kO[0:P // 2, :, :], conv_in[:, :, 0:4])):
                pool.memset(half, 0.0).then_inc(masks_made, 1)
                pool.wait_ge(masks_made, 6 + i)
            for norm in range(3):
                if norm == 1:
                    pool.wait_ge(a_exp, 1)
                    select(fdc[:, 3:4], fdc[:, 3:4], ALU.is_ge, 1.0, -H, 1, 0, 1).then_inc(a_ready, 1)
                    for b in range(WT // 2):
                        pool.wait_ge(gated, b // 2 + 1)
                        if b == 0:
                            pool.wait_ge(sums_made, norm)
                        pair = xsT[:, 2 * b:2 * b + 2, :]
                        if b > 0:
                            linked()
                        link(pool.tensor_tensor(sq[:, :, :] if b > 0 else sumsq[:, :, :], pair, pair, ALU.mult))
                        if b > 0:
                            linked()
                            link(pool.tensor_tensor(sumsq[:, :, :], sumsq[:, :, :], sq[:, :, :], ALU.add))
                    linked()
                    pool.tensor_tensor(sumsq[:, 0, :], sumsq[:, 0, :], sumsq[:, 1, :], ALU.add).then_inc(y_squared, 1)
                for b in range(KD // 2):
                    pool.wait_ge(x_new, norm * (KD // 2) + b + 1)
                    if b == 0 and norm > 0:
                        pool.wait_ge(sums_made, norm)
                        pool.wait_ge(y_sums_made, 1)
                    pair = xT[:, 2 * b:2 * b + 2, :]
                    if b == 0:
                        link(pool.tensor_tensor(sumsq[:, :, :], pair, pair, ALU.mult))
                        continue
                    linked()
                    link(pool.tensor_tensor(sq[:, :, :], pair, pair, ALU.mult))
                    linked()
                    link(pool.tensor_tensor(sumsq[:, :, :], sumsq[:, :, :], sq[:, :, :], ALU.add))
                linked()
                pool.tensor_tensor(sumsq[:, 0, :], sumsq[:, 0, :], sumsq[:, 1, :], ALU.add).then_inc(squares_made, 1)

        @block.tensor
        def _(pe):
            def keep_busy(times):
                for _ in range(times):
                    pe.matmul(ps[:, 5, :], idle_in[:, 0:P], idle_in[:, :], start=True, stop=True)

            pe.wait_ge(idle_in_made, 1)
            keep_busy(4)
            pe.wait_ge(consts_made, 4)
            pe.wait_ge(gain_landed, 16)
            pe.transpose(ps[:, 4, 0:KD], mix_rows[:, :], ident[0:KD, 0:KD]).then_inc(gain_turned, 1)

            def turn_x(b):
                for j, (first, _) in enumerate(X_PIECES):
                    if b == first:
                        pe.wait_ge(x_landed[j], 16)
                if b >= len(X_BANKS):
                    pe.wait_ge(x_new, b - len(X_BANKS) + 1)
                for kk in range(2):
                    for t in range(TT):
                        k = 2 * b + kk
                        mm = pe.transpose(ps[:, X_BANKS[b % len(X_BANKS)], kk * T + t * P:kk * T + t * P + P],
                                          xtok[:, t, k * P:(k + 1) * P], ident[:, :])
                mm.then_inc(x_turned, 1)

            keep_busy(2)
            turn_x(0)
            keep_busy(3)
            turn_x(1)
            keep_busy(5)

            def turn_x_early():
                turn_x(2)
                turn_x(3)

            def turn_par():
                pe.wait_ge(par_landed, 16 * 12)
                pe.wait_ge(x_new, NORM)
                for i, r in enumerate(par_spans):
                    mm = pe.transpose(ps[:, 1, i * P:i * P + r], par_rows[0:r, i, :], ident[0:r, 0:r])
                mm.then_inc(par_turned, 1)

            def turn_p():
                pe.wait_ge(p_landed, 16)
                pe.wait_ge(x_new, NORM - 1)
                for kk in range(2):
                    for t in range(TT):
                        mm = pe.transpose(ps[:, 0, kk * T + t * P:kk * T + t * P + P],
                                          ptok[:, t, kk * P:(kk + 1) * P], ident[:, :])
                mm.then_inc(p_turned, 1)

            def stats(norm, bank, columns=True, rows_=True):
                pe.wait_ge(squares_made, norm + 1)
                if rows_:
                    mm = pe.matmul(ps[:, bank, 0:T], ones[:, :], sumsq[:, 0, :], start=True, stop=True, skip_group_check=True)
                if columns:
                    for t in range(TT):
                        mm = pe.matmul(ps[:, bank, T + t:T + t + 1], sumsq[:, 0, t * P:(t + 1) * P], ones[:, 0:1],
                                       start=True, stop=True, skip_group_check=True)
                mm.then_inc(sums_made, 1)

            def stats0():
                turn_p()
                pe.wait_ge(x_new, KD // 2)
                stats(0, SPARE_BANK)

            def fd():
                pe.wait_ge(wfd_lo_made, 1)
                for k in range(KD):
                    pe.matmul(ps[0:4 * H, TURN_BANK, 0:T], w_fd_parts[:, k, :], hHi[:, k, :],
                              start=k == 0, stop=False, skip_group_check=True)
                    mm = pe.matmul(ps[0:2 * H, TURN_BANK, 0:T], w_fd_parts[:, k, 0:2 * H], hLo[:, k, :],
                                   start=False, stop=k == KD - 1, skip_group_check=True)
                mm.then_inc(fd_ready, 1)

            def cums():
                pe.wait_ge(fd_step, CUMULATE_STEPS)
                pe.wait_ge(root_made, 1)
                for i, row in enumerate((6, 1)):
                    for t in range(TT):
                        mm = pe.transpose(ps[:, SPARE_BANK, (i * TT + t) * 2 * H:(i * TT + t + 1) * 2 * H],
                                          fdw[:, row, t * P:(t + 1) * P], ident[0:2 * H, 0:2 * H])
                mm.then_inc(dt_turned, 1)

            def cb(g):
                if g == 0:
                    pe.wait_ge(silu_made, 2)
                    pe.wait_ge(dt_copied, 2)
                else:
                    pe.wait_ge(cb_copied, g)
                for s, l0, width, dst in ((0, 0, T, 0), (1, P, P, T)):
                    mm = pe.matmul(ps[:, SPARE_BANK, dst:dst + width], bcT[:, g, s * P:(s + 1) * P],
                                   bcT[:, G + g, l0:l0 + width], start=True, stop=True, skip_group_check=True)
                mm.then_inc(cb_ready, 1)

            def exponent_terms(bank, j, row, mask, start):
                both = 4 * H
                pe.matmul(ps[:, bank, 0:3 * P], sel[0:both, j:j + 1].to_broadcast([both, P]), row[:, :],
                          start=start, stop=False, skip_group_check=True)
                for dst in (0, T):
                    mm = pe.matmul(ps[:, bank, dst:dst + P], ident_bf[:, :], mask[:, :],
                                   start=False, stop=True, skip_group_check=True)
                return mm

            def fox(i):
                if 2 <= i < H + 2:
                    h = i - 2
                    pe.wait_ge(prob_normed, 2 * h + 2)
                    if h >= 1:
                        pe.wait_ge(prob_lo_made, h)
                    for b in range(3):
                        mm = pe.transpose(ps[:, TURN_BANK, b * P:(b + 1) * P], prob[:, h % 2, b * P:(b + 1) * P], ident[:, :])
                    mm.then_inc(prob_turned, 1)
                if i >= 3:
                    h = i - 3
                    pe.wait_ge(prob_lo_made, h + 1)
                    if h % (H // 2) == 0:
                        pe.wait_ge(*evacuated[f"v{h // (H // 2)}"])
                    if h < H - 1:
                        pe.wait_ge(prob_made, 2 * h + 4)
                    for n, (probs, width) in enumerate(((probT_hi, 2 * HD), (probT_lo, HD))):
                        for t, (a, b, dst) in enumerate(((0, T, 0), (T, 3 * P, P))):
                            mm = pe.matmul(ps[0:width, s_bank(h + 1), dst:T], v_parts[:, t, h, 0:width], probs[:, h % 2, a:b],
                                           start=n == 0 and t == 0, stop=n == 1, skip_group_check=True)
                    mm.then_inc(o_ready, 1)
                if i < H:
                    h = i
                    bank = s_bank(h)
                    if h == 0:
                        pe.wait_ge(*evacuated["k1"])
                        pe.wait_ge(y_summed, H)
                    if h == 3:
                        pe.wait_ge(prob_made, 2)
                    if h >= 4:
                        pe.wait_ge(y_made, h - 3)
                    keys = (kE, kO)[h % 2]
                    pe.matmul(ps[:, bank, 0:P], qT[:, h // 2, 0:P], keys[:, h // 2, 0:P],
                              start=True, stop=False, skip_group_check=True)
                    pe.matmul(ps[:, bank, P:3 * P], qT[:, h // 2, P:T], keys[:, h // 2, :],
                              start=False, stop=False, skip_group_check=True)
                    exponent_terms(bank, h, fox_row, mask_q, start=False).then_inc(s_ready, 1)

            def ssd(i):
                if i >= 2:
                    h = i - 2
                    pe.wait_ge(m_lo_made, h + 1)
                    for n, (m, width) in enumerate(((mT_hi, 2 * HD), (mT_lo, HD))):
                        for t, (a, b, dst) in enumerate(((0, T, 0), (T, 3 * P, P))):
                            mm = pe.matmul(ps[0:width, s_bank(h), dst:T], xdt_parts[:, t, h, 0:width], m[:, h % 2, a:b],
                                           start=n == 0 and t == 0, stop=n == 1, skip_group_check=True)
                    mm.then_inc(yo_ready, 1)
                if i < H:
                    h = i
                    if h == 0:
                        pe.wait_ge(cum_ready, 2)
                        pe.wait_ge(xdt_lo_made, 2 * TT)
                    if h >= 3:
                        pe.wait_ge(y_summed, h - 2)
                    exponent_terms(s_bank(h), H + h, ssd_row, mask_s, start=True).then_inc(e_ready, 1)

            def turn_xs(half):
                pe.wait_ge(silu_made, 4 + 2 * half)
                if half == 0:
                    pe.wait_ge(par_copied, 1)
                    pe.wait_ge(p_lo_made, 1)
                else:
                    pe.wait_ge(fd_step, CUMULATE_STEPS)
                    pe.wait_ge(cb_copied, G)
                for t in range(TT):
                    for j in range(WT // 2):
                        mm = pe.transpose(ps[:, XS_BANKS[TT * half + t], j * P:(j + 1) * P],
                                          xsT[:, WT // 2 * half + j, t * P:(t + 1) * P], ident[:, :])
                    mm.then_inc(xs_turned, 1)

            def gate_norm():
                pe.wait_ge(y_squared, 1)
                pe.wait_ge(y_made, H)
                pe.matmul(ps[:, SPARE_BANK, 0:T], ones[:, :], sumsq[:, 0, :], start=True, stop=True).then_inc(y_sums_made, 1)

            steps = dict(turn_par=turn_par, stats0=stats0, fd=fd, cums=cums, cb=cb, fox=fox, ssd=ssd, turn_xs=turn_xs,
                         gate_norm=gate_norm)
            for n, (g, c) in enumerate(front):
                if c == 0:
                    wait_banks(pe, g.name, g.banks)
                    if g.name == "o2":
                        pe.wait_ge(y_made, H)
                    if g.name == "o3":
                        pe.wait_ge(mix_lo_made, WT)
                if g.name == "q0":
                    pe.wait_ge(h_lo_made, 2 * c + 2)
                if g.name == "bc" and c == 0:
                    pe.wait_ge(gain_copied, 1)
                if g.name == "o0":
                    pe.wait_ge(mix_lo_made, c + 1)
                multiply_group(pe, n, g, c, between=turn_x_early if n == 0 else None)
                if n + len(X_BANKS) < NORM:
                    turn_x(n + len(X_BANKS))
                run(pe_after, n, steps)
            flush(pe_after, len(front), steps)

            def ffn_chunk(n, k, half, q=0):
                return multiply(pe, n, lambda _: hHi[:, k, :], lambda _: hLo[:, k, :],
                                [(k, m, k == 0, k == KD - 1) for m in range(2 * MT)],
                                [4 * half + b for b in range(4)], q)

            for k in range(KD):
                if k == 0:
                    for name in ("o1", "o2"):
                        pe.wait_ge(*evacuated[name])
                pe.wait_ge(h_lo_made, KD + k + 1)
                ffn_chunk(n_ffn + k, k, 0)
                if k == KD // 2:
                    pe.wait_ge(*evacuated["o0"])
                if k == STATS1_AT:
                    stats(1, 4, columns=False)
            pe.wait_ge(root_made, 2)
            with pe.Fori(0, NG // 2) as i:
                for j in range(2):
                    for k in range(KD):
                        if k == 0:
                            pe.wait_ge(ffn_out, i * 4 + (1, 3)[j])
                        ffn_chunk(n_ffn + (1 + j) * KD + k, k, 1 - j, i * (2 * KD // RING))

            for g in range(NDN):
                n0 = n_down + g * KDN

                def chunk(j, q, first=False, last=False):
                    at_ = (lambda t, k: t[:, 2 * j + k, :]) if isinstance(q, int) else \
                        (lambda t, k: t[:, bass.ds(q * (2 * RING) + (2 * j + k), 1), :])
                    return multiply(pe, n0 + j, lambda k: at_(actHi, k), lambda k: at_(actLo, k),
                                    pair_tiles(first, last), down_banks[g], q)

                pe.wait_ge(ffn_lo, 2 * (NG - 1) if g == 0 else 2 * NG)
                for j in range(2):
                    chunk(j, 0, first=j == 0)
                with pe.Fori(0, KDN // RING - 1) as q:
                    for j in range(2, 2 + RING):
                        chunk(j, q)
                if g == 0:
                    pe.wait_ge(ffn_lo, 2 * NG)
                for j in range(KDN - RING, KDN):
                    chunk(j, 0, last=j == KDN - 1)

            def turn_residual(i):
                pe.wait_ge(x_new, 3 * NORM - 2 * (NDN - 1 - i) if i < NDN - 1 else 3 * NORM)
                if i == 0:
                    pe.wait_ge(*evacuated["dn3"])
                else:
                    pe.wait_ge(xtok_copied, TT * i)
                for t in range(TT):
                    for m in range(MT):
                        mm = pe.transpose(ps[:, XTOK_BANKS[t], m * P:(m + 1) * P],
                                          xT[:, MT * i + m, t * P:(t + 1) * P], ident[:, :])
                    mm.then_inc(xtok_turned, 1)

            for n, (g, c) in enumerate(tail):
                i = n // GROUP
                if g.name[:2] == "pg" and c == 0:
                    if i < 2:
                        pe.wait_ge(*evacuated[f"dn{i}"])
                        if i == 1:
                            pe.wait_ge(root_made, 3)
                    else:
                        pe.wait_ge(ple_sig, TT * (i - 1))
                if g.name[:2] == "pp":
                    if i == 0:
                        pe.wait_ge(*evacuated["dn2"])
                    else:
                        pe.wait_ge(ple_mul, TT * i)
                if g.name == "pg0":
                    pe.wait_ge(h_lo_made, 2 * KD + 2 * c + 2)
                multiply_group(pe, n_ple + n, g, c, (0, 1) if i < NDN - 1 or g.name[:2] == "pp" else (0,))
                if n == STATS2_AT:
                    stats(2, GATE_BANKS[1][0], rows_=False)
                if n % GROUP == XTURN_AT:
                    turn_residual(i)
            for n, (g, c) in enumerate(tail):
                if n >= len(tail) - GROUP and g.name[:2] == "pg":
                    multiply_group(pe, n_ple + n, g, c, (1,))

        @block.scalar
        def _(act):
            def copy(dst, src, scale=1.0):
                return act.activation(dst, src, ACT.Copy, scale=scale)

            def make_h(norm, k, gain):
                act.wait_ge(x_new, norm * NORM + k // 2 + 1)
                copy(hHi[:, k, :], xT[:, k, :], gain[:, k:k + 1]).then_inc(h_hi_made, 1)

            def stats(norm, bank, a=0, b=T):
                act.wait_ge(sums_made, norm + 1)
                act.wait_ge(tables_loaded, 1)
                act.activation(root[:, a:b], ps[:, bank, a:b], ACT.Sqrt, bias=eps[:, :], scale=1.0 / D).then_inc(root_made, 1)

            def conv_silu(u):
                act.wait_ge(conv_step, CONV_STEPS * (u + 1))
                dst = bcT[:, 2 * u:2 * u + 2, :] if u < 2 else xsT[:, 2 * (u - 2):2 * (u - 2) + 2, :]
                act.activation(dst, conv_out[:, u % 2, :, :], ACT.Silu).then_inc(silu_made, 1)

            def leave_v(g):
                act.wait_ge(w_used, done[g.name] + 1)
                half = int(g.name[1])
                heads = slice(half * H // 2, (half + 1) * H // 2)
                for t in range(TT):
                    act.activation(v_parts[:, t, heads, 0:HD], ps[:, g.banks[t], :].rearrange("p (h d) -> p h d", d=HD),
                                   ACT.Copy, scale=rms_col[:, t:t + 1]).then_inc(v_hi_made, 1)

            def leave_z(half):
                for b in (2 * half, 2 * half + 1):
                    act.wait_ge(z_scaled, b + 1)
                    tiles = zT[:, 2 * b:2 * b + 2, :]
                    act.activation(tiles, tiles, ACT.Silu).then_inc(z_made, 1)

            def turn_xs(half):
                heads = slice(half * H // 2, (half + 1) * H // 2)
                for t in range(TT):
                    act.wait_ge(xdt_made, TT * half + t + 1)
                    copy(xdt_parts[:, t, heads, 0:HD],
                         xdt[:, t, half * COLS:(half + 1) * COLS].rearrange("p (h d) -> p h d", d=HD)).then_inc(xdt_hi_made, 1)

            def p_hi():
                act.wait_ge(p_turned, 1)
                copy(pHi[:, :, :], ps[:, 0, :]).then_inc(p_hi_made, 1)

            def stats0():
                p_hi()
                stats(0, SPARE_BANK, 0, T + TT)

            def fd():
                act.wait_ge(fd_step, 4)
                act.activation(fdw[:, 2, :], fdw[:, 1, :], ACT.Abs).then_inc(fd_abs, 1)
                act.wait_ge(fd_abs, 1)
                act.activation(fdw[:, 3, :], fdw[:, 2, :], ACT.Exp, scale=-1.0).then_inc(fd_exp, 1)
                act.wait_ge(alog_landed, 16)
                act.activation(fdc[:, 3:4], fdc[:, 2:3], ACT.Exp).then_inc(a_exp, 1)

            def fox(i):
                if 2 <= i < H + 2:
                    h = i - 2
                    act.wait_ge(prob_turned, h + 1)
                    if h >= 2:
                        act.wait_ge(o_ready, h - 1)
                    copy(probT_hi[:, h % 2, :], ps[:, TURN_BANK, 0:3 * P]).then_inc(prob_hi_made, 1)
                if i >= 3:
                    h = i - 3
                    act.wait_ge(o_ready, h + 1)
                    if h >= 2:
                        act.wait_ge(y_made, h - 1)
                    copy(y_part[:, h % 2, :], ps[HD:2 * HD, s_bank(h + 1), 0:T]).then_inc(y_part_made, 1)
                if i < H:
                    h = i
                    act.wait_ge(max_made, 2 * h + 2)
                    if h >= 2:
                        act.wait_ge(prob_turned, h - 1)
                    for t, (a, b) in enumerate(((0, P), (P, 3 * P))):
                        act.activation(prob[:, h % 2, a:b], ps[:, s_bank(h), a:b], ACT.Exp,
                                       bias=neg_max[:, h, t:t + 1], accum_out=row_sum[:, h, t:t + 1]).then_inc(prob_made, 1)

            def ssd(i):
                if 1 <= i < H + 1:
                    h = i - 1
                    act.wait_ge(m_made, h + 1)
                    if h >= 2:
                        act.wait_ge(yo_ready, h - 1)
                    copy(mT_hi[:, h % 2, :], mT[:, h % 2, :]).then_inc(m_hi_made, 1)
                if i >= 2:
                    h = i - 2
                    act.wait_ge(yo_ready, h + 1)
                    if h >= 2:
                        act.wait_ge(y_summed, h - 1)
                    copy(y_part[:, h % 2, :], ps[HD:2 * HD, s_bank(h), 0:T]).then_inc(yo_part_made, 1)
                if i < H:
                    h = i
                    act.wait_ge(e_ready, h + 1)
                    if h >= 2:
                        act.wait_ge(m_made, h - 1)
                    if h == 0:
                        act.wait_ge(dt_copied, 2)
                    for t, (a, b) in enumerate(((0, T), (T, 3 * P))):
                        act.activation(decay[:, h % 2, a:b], ps[:, s_bank(h), a:b], ACT.Exp,
                                       bias=ncum_tok[:, t, H + h:H + h + 1]).then_inc(decay_made, 1)

            def split_fox(b):
                act.wait_ge(y_made, H)
                copy(mixHi[:, 2 * b:2 * b + 2, :], y_foxT[:, 2 * b:2 * b + 2, :]).then_inc(mix_hi_made, 1)

            def gate_norm():
                act.wait_ge(y_sums_made, 1)
                act.activation(root[:, 0:T], ps[:, SPARE_BANK, 0:T], ACT.Sqrt, bias=eps[:, :], scale=1.0 / W).then_inc(y_root_made, 1)

            def split_ssd(b):
                act.wait_ge(y_normed, 2 * b + 2)
                copy(mixHi[:, WT + 2 * b:WT + 2 * b + 2, :], xsT[:, 2 * b:2 * b + 2, :]).then_inc(mix_hi_made, 1)

            def leave_out(i):
                for k in range(MT * i, MT * (i + 1)):
                    make_h(1, k, par_ffn)

            steps = dict(leave_v=leave_v, leave_z=leave_z, stats0=stats0, fd=fd, fox=fox, ssd=ssd, turn_xs=turn_xs,
                         conv_silu=conv_silu, split_fox=split_fox, gate_norm=gate_norm, split_ssd=split_ssd, leave_out=leave_out)
            act.wait_ge(consts_made, 4)
            copy(root[:, 0:1], eps[:, :]).then_inc(tables_loaded, 1)
            act.wait_ge(gain_copied, 1)
            for n in range(len(front)):
                make_hi(act, n)
                if n < NORM:
                    for k in (2 * n, 2 * n + 1):
                        make_h(0, k, par_mix)
                if n == NORM - 1:
                    act.wait_ge(fd_landed, 32)
                    copy(w_fd_parts[:, :, 0:2 * H], w_fd[:, :, :]).then_inc(wfd_hi_made, 1)
                run(act_after, n, steps)
            for k in range(KD):
                make_hi(act, n_ffn + k)
                run(act_after, n_ffn + k, steps)
                if k == LEAD:
                    leave_out(NDN - 1)
                if k == STATS1_AT + LEAD:
                    stats(1, 4)

            def ffn_unit_silu(u):
                act.wait_ge(ffn_step, u * GATE_STEPS + GATE_STEPS)
                act.activation(silu_g[:, :, :], gate_out[:, :, :], ACT.Silu).then_inc(ffn_silu, 1)

            def ffn_unit_hi(u):
                act.wait_ge(ffn_act, u + 1)
                dst = actHi[:, 2 * u:2 * u + 2, :] if isinstance(u, int) else actHi[:, bass.ds(u * 2, 2), :]
                copy(dst, gate_out[:, :, :]).then_inc(ffn_hi, 1)

            with act.Fori(0, NG // 2) as i:
                for j in range(2):
                    for k in range(KD):
                        make_hi(act, n_ffn + (1 + j) * KD + k, i * (2 * KD // RING))
                        for b in range(2):
                            if k == UNIT_AT[b] + U_SILU:
                                ffn_unit_silu(i * 4 + (2 * j + b))
                            if k == UNIT_AT[b] + U_HI:
                                ffn_unit_hi(i * 4 + (2 * j + b))
            for g in range(NDN):
                n0 = n_down + g * KDN
                peeled = 18 if g == 0 else 6
                for c in range(peeled):
                    make_hi(act, n0 + c)
                    if g == 0:
                        for b in range(2):
                            if c == UNIT_AT[b] + U_SILU:
                                ffn_unit_silu(2 * (NG - 1) + b)
                            if c == UNIT_AT[b] + U_HI:
                                ffn_unit_hi(2 * (NG - 1) + b)
                    elif c == LEAD:
                        for k in range(MT * (g - 1), MT * g):
                            make_h(2, k, par_ple)
                with act.Fori(0, (KDN - peeled) // RING) as q:
                    for j in range(RING):
                        make_hi(act, n0 + peeled + j, q)

            def ple_sigmoid(i, only=(0, 1)):
                for t in only:
                    if t == 0:
                        act.wait_ge(gate_first, i + 1)
                        act.wait_ge(rms_made, 3)
                    else:
                        act.wait_ge(w_used, n_ple + GROUP * (i + 1) if i < NDN - 1 else n_last + 1)
                    if i > 0:
                        act.wait_ge(ple_mul, TT * (i - 1) + t + 1)
                    act.activation(pg_sig[:, t, :], ps[:, GATE_BANKS[i % 2][t], :], ACT.Sigmoid,
                                   scale=rms_col[:, t:t + 1]).then_inc(ple_sig, 1)

            def copy_residual(i):
                for t in range(TT):
                    act.wait_ge(xtok_turned, TT * i + t + 1)
                    copy(out_tok[:, t, i * COLS:(i + 1) * COLS], ps[:, XTOK_BANKS[t], :]).then_inc(xtok_copied, 1)

            def square(i, t):
                act.wait_ge(out_added, TT * i + t + 1)
                if i + t > 0:
                    act.wait_ge(out_squared, TT * i + t)
                act.activation(squares[:, :], out_tok[:, t, i * COLS:(i + 1) * COLS], ACT.Square,
                               accum_out=out_ssq[:, t, i:i + 1]).then_inc(out_squared, 1)

            for n in range(len(tail)):
                make_hi(act, n_ple + n)
                if n == LEAD:
                    for k in range(MT * (NDN - 1), KD):
                        make_h(2, k, par_ple)
                if n == STATS2_AT + LEAD - 1:
                    stats(2, GATE_BANKS[1][0], T, T + TT)
                if n % GROUP == XCOPY_AT:
                    copy_residual(n // GROUP)
                for i in range(NDN - 1):
                    if n == i * GROUP + SIG_AT:
                        ple_sigmoid(i)
                    if n == i * GROUP + SQUARE_AT:
                        for t in range(TT):
                            square(i, t)
            for t in range(TT):
                ple_sigmoid(NDN - 1, (t,))
                act.activation(out_root[:, t:t + 1], eps[:, :], ACT.Sqrt).then_inc(tables_loaded, 1)
                square(NDN - 1, t)
                act.wait_ge(out_sum_made, t + 1)
                act.wait_ge(tables_loaded, 2 + 2 * t)
                act.activation(out_root[:, t:t + 1], out_sum[:, t:t + 1], ACT.Sqrt, bias=eps[:, :], scale=1.0 / D).then_inc(out_root_made, 1)
                act.wait_ge(out_gained, TT * (NDN - 1))
                act.wait_ge(out_rms_made, t + 1)
                for i in range(NDN // 2):
                    piece = out_tok[:, t, i * COLS:(i + 1) * COLS]
                    copy(piece, piece, out_rms[:, t:t + 1]).then_inc(out_final_act, 1)
                if t == 0:
                    act.activation(unread[:, :], eps[:, :], ACT.Sigmoid).then_inc(tables_loaded, 1)

        @block.vector
        def _(dve):
            def make_h(norm, k, gain):
                dve.wait_ge(h_hi_made, norm * KD + k + 1)
                dve.scalar_tensor_tensor(hLo[:, k, :], xT[:, k, :], gain[:, k:k + 1], hHi[:, k, :],
                                         ALU.mult, ALU.subtract).then_inc(h_lo_made, 1)

            def add_to_residual(norm, i, banks):
                for b in range(2):
                    k = MT * i + 2 * b
                    dve.tensor_tensor(xT[:, k:k + 2, :], ps[:, banks[b], :].rearrange("p (a t) -> p a t", a=2),
                                      xT[:, k:k + 2, :], ALU.add).then_inc(x_new, 1)

            def stats(norm):
                dve.wait_ge(root_made, norm + 1)
                if norm == 0:
                    dve.reciprocal(rms_col[:, :], root[:, T:T + TT])
                if norm == 3:
                    dve.reciprocal(rms_col[:, :], root[:, T:T + TT]).then_inc(rms_made, 1)
                    return
                for j in range(2):
                    ins = dve.reciprocal(rms[:, j, :], root[:, 0:T])
                ins.then_inc(rms_made, 1)
                dve.wait_ge(rms_made, norm + 1)

            pair = lambda bank: ps[:, bank, :].rearrange("p (a t) -> p a t", a=2)

            def conv_channel(u):
                return WT + 2 * u if u < 2 else 2 * (u - 2)

            def conv_tap(u, back):
                for e in range(2):
                    dst, src = conv_out[:, u % 2, e, :], conv_in[:, e, 4 - back:4 - back + T]
                    ch = conv_channel(u) + e
                    weight = par_cw[KC - 1 - back][:, ch:ch + 1]
                    if back == 0:
                        ins = dve.tensor_scalar(dst, src, weight, par_cb[:, ch:ch + 1], ALU.mult, ALU.add)
                    else:
                        dve.wait_ge(conv_step, CONV_STEPS * u + 2 * back + e)
                        ins = dve.scalar_tensor_tensor(dst, src, weight, dst, ALU.mult, ALU.add)
                    ins.then_inc(conv_step, 1)

            def conv_start(name, b):
                u = 2 * ("bc", "x0", "x1").index(name) + b
                dve.wait_ge(w_used, done[name] + 1)
                if u == 0:
                    dve.wait_ge(par_copied, 1)
                    dve.wait_ge(masks_made, 8)
                else:
                    dve.wait_ge(conv_step, CONV_STEPS * u)
                bank = groups[name].banks[b]
                dve.tensor_tensor(conv_in[:, :, 4:4 + T], pair(bank), rms[:, :, :], ALU.mult).then_inc(conv_step, 1)
                if u >= 2:
                    dve.wait_ge(silu_made, u - 1)
                dve.wait_ge(conv_step, CONV_STEPS * u + 1)
                for back in range(0, 2):
                    conv_tap(u, back)

            def conv_taps(u):
                for back in range(2, KC):
                    conv_tap(u, back)

            def leave(g):
                dve.wait_ge(w_used, done[g.name] + 1)
                for b in range(2):
                    bank = g.banks[b]
                    k = MT * int(g.name[1]) + 2 * b
                    if g.name[0] == "q":
                        ins = dve.scalar_tensor_tensor(qT[:, k:k + 2, :], pair(bank), HD ** -0.5, rms[:, :, :],
                                                       ALU.mult, ALU.mult)
                    else:
                        for keys, a in ((kE, 0), (kO, P // 2)):
                            r = slice(a, a + P // 2)
                            ins = dve.tensor_tensor(keys[r, k:k + 2, :], ps[r, bank, :].rearrange("p (a t) -> p a t", a=2),
                                                    rms[r, :, :], ALU.mult)
                    if b == 1:
                        ins.then_inc(dve_evac, 1)

            def stats0():
                dve.wait_ge(p_hi_made, 1)
                dve.tensor_tensor(pLo[:, :, :], pair(0), pHi[:, :, :], ALU.subtract).then_inc(p_lo_made, 1)
                stats(0)

            fd_count = [0]
            fdr = lambda i: fdw[:, i, :]

            def link(ins):
                fd_count[0] += 1
                ins.then_inc(fd_step, 1)
                dve.wait_ge(fd_step, fd_count[0])

            def fd():
                dve.wait_ge(fd_ready, 1)
                link(dve.tensor_copy(fdr(1), ps[2 * H:4 * H, TURN_BANK, 0:T]))
                link(dve.tensor_tensor(fdr(1), ps[0:2 * H, TURN_BANK, 0:T], fdr(1), ALU.add))
                link(dve.tensor_tensor(fdr(1), fdr(1), rms[0:2 * H, 0, :], ALU.mult))
                dve.wait_ge(small_landed, 48)
                dve.wait_ge(masks_made, 8)
                link(dve.tensor_scalar(fdr(1), fdr(1), fdc[:, 0:1], fdc[:, 1:2], ALU.add, ALU.mult))

            def softplus():
                dve.wait_ge(fd_exp, 1)
                link(dve.tensor_scalar(fdr(4), fdr(3), 2.0, None, ALU.add))
                link(dve.reciprocal(fdr(4), fdr(4)))
                link(dve.tensor_tensor(fdr(4), fdr(3), fdr(4), ALU.mult))
                link(dve.tensor_tensor(fdr(5), fdr(4), fdr(4), ALU.mult))
                link(dve.tensor_scalar(fdr(6), fdr(5), 1.0 / 15, None, ALU.mult))
                for n in (13, 11, 9):
                    link(dve.scalar_tensor_tensor(fdr(6), fdr(6), 1.0 / n, fdr(5), ALU.add, ALU.mult))

            def cumulate():
                for n in (7, 5, 3):
                    link(dve.scalar_tensor_tensor(fdr(6), fdr(6), 1.0 / n, fdr(5), ALU.add, ALU.mult))
                link(dve.scalar_tensor_tensor(fdr(6), fdr(6), 1.0, fdr(4), ALU.add, ALU.mult))
                link(dve.tensor_scalar(fdr(5), fdr(1), 0.0, None, ALU.max))
                link(dve.scalar_tensor_tensor(fdr(6), fdr(6), 2.0, fdr(5), ALU.mult, ALU.add))
                assert fd_count[0] == SOFTPLUS_STEPS
                dve.wait_ge(a_ready, 1)
                link(dve.tensor_scalar(fdr(7), fdr(6), fdc[:, 3:4], -1.0, ALU.mult, ALU.mult))
                link(dve.tensor_tensor_scan(fdr(1), fdr(0), fdr(7), 0.0, ALU.mult, ALU.add))
                assert fd_count[0] == CUMULATE_STEPS

            def make_row(attention):
                n, c = 2 * H, fdr(1)
                src = fdw[:, 2 + 2 * attention:4 + 2 * attention, :].rearrange("h a t -> h (a t)")[:, 0:3 * P]
                if attention:
                    dst = fox_row
                    link(dve.tensor_scalar(src[:, 0:P], c[:, 0:P], -1.0, None, ALU.mult))
                    link(dve.tensor_scalar(src[:, P:3 * P], c, -1.0, None, ALU.mult))
                    dve.tensor_copy(ident_bf[:, :], ident[:, :])
                else:
                    dst = ssd_row
                    link(dve.tensor_copy(src[:, 0:P], c[:, 0:P]))
                    link(dve.tensor_scalar(src[:, P:T], c[:, P:T], c[:, P - 1:P], None, ALU.add))
                    link(dve.tensor_copy(src[:, T:3 * P], c[:, P:T]))
                    dve.tensor_copy(sel[:, :], sel_f[:, :])
                link(dve.tensor_copy(dst[0:n, :], src))
                dve.tensor_tensor(dst[n:2 * n, :], src, dst[0:n, :], ALU.subtract).then_inc(cum_ready, 1)

            def cums():
                dve.wait_ge(dt_turned, 1)
                tok = lambda i: ps[:, SPARE_BANK, i * TT * 2 * H:(i + 1) * TT * 2 * H].rearrange("p (t h) -> p t h", t=TT)
                dve.tensor_copy(dt_tok[:, :, :], tok(0)).then_inc(dt_copied, 1)
                dve.tensor_scalar(ncum_tok[:, :, :], tok(1), -1.0, None, ALU.mult).then_inc(dt_copied, 1)

            def cb(g):
                dve.wait_ge(cb_ready, g + 1)
                dve.tensor_copy(cbT[:, g, :], ps[:, SPARE_BANK, 0:3 * P]).then_inc(cb_copied, 1)

            def leave_v(g):
                half = int(g.name[1])
                heads = slice(half * H // 2, (half + 1) * H // 2)
                for t in range(TT):
                    dve.wait_ge(v_hi_made, TT * half + t + 1)
                    dve.scalar_tensor_tensor(v_parts[:, t, heads, HD:2 * HD], ps[:, g.banks[t], :].rearrange("p (h d) -> p h d", d=HD),
                                             rms_col[:, t:t + 1], v_parts[:, t, heads, 0:HD],
                                             ALU.mult, ALU.subtract).then_inc(v_lo_made, 1)

            def fox(i):
                if i < H:
                    h = i
                    dve.wait_ge(s_ready, h + 1)
                    for t, (a, b) in enumerate(((0, P), (P, 3 * P))):
                        dve.reduce_max(neg_max[:, h, t:t + 1], ps[:, s_bank(h), a:b], AX_X, negate=True).then_inc(max_made, 1)
                if 1 <= i < H + 1:
                    h = i - 1
                    dve.wait_ge(prob_made, 2 * h + 2)
                    dve.reciprocal(row_inv[:, h, :], row_sum[:, h, :]).then_inc(inv_made, 1)
                    dve.wait_ge(inv_made, h + 1)
                    for t, (a, b) in enumerate(((0, P), (P, 3 * P))):
                        dve.tensor_scalar(prob[:, h % 2, a:b], prob[:, h % 2, a:b], row_inv[:, h, t:t + 1], None,
                                          ALU.mult).then_inc(prob_normed, 1)
                if 2 <= i < H + 2:
                    h = i - 2
                    dve.wait_ge(prob_hi_made, h + 1)
                    dve.tensor_tensor(probT_lo[:, h % 2, :], ps[:, TURN_BANK, 0:3 * P], probT_hi[:, h % 2, :],
                                      ALU.subtract).then_inc(prob_lo_made, 1)
                if i >= 3:
                    h = i - 3
                    dve.wait_ge(y_part_made, h + 1)
                    at_ = (h % 2) * HD
                    dve.tensor_tensor(y_foxT[at_:at_ + HD, h // 2, :], ps[0:HD, s_bank(h + 1), 0:T], y_part[:, h % 2, :],
                                      ALU.add).then_inc(y_made, 1)

            def ssd(i):
                if 1 <= i < H + 1:
                    h = i - 1
                    dve.wait_ge(m_hi_made, h + 1)
                    dve.tensor_tensor(mT_lo[:, h % 2, :], mT[:, h % 2, :], mT_hi[:, h % 2, :], ALU.subtract).then_inc(m_lo_made, 1)
                if i >= 2:
                    h = i - 2
                    rows_ = slice((h % 2) * HD, (h % 2 + 1) * HD)
                    dve.wait_ge(yo_part_made, h + 1)
                    if h >= 1:
                        dve.wait_ge(ys_made, h)
                    dve.tensor_tensor(y_sum[rows_, :], ps[0:HD, s_bank(h), 0:T], y_part[:, h % 2, :], ALU.add).then_inc(y_summed, 1)
                if i < H:
                    h = i
                    dve.wait_ge(decay_made, 2 * h + 2)
                    if h >= 2:
                        dve.wait_ge(m_lo_made, h - 1)
                    dve.tensor_tensor(mT[:, h % 2, :], decay[:, h % 2, :], cbT[:, h * G // H, :], ALU.mult).then_inc(m_made, 1)
                if i >= 2:
                    h = i - 2
                    rows_ = slice((h % 2) * HD, (h % 2 + 1) * HD)
                    dve.wait_ge(y_summed, h + 1)
                    head = xsT[rows_, h // 2, :]
                    dve.scalar_tensor_tensor(head, head, d_all[rows_, h:h + 1], y_sum[rows_, :], ALU.mult, ALU.add).then_inc(ys_made, 1)

            def turn_xs(half):
                heads = slice(half * H // 2, (half + 1) * H // 2)
                h0 = H + half * (H // 2)
                by_head = lambda t: t.rearrange("p (h d) -> p h d", d=HD)
                cols = slice(half * COLS, (half + 1) * COLS)
                for t in range(TT):
                    i = TT * half + t
                    dve.wait_ge(xs_turned, i + 1)
                    if i == 0:
                        dve.wait_ge(dt_copied, 1)
                    dve.tensor_tensor(by_head(xdt[:, t, cols]), by_head(ps[:, XS_BANKS[i], :]),
                                      dt_tok[:, t, h0:h0 + H // 2].unsqueeze(2).to_broadcast([P, H // 2, HD]),
                                      ALU.mult).then_inc(xdt_made, 1)
                for t in range(TT):
                    dve.wait_ge(xdt_hi_made, TT * half + t + 1)
                    dve.tensor_tensor(xdt_parts[:, t, heads, HD:2 * HD], by_head(xdt[:, t, cols]), xdt_parts[:, t, heads, 0:HD],
                                      ALU.subtract).then_inc(xdt_lo_made, 1)

            def split_fox(b):
                dve.wait_ge(mix_hi_made, b + 1)
                dve.tensor_tensor(mixLo[:, 2 * b:2 * b + 2, :], y_foxT[:, 2 * b:2 * b + 2, :], mixHi[:, 2 * b:2 * b + 2, :],
                                  ALU.subtract).then_inc(mix_lo_made, 1)

            def leave_z(half):
                dve.wait_ge(w_used, done[f"z{half}"] + 1)
                for b in range(2):
                    k = MT * half + 2 * b
                    dve.tensor_tensor(zT[:, k:k + 2, :], pair(groups[f"z{half}"].banks[b]), rms[:, :, :], ALU.mult).then_inc(z_scaled, 1)

            def gate_mul(half):
                dve.wait_ge(ys_made, H)
                dve.wait_ge(z_made, 2 * half + 2)
                tiles = slice(MT * half, MT * (half + 1))
                dve.tensor_tensor(xsT[:, tiles, :], xsT[:, tiles, :], zT[:, tiles, :], ALU.mult).then_inc(gated, 1)

            def gate_norm():
                dve.wait_ge(y_root_made, 1)
                dve.reciprocal(y_rms[:, :], root[:, 0:T]).then_inc(y_rms_made, 1)

            def scale_ssd(b):
                dve.wait_ge(y_rms_made, 1)
                for k in (2 * b, 2 * b + 1):
                    dve.scalar_tensor_tensor(xsT[:, k, :], xsT[:, k, :], par_ssdn[:, k:k + 1], y_rms[:, :],
                                             ALU.mult, ALU.mult).then_inc(y_normed, 1)

            def split_ssd(b):
                dve.wait_ge(mix_hi_made, WT // 2 + b + 1)
                dve.tensor_tensor(mixLo[:, WT + 2 * b:WT + 2 * b + 2, :], xsT[:, 2 * b:2 * b + 2, :],
                                  mixHi[:, WT + 2 * b:WT + 2 * b + 2, :], ALU.subtract).then_inc(mix_lo_made, 1)

            def leave_out(i):
                dve.wait_ge(w_used, done[f"o{i}"] + 1)
                add_to_residual(1, i, out_groups[i].banks)
                for k in range(MT * i, MT * (i + 1)):
                    make_h(1, k, par_ffn)

            def turn_par():
                dve.wait_ge(par_turned, 1)
                for i, r in enumerate(par_spans):
                    ins = dve.tensor_copy(par[:, i, 0:r], ps[:, 1, i * P:i * P + r])
                ins.then_inc(par_copied, 1)

            def copy_x(b):
                dve.wait_ge(x_turned, b + 1)
                dve.tensor_copy(xT[:, 2 * b:2 * b + 2, :], pair(X_BANKS[b % len(X_BANKS)])).then_inc(x_new, 1)

            steps = dict(leave=leave, turn_par=turn_par, stats0=stats0, fd=fd, softplus=softplus, cumulate=cumulate, make_row=make_row,
                         cums=cums, cb=cb, conv_start=conv_start, conv_taps=conv_taps, fox=fox, ssd=ssd, turn_xs=turn_xs,
                         leave_v=leave_v, leave_z=leave_z, split_fox=split_fox, gate_mul=gate_mul, gate_norm=gate_norm,
                         scale_ssd=scale_ssd, split_ssd=split_ssd,
                         leave_out=leave_out)
            dve.memset(idle_in[:, :], 0.0).then_inc(idle_in_made, 1)
            dve.wait_ge(gain_turned, 1)
            dve.tensor_copy(par_mix[:, :], ps[:, 4, 0:KD]).then_inc(gain_copied, 1)
            dve.wait_ge(gain_copied, 1)
            copy_x(0)
            for n in range(len(front)):
                make_lo(dve, n)
                if n < NORM:
                    for k in (2 * n, 2 * n + 1):
                        make_h(0, k, par_mix)
                if n == 0:
                    copy_x(1)
                if n == 1:
                    copy_x(2)
                if 1 <= n and n + 2 < NORM:
                    copy_x(n + 2)
                if n == NORM:
                    dve.wait_ge(wfd_hi_made, 1)
                    dve.tensor_tensor(w_fd_parts[:, :, 2 * H:4 * H], w_fd[:, :, :], w_fd_parts[:, :, 0:2 * H],
                                      ALU.subtract).then_inc(wfd_lo_made, 1)
                run(dve_after, n, steps)
            for k in range(KD):
                make_lo(dve, n_ffn + k)
                run(dve_after, n_ffn + k, steps)
                if k == LEAD:
                    leave_out(NDN - 1)
                    dve.memset(gate_in[:, :, :, 0:4], 0.0).then_inc(ffn_out, 1)
                if k == STATS1_AT + LEAD:
                    stats(1)

            def ffn_unit_conv(u, half, b):
                reg = not isinstance(u, int)
                ch = lambda t, e: t[:, bass.ds(u * 2 + e, 1)] if reg else t[:, 2 * u + e:2 * u + e + 1]
                base = u * GATE_STEPS
                buf = gate_in[:, b, :, :]
                dve.tensor_tensor(buf[:, :, 4:4 + T], pair(4 * half + b), rms[:, :, :], ALU.mult).then_inc(ffn_step, 1)
                dve.wait_ge(ffn_step, base + 1)
                for e in range(2):
                    dve.tensor_scalar(gate_out[:, e, :], buf[:, e, 4:4 + T], ch(par_fw[KF - 1], e), ch(par_fb, e),
                                      ALU.mult, ALU.add).then_inc(ffn_step, 1)

            def ffn_unit_taps(u, b):
                reg = not isinstance(u, int)
                ch = lambda t, e: t[:, bass.ds(u * 2 + e, 1)] if reg else t[:, 2 * u + e:2 * u + e + 1]
                base = u * GATE_STEPS
                buf = gate_in[:, b, :, :]
                for back in range(1, KF):
                    for e in range(2):
                        dve.wait_ge(ffn_step, base + (2 * back + e))
                        dve.scalar_tensor_tensor(gate_out[:, e, :], buf[:, e, 4 - back:4 - back + T],
                                                 ch(par_fw[KF - 1 - back], e), gate_out[:, e, :],
                                                 ALU.mult, ALU.add).then_inc(ffn_step, 1)

            def ffn_unit_act(u, half, b):
                dve.tensor_tensor(up[:, :, :], pair(4 * half + 2 + b), rms[:, :, :], ALU.mult).then_inc(ffn_out, 1)
                dve.wait_ge(ffn_out, u + 2)
                dve.wait_ge(ffn_silu, u + 1)
                dve.tensor_tensor(gate_out[:, :, :], up[:, :, :], silu_g[:, :, :], ALU.mult).then_inc(ffn_act, 1)

            def ffn_unit_lo(u):
                dve.wait_ge(ffn_hi, u + 1)
                sl = slice(2 * u, 2 * u + 2) if isinstance(u, int) else bass.ds(u * 2, 2)
                dve.tensor_tensor(actLo[:, sl, :], gate_out[:, :, :], actHi[:, sl, :], ALU.subtract).then_inc(ffn_lo, 1)

            def ffn_steps(k, u0, half, group_end):
                for b in range(2):
                    u = u0 + b
                    if k == UNIT_AT[b] + U_IN:
                        if b == 0:
                            dve.wait_ge(w_used, group_end)
                        ffn_unit_conv(u, half, b)
                    if k == UNIT_AT[b] + U_TAPS:
                        ffn_unit_taps(u, b)
                    if k == UNIT_AT[b] + U_ACT:
                        ffn_unit_act(u, half, b)
                    if k == UNIT_AT[b] + U_LO:
                        ffn_unit_lo(u)

            with dve.Fori(0, NG // 2) as i:
                for j in range(2):
                    for k in range(KD):
                        make_lo(dve, n_ffn + (1 + j) * KD + k, i * (2 * KD // RING))
                        ffn_steps(k, i * 4 + 2 * j, j, i * (2 * KD) + (n_ffn + (1 + j) * KD))
            for g in range(NDN):
                n0 = n_down + g * KDN
                peeled = 18 if g == 0 else 6
                for c in range(peeled):
                    make_lo(dve, n0 + c)
                    if g == 0:
                        ffn_steps(c, 2 * (NG - 1), 0, n_down)
                    elif c == LEAD:
                        dve.wait_ge(w_used, n0)
                        add_to_residual(2, g - 1, down_banks[g - 1])
                        for k in range(MT * (g - 1), MT * g):
                            make_h(2, k, par_ple)
                with dve.Fori(0, (KDN - peeled) // RING) as q:
                    for j in range(RING):
                        make_lo(dve, n0 + peeled + j, q)

            def gate_projection(i, t):
                dve.wait_ge(ple_sig, TT * i + t + 1)
                if i > 0:
                    dve.wait_ge(out_added, TT * (i - 1) + t + 1)
                dve.tensor_tensor(gate_x[:, t, :], ps[:, PROJ_BANKS[t], :], pg_sig[:, t, :], ALU.mult).then_inc(ple_mul, 1)

            def ple_add(i, t):
                dve.wait_ge(ple_mul, TT * i + t + 1)
                dve.wait_ge(xtok_copied, TT * i + t + 1)
                cols = out_tok[:, t, i * COLS:(i + 1) * COLS]
                dve.tensor_tensor(cols, cols, gate_x[:, t, :], ALU.add).then_inc(out_added, 1)

            def ple_gain(i, t):
                dve.wait_ge(out_squared, TT * i + t + 1)
                if i + t == 0:
                    dve.wait_ge(gain_fin_landed, 16)
                cols = out_tok[:, t, i * COLS:(i + 1) * COLS]
                dve.tensor_tensor(cols, cols, gain_fin[:, i * COLS:(i + 1) * COLS], ALU.mult).then_inc(out_gained, 1)

            for n in range(len(tail)):
                make_lo(dve, n_ple + n)
                if n == LEAD:
                    dve.wait_ge(w_used, n_ple)
                    add_to_residual(2, NDN - 1, down_banks[NDN - 1])
                    for k in range(MT * (NDN - 1), KD):
                        make_h(2, k, par_ple)
                if n == STATS2_AT + LEAD - 1:
                    dve.wait_ge(root_made, 3)
                    dve.reciprocal(rms_col[:, :], root[:, T:T + TT]).then_inc(rms_made, 1)
                for i in range(NDN - 1):
                    for place, step in ((MUL_AT, gate_projection), (ADD_AT, ple_add), (GAIN_AT, ple_gain)):
                        if n == i * GROUP + place:
                            for t in range(TT):
                                step(i, t)
            for t in range(TT):
                gate_projection(NDN - 1, t)
                ple_add(NDN - 1, t)
                dve.wait_ge(out_gained, TT * (NDN - 1))
                dve.wait_ge(out_squared, TT * (NDN - 1) + t + 1)
                dve.reduce_sum(out_sum[:, t:t + 1], out_ssq[:, t, :], AX_X).then_inc(out_sum_made, 1)
                dve.wait_ge(out_root_made, t + 1)
                dve.reciprocal(out_rms[:, t:t + 1], out_root[:, t:t + 1]).then_inc(out_rms_made, 1)
                dve.wait_ge(out_rms_made, t + 1)
                for i in range(NDN // 2, NDN):
                    piece = out_tok[:, t, i * COLS:(i + 1) * COLS]
                    if i < NDN - 1:
                        ins = dve.tensor_scalar(piece, piece, out_rms[:, t:t + 1], None, ALU.mult)
                    else:
                        ins = dve.scalar_tensor_tensor(piece, piece, out_rms[:, t:t + 1], gain_fin[:, i * COLS:D],
                                                       ALU.mult, ALU.mult)
                    ins.then_inc(out_final, 1)


_INS = ["x", "p", "mix_norm_w", "w_in", "fox_forget_bias", "ssd_conv_w", "ssd_conv_b", "ssd_dt_bias", "ssd_A_log",
        "ssd_D", "ssd_norm_w", "w_out", "ffn_norm_w", "w_gate_up", "ffn_conv_w", "ffn_conv_b", "w_down",
        "ple_norm_w", "w_ple_gate", "w_ple_proj", "final_norm_w"]


def kernel(**inputs):
    import numpy as np
    import concourse.bacc as bacc
    from concourse.bass_utils import run_bass_kernel_spmd

    nc = bacc.Bacc("TRN2", target_bir_lowering=False, num_devices=1)
    arrays, args = {}, []
    for name in _INS:
        a = np.ascontiguousarray(inputs[name])
        arrays[f"in_{name}"] = a
        args.append(nc.dram_tensor(f"in_{name}", a.shape, mybir.dt.from_np(a.dtype), kind="ExternalInput").ap())
    out = nc.dram_tensor("out_x", arrays["in_x"].shape, F32, kind="ExternalOutput").ap()
    build(nc, *args, out)
    r = run_bass_kernel_spmd(nc, [arrays], core_ids=[0])
    return r.results[0]["out_x"]
```
